# Optimizing a Trainium2 kernel written in Bass

```python
import jax, jax.numpy as jnp
from jax import lax
import numpy as np
import math

D_MODEL = 1024
BATCH = 1
SEQ = 256
DEPTH = 1

HEAD_DIM = 64
FOX_HEADS = 8
NSA_HEADS = 8
NSA_GROUPS = 2
NSA_HPG = NSA_HEADS // NSA_GROUPS
BRANCH_WIDTH = 512
N_BRANCH = 2
N_NSA_BRANCH = 3
ROPE_DIM = HEAD_DIM // 4
ROPE_THETA = 500000.0
Q_BLOCK = 128
CMP_LEN = 32
CMP_STRIDE = 16
CMP_HIDDEN = 2 * HEAD_DIM
SLC_LEN = 64
SLC_TOP = 16
WINDOW = 512
FORGET_BIAS_INIT = 4.0
FORCED_SCORE = 1e9
NEG_INF = -1e30
PEER_HEADS = 8
N_KEYS = 128
N_EXPERTS = N_KEYS * N_KEYS
PEER_QDIM = 256
PEER_TOPK = 16
PEER_CHUNK = 128
RMS_EPS = 1e-6

KV_WIDTH = NSA_GROUPS * HEAD_DIM
IN_SPLITS = (BRANCH_WIDTH, BRANCH_WIDTH, BRANCH_WIDTH, FOX_HEADS, BRANCH_WIDTH,
             KV_WIDTH, KV_WIDTH, KV_WIDTH, KV_WIDTH, KV_WIDTH, KV_WIDTH,
             NSA_HEADS * N_NSA_BRANCH, N_BRANCH * D_MODEL)
D_IN = sum(IN_SPLITS)


def rmsnorm(x, g):
    xf = x.astype(jnp.float32)
    y = xf * lax.rsqrt(jnp.mean(xf * xf, axis=-1, keepdims=True) + RMS_EPS)
    return (y * g.astype(jnp.float32)).astype(x.dtype)

def split_columns(t, sizes):
    offs = np.cumsum((0,) + tuple(sizes))
    return [t[..., int(a):int(b)] for a, b in zip(offs[:-1], offs[1:])]

def rope_tables(pos):
    inv = jnp.power(ROPE_THETA, -jnp.arange(0, ROPE_DIM, 2, dtype=jnp.float32) / ROPE_DIM)
    ang = pos[:, None] * inv[None, :]
    return jnp.cos(ang), jnp.sin(ang)

def apply_partial_rope(x, cos, sin):
    half = ROPE_DIM // 2
    xr = x[..., :ROPE_DIM].astype(jnp.float32)
    x1, x2 = xr[..., :half], xr[..., half:]
    c, s = cos[:, None, :], sin[:, None, :]
    rot = jnp.concatenate([x1 * c - x2 * s, x1 * s + x2 * c], axis=-1)
    return jnp.concatenate([rot.astype(x.dtype), x[..., ROPE_DIM:]], axis=-1)

def fox_attention(q, k, v, log_f):
    B_, S_, H, Dh = q.shape
    scale = Dh ** -0.5
    c = jnp.swapaxes(jnp.cumsum(log_f, axis=1), 1, 2)
    k_pos = jnp.arange(S_)

    def block(i):
        q0 = i * Q_BLOCK
        q_pos = q0 + jnp.arange(Q_BLOCK)
        qb = lax.dynamic_slice_in_dim(q, q0, Q_BLOCK, axis=1)
        cb = lax.dynamic_slice_in_dim(c, q0, Q_BLOCK, axis=2)
        logits = jnp.einsum('bqhd,bkhd->bhqk', qb, k).astype(jnp.float32) * scale
        logits = logits + (cb[..., :, None] - c[..., None, :])
        mask = k_pos[None, :] <= q_pos[:, None]
        p = jax.nn.softmax(jnp.where(mask, logits, NEG_INF), axis=-1)
        return jnp.einsum('bhqk,bkhd->bqhd', p.astype(v.dtype), v).reshape(B_, Q_BLOCK, H * Dh)

    out = lax.map(block, jnp.arange(S_ // Q_BLOCK))
    return jnp.moveaxis(out, 0, 1).reshape(B_, S_, H * Dh)

def compress_kv(k, v, cmp_pos, w1, w2):
    B_, S_ = k.shape[0], k.shape[1]
    n_cmp = (S_ - CMP_LEN) // CMP_STRIDE + 1
    starts = np.arange(n_cmp) * CMP_STRIDE
    idx = starts[:, None] + np.arange(CMP_LEN)[None, :]

    def phi(t, j):
        blocks = t[:, idx] + cmp_pos[j][None, None, :, None, :]
        flat = jnp.swapaxes(blocks, 2, 3).reshape(B_, n_cmp, NSA_GROUPS, CMP_LEN * HEAD_DIM)
        return jax.nn.gelu(flat @ w1[j], approximate=False) @ w2[j]

    return phi(k, 0), phi(v, 1), jnp.asarray(starts + CMP_LEN - 1, dtype=jnp.int32)

def nsa_attention(q, k_cmp, v_cmp, cmp_end, k_slc, v_slc, k_win, v_win, gates):
    B_, S_, H, Dh = q.shape
    G = NSA_GROUPS
    scale = Dh ** -0.5
    n_cmp = k_cmp.shape[1]
    n_slc = S_ // SLC_LEN
    top = min(SLC_TOP, n_slc)
    cs = np.arange(n_cmp)[:, None] * CMP_STRIDE
    ss = np.arange(n_slc)[None, :] * SLC_LEN
    ov = np.clip(np.minimum(cs + CMP_LEN, ss + SLC_LEN) - np.maximum(cs, ss), 0, None) / CMP_LEN
    overlap = jnp.asarray(ov, dtype=jnp.float32)
    kb = k_slc.reshape(B_, n_slc, SLC_LEN, G, Dh).transpose(0, 3, 1, 2, 4)
    vb = v_slc.reshape(B_, n_slc, SLC_LEN, G, Dh).transpose(0, 3, 1, 2, 4)
    pad = ((0, 0), (WINDOW, 0), (0, 0), (0, 0))
    kwp, vwp = jnp.pad(k_win, pad), jnp.pad(v_win, pad)
    bi = jnp.arange(B_)[:, None, None, None]
    gi = jnp.arange(G)[None, :, None, None]
    blk_ids = jnp.arange(n_slc)

    def block(i):
        q0 = i * Q_BLOCK
        q_pos = q0 + jnp.arange(Q_BLOCK)
        qb = lax.dynamic_slice_in_dim(q, q0, Q_BLOCK, axis=1).reshape(B_, Q_BLOCK, G, NSA_HPG, Dh)
        gb = lax.dynamic_slice_in_dim(gates, q0, Q_BLOCK, axis=1).reshape(B_, Q_BLOCK, G, NSA_HPG, N_NSA_BRANCH)
        lc = jnp.einsum('bqghd,bngd->bghqn', qb, k_cmp).astype(jnp.float32) * scale
        mc = cmp_end[None, :] <= q_pos[:, None]
        pc = jax.nn.softmax(jnp.where(mc, lc, NEG_INF), axis=-1) * mc
        o_cmp = jnp.einsum('bghqn,bngd->bqghd', pc.astype(v_cmp.dtype), v_cmp)
        imp = jnp.einsum('bghqn,nj->bgqj', pc, overlap)
        q_blk = q_pos // SLC_LEN
        forced = (blk_ids[None, :] == 0) | (blk_ids[None, :] == q_blk[:, None]) | (blk_ids[None, :] == q_blk[:, None] - 1)
        causal = blk_ids[None, :] <= q_blk[:, None]
        score = jnp.where(forced, FORCED_SCORE, jnp.where(causal, imp, -1.0))
        _, sel = lax.top_k(score, top)
        k_sel = kb[bi, gi, sel]
        v_sel = vb[bi, gi, sel]
        ls = jnp.einsum('bqghd,bgqkld->bghqkl', qb, k_sel).astype(jnp.float32) * scale
        tok = sel[..., None] * SLC_LEN + jnp.arange(SLC_LEN)
        ms = (tok <= q_pos[None, None, :, None, None])[:, :, None]
        ls = jnp.where(ms, ls, NEG_INF).reshape(B_, G, NSA_HPG, Q_BLOCK, top * SLC_LEN)
        ps = jax.nn.softmax(ls, axis=-1).reshape(B_, G, NSA_HPG, Q_BLOCK, top, SLC_LEN)
        o_slc = jnp.einsum('bghqkl,bgqkld->bqghd', ps.astype(v_sel.dtype), v_sel)
        kwb = lax.dynamic_slice_in_dim(kwp, q0, WINDOW + Q_BLOCK, axis=1)
        vwb = lax.dynamic_slice_in_dim(vwp, q0, WINDOW + Q_BLOCK, axis=1)
        k_pos = q0 - WINDOW + jnp.arange(WINDOW + Q_BLOCK)
        lw = jnp.einsum('bqghd,bkgd->bghqk', qb, kwb).astype(jnp.float32) * scale
        rel = q_pos[:, None] - k_pos[None, :]
        mw = (rel >= 0) & (rel < WINDOW) & (k_pos[None, :] >= 0)
        pw = jax.nn.softmax(jnp.where(mw, lw, NEG_INF), axis=-1)
        o_win = jnp.einsum('bghqk,bkgd->bqghd', pw.astype(vwb.dtype), vwb)
        o = gb[..., 0:1] * o_cmp + gb[..., 1:2] * o_slc + gb[..., 2:3] * o_win
        return o.astype(q.dtype).reshape(B_, Q_BLOCK, H * Dh)

    out = lax.map(block, jnp.arange(S_ // Q_BLOCK))
    return jnp.moveaxis(out, 0, 1).reshape(B_, S_, H * Dh)

def hybrid_mixer(h, w_in, fox_f_bias, cmp_pos, cmp_w1, cmp_w2, w_branch, w_out):
    B_, S_, _ = h.shape
    proj = h @ w_in
    (fq, fk, fv, f_logit, nq, kc, vc, ksl, vsl, kwn, vwn,
     nsa_gate_logit, merge_logit) = split_columns(proj, IN_SPLITS)
    heads = lambda t, n: t.reshape(B_, S_, n, HEAD_DIM)
    log_f = jax.nn.log_sigmoid(f_logit.astype(jnp.float32) + fox_f_bias.astype(jnp.float32))
    y_fox = fox_attention(heads(fq, FOX_HEADS), heads(fk, FOX_HEADS), heads(fv, FOX_HEADS), log_f)
    cos, sin = rope_tables(jnp.arange(S_, dtype=jnp.float32))
    q_nsa = apply_partial_rope(heads(nq, NSA_HEADS), cos, sin)
    k_slc = apply_partial_rope(heads(ksl, NSA_GROUPS), cos, sin)
    k_win = apply_partial_rope(heads(kwn, NSA_GROUPS), cos, sin)
    k_cmp, v_cmp, cmp_end = compress_kv(heads(kc, NSA_GROUPS), heads(vc, NSA_GROUPS), cmp_pos, cmp_w1, cmp_w2)
    k_cmp = apply_partial_rope(k_cmp, *rope_tables(cmp_end.astype(jnp.float32)))
    gates = jax.nn.sigmoid(nsa_gate_logit.astype(jnp.float32)).reshape(B_, S_, NSA_HEADS, N_NSA_BRANCH)
    y_nsa = nsa_attention(q_nsa, k_cmp, v_cmp, cmp_end, k_slc, heads(vsl, NSA_GROUPS),
                          k_win, heads(vwn, NSA_GROUPS), gates)
    g = jax.nn.sigmoid(merge_logit.astype(jnp.float32)).reshape(B_, S_, N_BRANCH, D_MODEL).astype(h.dtype)
    ys = jnp.stack([y_fox, y_nsa], axis=2)
    up = jnp.einsum('bsnc,ncd->bsnd', ys, w_branch)
    merged = jnp.sum(g * up, axis=2)
    return merged @ w_out

def peer_ffn(h, wq, subkeys, u, v):
    B_, S_, D = h.shape
    T = B_ * S_
    hf = h.reshape(T, D)
    q = (hf @ wq).reshape(T, PEER_HEADS, 2, PEER_QDIM // 2)
    s = jnp.einsum('thpd,hpnd->thpn', q, subkeys).astype(jnp.float32)
    s1, i1 = lax.top_k(s[:, :, 0], PEER_TOPK)
    s2, i2 = lax.top_k(s[:, :, 1], PEER_TOPK)
    cand = (s1[..., :, None] + s2[..., None, :]).reshape(T, PEER_HEADS, PEER_TOPK * PEER_TOPK)
    cand_idx = (i1[..., :, None] * N_KEYS + i2[..., None, :]).reshape(T, PEER_HEADS, PEER_TOPK * PEER_TOPK)
    top_s, pos = lax.top_k(cand, PEER_TOPK)
    idx = jnp.take_along_axis(cand_idx, pos, axis=-1)
    w = jax.nn.softmax(top_s, axis=-1)

    def chunk(args):
        x_c, idx_c, w_c = args
        act = jax.nn.gelu(jnp.einsum('cd,chkd->chk', x_c, u[idx_c]).astype(jnp.float32), approximate=False)
        coef = (w_c * act).astype(v.dtype)
        return jnp.einsum('chk,chkd->cd', coef, v[idx_c])

    nc = T // PEER_CHUNK
    out = lax.map(chunk, (hf.reshape(nc, PEER_CHUNK, D),
                          idx.reshape(nc, PEER_CHUNK, PEER_HEADS, PEER_TOPK),
                          w.reshape(nc, PEER_CHUNK, PEER_HEADS, PEER_TOPK)))
    return out.reshape(B_, S_, D)

def first_inputs(seed: int = 0) -> dict:
    key = jax.random.key(seed)
    ks = jax.random.split(key, 16)
    f32 = jnp.float32
    nrm = lambda k, shape, scale: scale * jax.random.normal(k, shape, f32)
    L = DEPTH
    return {
        "x": jax.random.normal(ks[0], (BATCH, SEQ, D_MODEL), f32),
        "norm_mix": 1.0 + nrm(ks[1], (L, D_MODEL), 0.02),
        "w_in": nrm(ks[2], (L, D_MODEL, D_IN), D_MODEL ** -0.5),
        "fox_f_bias": FORGET_BIAS_INIT + nrm(ks[3], (L, FOX_HEADS), 0.1),
        "nsa_cmp_pos": nrm(ks[4], (L, 2, CMP_LEN, HEAD_DIM), 0.02),
        "nsa_cmp_w1": nrm(ks[5], (L, 2, CMP_LEN * HEAD_DIM, CMP_HIDDEN), (CMP_LEN * HEAD_DIM) ** -0.5),
        "nsa_cmp_w2": nrm(ks[6], (L, 2, CMP_HIDDEN, HEAD_DIM), CMP_HIDDEN ** -0.5),
        "w_branch": nrm(ks[7], (L, N_BRANCH, BRANCH_WIDTH, D_MODEL), BRANCH_WIDTH ** -0.5),
        "w_out": nrm(ks[8], (L, D_MODEL, D_MODEL), D_MODEL ** -0.5),
        "norm_ffn": 1.0 + nrm(ks[9], (L, D_MODEL), 0.02),
        "peer_wq": nrm(ks[10], (L, D_MODEL, PEER_HEADS * PEER_QDIM), D_MODEL ** -0.5),
        "peer_subkeys": nrm(ks[11], (L, PEER_HEADS, 2, N_KEYS, PEER_QDIM // 2), (PEER_QDIM // 2) ** -0.5),
        "peer_u": nrm(ks[12], (L, N_EXPERTS, D_MODEL), D_MODEL ** -0.5),
        "peer_v": nrm(ks[13], (L, N_EXPERTS, D_MODEL), (PEER_HEADS * PEER_TOPK) ** -0.5),
        "norm_final": 1.0 + nrm(ks[14], (D_MODEL,), 0.02),
    }

def first_block(x, norm_mix, w_in, fox_f_bias, nsa_cmp_pos, nsa_cmp_w1, nsa_cmp_w2, w_branch, w_out,
              norm_ffn, peer_wq, peer_subkeys, peer_u, peer_v, norm_final):
    h = x
    for l in range(DEPTH):
        h = h + hybrid_mixer(rmsnorm(h, norm_mix[l]), w_in[l], fox_f_bias[l], nsa_cmp_pos[l],
                             nsa_cmp_w1[l], nsa_cmp_w2[l], w_branch[l], w_out[l])
        h = h + peer_ffn(rmsnorm(h, norm_ffn[l]), peer_wq[l], peer_subkeys[l], peer_u[l], peer_v[l])
    return rmsnorm(h, norm_final)


DEPTH_2 = 2

N_META = 16
NORM_EPS = 1e-6

ATTN_HEAD_DIM = 64
ATTN_HEADS = D_MODEL // ATTN_HEAD_DIM
ATTN_KV_HEADS = ATTN_HEADS // 8
ATTN_GROUPS = ATTN_HEADS // ATTN_KV_HEADS
ATTN_WIDTH = ATTN_HEADS * ATTN_HEAD_DIM
ATTN_KV_WIDTH = ATTN_KV_HEADS * ATTN_HEAD_DIM
ATTN_IN = 2 * ATTN_WIDTH + 2 * ATTN_KV_WIDTH
WINDOW_2 = 128
ATTN_BLOCK = 128

DN_HEAD_DIM_K = 128
DN_HEAD_DIM_V = 128
DN_K_HEADS = D_MODEL // DN_HEAD_DIM_K
DN_V_HEADS = 2 * DN_K_HEADS
DN_KEY_WIDTH = DN_K_HEADS * DN_HEAD_DIM_K
DN_VALUE_WIDTH = DN_V_HEADS * DN_HEAD_DIM_V
DN_CONV = 4
DN_CHUNK = 64
DN_CONV_WIDTH = 2 * DN_KEY_WIDTH + DN_VALUE_WIDTH
DN_IN = DN_CONV_WIDTH + DN_VALUE_WIDTH + 2 * DN_V_HEADS

N_ATTN_LAYERS = (DEPTH_2 + 1) // 2
N_DN_LAYERS = DEPTH_2 // 2


def rms_norm(x, w):
    xf = x.astype(jnp.float32)
    y = xf * lax.rsqrt(jnp.mean(xf * xf, axis=-1, keepdims=True) + NORM_EPS)
    return (y * w.astype(jnp.float32)).astype(x.dtype)

def l2_norm(x):
    xf = x.astype(jnp.float32)
    return xf * lax.rsqrt(jnp.sum(xf * xf, axis=-1, keepdims=True) + NORM_EPS)

def alibi_slopes(n_heads):
    return jnp.asarray(np.exp2(-8.0 * np.arange(1, n_heads + 1) / n_heads), dtype=jnp.float32)

def banded_sink_attention(q, k, v, sinks):
    B, L = q.shape[:2]
    pad = ATTN_BLOCK - N_META
    Lp = L + pad
    nb = Lp // ATTN_BLOCK
    padt = lambda t: jnp.pad(t, ((0, 0), (pad, 0), (0, 0), (0, 0)))
    qb = padt(q).reshape(B, nb, ATTN_BLOCK, ATTN_KV_HEADS, ATTN_GROUPS, ATTN_HEAD_DIM)
    kb = padt(k).reshape(B, nb, ATTN_BLOCK, ATTN_KV_HEADS, ATTN_HEAD_DIM)
    vb = padt(v).reshape(B, nb, ATTN_BLOCK, ATTN_KV_HEADS, ATTN_HEAD_DIM)
    prev = lambda t: jnp.pad(t, ((0, 0), (1, 0), (0, 0), (0, 0), (0, 0)))[:, :-1]
    k_band = jnp.concatenate([prev(kb), kb], axis=2)
    v_band = jnp.concatenate([prev(vb), vb], axis=2)
    k_meta = k[:, :N_META]
    v_meta = v[:, :N_META]

    scale = ATTN_HEAD_DIM ** -0.5
    s_band = jnp.einsum('bnqhgd,bnkhd->bnhgqk', qb, k_band,
                        preferred_element_type=jnp.float32) * scale
    s_meta = jnp.einsum('bnqhgd,bmhd->bnhgqm', qb, k_meta,
                        preferred_element_type=jnp.float32) * scale

    pos_q = jnp.arange(Lp, dtype=jnp.int32).reshape(nb, ATTN_BLOCK) - pad
    pos_kb = jnp.concatenate([pos_q - ATTN_BLOCK, pos_q], axis=-1)
    pos_meta = jnp.arange(N_META, dtype=jnp.int32)
    dist_band = pos_q[:, :, None] - pos_kb[:, None, :]
    valid_band = (pos_kb[:, None, :] >= N_META) & (dist_band >= 0) & (dist_band < WINDOW_2)
    dist_meta = pos_q[:, :, None] - pos_meta[None, None, :]
    valid_meta = dist_meta >= 0

    slopes = alibi_slopes(ATTN_HEADS).reshape(1, 1, ATTN_KV_HEADS, ATTN_GROUPS, 1, 1)
    clipdist = lambda d: jnp.minimum(d, WINDOW_2).astype(jnp.float32)[None, :, None, None]
    s_band = jnp.where(valid_band[None, :, None, None], s_band - slopes * clipdist(dist_band), -jnp.inf)
    s_meta = jnp.where(valid_meta[None, :, None, None], s_meta - slopes * clipdist(dist_meta), -jnp.inf)

    sink = jnp.broadcast_to(
        sinks.astype(jnp.float32).reshape(1, 1, ATTN_KV_HEADS, ATTN_GROUPS, 1, 1),
        s_band.shape[:-1] + (1,))
    p = jax.nn.softmax(jnp.concatenate([s_band, s_meta, sink], axis=-1), axis=-1)
    p_band = p[..., :2 * ATTN_BLOCK].astype(v.dtype)
    p_meta = p[..., 2 * ATTN_BLOCK:2 * ATTN_BLOCK + N_META].astype(v.dtype)
    o = (jnp.einsum('bnhgqk,bnkhd->bnqhgd', p_band, v_band)
         + jnp.einsum('bnhgqm,bmhd->bnqhgd', p_meta, v_meta))
    return o.reshape(B, Lp, ATTN_WIDTH)[:, pad:]

def attention_mixer(h, norm_w, w_in, q_norm_w, k_norm_w, sinks, w_out):
    B, L, _ = h.shape
    u = rms_norm(h, norm_w) @ w_in
    q, k, v, gate = jnp.split(
        u, [ATTN_WIDTH, ATTN_WIDTH + ATTN_KV_WIDTH, ATTN_WIDTH + 2 * ATTN_KV_WIDTH], axis=-1)
    q = rms_norm(q.reshape(B, L, ATTN_HEADS, ATTN_HEAD_DIM), q_norm_w)
    k = rms_norm(k.reshape(B, L, ATTN_KV_HEADS, ATTN_HEAD_DIM), k_norm_w)
    v = v.reshape(B, L, ATTN_KV_HEADS, ATTN_HEAD_DIM)
    o = banded_sink_attention(q, k, v, sinks)
    return (o * jax.nn.silu(gate)) @ w_out

def causal_depthwise_conv(x, w):
    K, C = w.shape
    return lax.conv_general_dilated(
        x, w[:, None, :], window_strides=(1,), padding=[(K - 1, 0)],
        dimension_numbers=('NWC', 'WIO', 'NWC'), feature_group_count=C)

def chunked_gated_delta_rule(q, k, v, beta, g):
    B, L, H, _ = q.shape
    pad = DN_CHUNK - N_META
    Lc = L + pad
    n = Lc // DN_CHUNK

    def to_chunks(t):
        t = jnp.pad(t.astype(jnp.float32), [(0, 0), (pad, 0)] + [(0, 0)] * (t.ndim - 2))
        t = t.reshape((B, n, DN_CHUNK) + t.shape[2:])
        return jnp.swapaxes(jnp.moveaxis(t, 1, 0), 2, 3)

    xs = (to_chunks(q), to_chunks(k), to_chunks(v), to_chunks(beta), to_chunks(g))
    causal = jnp.tril(jnp.ones((DN_CHUNK, DN_CHUNK), dtype=bool))
    strict = jnp.tril(jnp.ones((DN_CHUNK, DN_CHUNK), dtype=bool), -1)
    eye = jnp.eye(DN_CHUNK, dtype=jnp.float32)

    def step(S, inp):
        qc, kc, vc, bc, gc = inp
        gcum = jnp.cumsum(gc, axis=-1)
        decay = jnp.exp(jnp.where(causal, gcum[..., :, None] - gcum[..., None, :], -jnp.inf))
        kb = kc * bc[..., None]
        m = jnp.where(strict, jnp.einsum('bhcd,bhsd->bhcs', kb, kc) * decay, 0.0)
        rhs = jnp.concatenate([vc * bc[..., None], kb * jnp.exp(gcum)[..., None]], axis=-1)
        sol = lax.linalg.triangular_solve(m + eye, rhs, left_side=True, lower=True,
                                          unit_diagonal=True)
        u, w = sol[..., :DN_HEAD_DIM_V], sol[..., DN_HEAD_DIM_V:]
        v_new = u - jnp.einsum('bhcd,bhdv->bhcv', w, S)
        attn = jnp.einsum('bhcd,bhsd->bhcs', qc, kc) * decay
        o = (jnp.einsum('bhcd,bhdv->bhcv', qc * jnp.exp(gcum)[..., None], S)
             + jnp.einsum('bhcs,bhsv->bhcv', attn, v_new))
        g_last = gcum[..., -1]
        k_state = kc * jnp.exp(g_last[..., None] - gcum)[..., None]
        S = S * jnp.exp(g_last)[..., None, None] + jnp.einsum('bhcd,bhcv->bhdv', k_state, v_new)
        return S, o

    S0 = jnp.zeros((B, H, DN_HEAD_DIM_K, DN_HEAD_DIM_V), jnp.float32)
    _, o = lax.scan(step, S0, xs)
    o = jnp.moveaxis(jnp.swapaxes(o, 2, 3), 0, 1).reshape(B, Lc, H, DN_HEAD_DIM_V)
    return o[:, pad:]

def deltanet_mixer(h, norm_w, w_in, conv_w, a_log, dt_bias, o_norm_w, w_out):
    B, L, _ = h.shape
    u = rms_norm(h, norm_w) @ w_in
    qkv, z, b, a = jnp.split(
        u, [DN_CONV_WIDTH, DN_CONV_WIDTH + DN_VALUE_WIDTH,
            DN_CONV_WIDTH + DN_VALUE_WIDTH + DN_V_HEADS], axis=-1)
    qkv = jax.nn.silu(causal_depthwise_conv(qkv, conv_w))
    q, k, v = jnp.split(qkv, [DN_KEY_WIDTH, 2 * DN_KEY_WIDTH], axis=-1)
    rep = DN_V_HEADS // DN_K_HEADS
    q = jnp.repeat(l2_norm(q.reshape(B, L, DN_K_HEADS, DN_HEAD_DIM_K)), rep, axis=2)
    k = jnp.repeat(l2_norm(k.reshape(B, L, DN_K_HEADS, DN_HEAD_DIM_K)), rep, axis=2)
    q = q * (DN_HEAD_DIM_K ** -0.5)
    v = v.reshape(B, L, DN_V_HEADS, DN_HEAD_DIM_V)
    beta = jax.nn.sigmoid(b.astype(jnp.float32))
    g = -jnp.exp(a_log.astype(jnp.float32)) * jax.nn.softplus(
        a.astype(jnp.float32) + dt_bias.astype(jnp.float32))
    o = chunked_gated_delta_rule(q, k, v, beta, g).astype(h.dtype)
    o = rms_norm(o, o_norm_w) * jax.nn.silu(z.reshape(B, L, DN_V_HEADS, DN_HEAD_DIM_V))
    return o.reshape(B, L, DN_VALUE_WIDTH) @ w_out

def second_inputs(seed: int = 0) -> dict:
    key = jax.random.key(seed)
    ks = jax.random.split(key, 20)
    f32 = jnp.float32
    nA, nB = N_ATTN_LAYERS, N_DN_LAYERS
    out_scale = 0.5
    dt = jnp.exp(jax.random.uniform(ks[13], (nB, DN_V_HEADS), f32,
                                    math.log(1e-3), math.log(1e-1)))
    return {
        "x": jax.random.normal(ks[0], (BATCH, SEQ, D_MODEL), f32),
        "meta_tokens": jax.random.normal(ks[1], (N_META, D_MODEL), f32),
        "attn_norm_w": 1.0 + 0.02 * jax.random.normal(ks[2], (nA, D_MODEL), f32),
        "attn_w_in": jax.random.normal(ks[3], (nA, D_MODEL, ATTN_IN), f32) * D_MODEL ** -0.5,
        "attn_q_norm_w": 1.0 + 0.02 * jax.random.normal(ks[4], (nA, ATTN_HEAD_DIM), f32),
        "attn_k_norm_w": 1.0 + 0.02 * jax.random.normal(ks[5], (nA, ATTN_HEAD_DIM), f32),
        "attn_sinks": 0.5 * jax.random.normal(ks[6], (nA, ATTN_HEADS), f32),
        "attn_w_out": jax.random.normal(ks[7], (nA, ATTN_WIDTH, D_MODEL), f32)
                      * ATTN_WIDTH ** -0.5 * out_scale,
        "dn_norm_w": 1.0 + 0.02 * jax.random.normal(ks[8], (nB, D_MODEL), f32),
        "dn_w_in": jax.random.normal(ks[9], (nB, D_MODEL, DN_IN), f32) * D_MODEL ** -0.5,
        "dn_conv_w": jax.random.normal(ks[10], (nB, DN_CONV, DN_CONV_WIDTH), f32) * DN_CONV ** -0.5,
        "dn_a_log": jnp.log(jax.random.uniform(ks[11], (nB, DN_V_HEADS), f32, 1.0, 16.0)),
        "dn_dt_bias": dt + jnp.log(-jnp.expm1(-dt)),
        "dn_o_norm_w": 1.0 + 0.02 * jax.random.normal(ks[12], (nB, DN_HEAD_DIM_V), f32),
        "dn_w_out": jax.random.normal(ks[14], (nB, DN_VALUE_WIDTH, D_MODEL), f32)
                    * DN_VALUE_WIDTH ** -0.5 * out_scale,
    }

def second_block(x, meta_tokens, attn_norm_w, attn_w_in, attn_q_norm_w, attn_k_norm_w,
              attn_sinks, attn_w_out, dn_norm_w, dn_w_in, dn_conv_w, dn_a_log,
              dn_dt_bias, dn_o_norm_w, dn_w_out):
    B = x.shape[0]
    meta = jnp.broadcast_to(meta_tokens.astype(x.dtype)[None], (B, N_META, x.shape[-1]))
    h = jnp.concatenate([meta, x], axis=1)
    for i in range(DEPTH_2):
        j = i // 2
        if i % 2 == 0:
            h = h + attention_mixer(h, attn_norm_w[j], attn_w_in[j], attn_q_norm_w[j],
                                    attn_k_norm_w[j], attn_sinks[j], attn_w_out[j])
        else:
            h = h + deltanet_mixer(h, dn_norm_w[j], dn_w_in[j], dn_conv_w[j], dn_a_log[j],
                                   dn_dt_bias[j], dn_o_norm_w[j], dn_w_out[j])
    return h[:, N_META:]


def setup_inputs(seed=0):
    out = dict(first_inputs(seed))
    for name, value in second_inputs(seed + 1).items():
        if name != "x":
            out[name + "_2"] = value
    return out


def reference(
    x, norm_mix, w_in, fox_f_bias, nsa_cmp_pos, nsa_cmp_w1, nsa_cmp_w2, w_branch, w_out,
    norm_ffn, peer_wq, peer_subkeys, peer_u, peer_v, norm_final, meta_tokens_2, attn_norm_w_2,
    attn_w_in_2, attn_q_norm_w_2, attn_k_norm_w_2, attn_sinks_2, attn_w_out_2, dn_norm_w_2,
    dn_w_in_2, dn_conv_w_2, dn_a_log_2, dn_dt_bias_2, dn_o_norm_w_2, dn_w_out_2,
):
    x = first_block(
        x, norm_mix, w_in, fox_f_bias, nsa_cmp_pos, nsa_cmp_w1, nsa_cmp_w2, w_branch, w_out,
        norm_ffn, peer_wq, peer_subkeys, peer_u, peer_v, norm_final,
    )
    return second_block(
        x, meta_tokens_2, attn_norm_w_2, attn_w_in_2, attn_q_norm_w_2, attn_k_norm_w_2,
        attn_sinks_2, attn_w_out_2, dn_norm_w_2, dn_w_in_2, dn_conv_w_2, dn_a_log_2,
        dn_dt_bias_2, dn_o_norm_w_2, dn_w_out_2,
    )


_drawn_inputs = setup_inputs


def setup_inputs(seed=0):
    import zlib

    import numpy as np

    out = dict(_drawn_inputs(seed))
    spreads = {}
    factors = {'norm_mix': 7.351,
     'fox_f_bias': 6.226,
     'nsa_cmp_pos': 8.0,
     'norm_ffn': 8.0,
     'norm_final': 2.683,
     'attn_norm_w_2': 8.0,
     'attn_q_norm_w_2': 8.0,
     'attn_k_norm_w_2': 8.0,
     'attn_sinks_2': 187.472,
     'dn_norm_w_2': 5.814,
     'dn_o_norm_w_2': 115.11}
    for name, (base, spread) in spreads.items():
        noise = np.random.default_rng([zlib.crc32(name.encode()), seed]).standard_normal(out[name].shape)
        drawn = base * np.exp(spread * noise) if base else spread * noise
        out[name] = __import__('jax').numpy.asarray(drawn.astype(out[name].dtype))
    for name, factor in factors.items():
        out[name] = (out[name] * factor).astype(out[name].dtype)
    return out
```

```python
from contextlib import ExitStack

import numpy as np
import concourse.bass as bass
from concourse import mybir

ALU = mybir.AluOpType
ACT = mybir.ActivationFunctionType
AX = mybir.AxisListType
F32 = mybir.dt.float32
U32 = mybir.dt.uint32

P = 128
D = 1024
KC = D // P
S = 256
NT = S // P
META = 16
L = META + S
HD = 64
NEG = -1e30
EPS = 1e-6
RING = 8
TILE = 1024

FQ, FK, NQ, KCMP, VCMP, KSL, KWN, MISC, MERGE = 0, 4, 8, 12, 13, 14, 16, 18, 19
N_IN_T = 35
GATE_ROW = 32
N_CMP = (S - 32) // 16 + 1
PH, TOPK = 8, 16
NKEY = 128
AH = 16
DNK, DNV = 8, 16
CH = 64
NCH = 5
PAD = NCH * CH - L


class Signal:

    def __init__(self, sem):
        self.sem, self.total, self.base = sem, 0, 0

    def up(self, n=1):
        self.total += n
        return self.sem, n

    def start(self):
        self.base = self.total

    def at(self, k):
        return self.sem, self.base + k

    def last(self):
        return self.sem, self.total


class Ring:

    def __init__(self, buf, landed, used):
        self.buf, self.landed, self.used = buf, landed, used
        self.slots, self.src, self.nth, self.count, self.next = [], [], [], [0] * RING, 0
        self.before, self.holder = [], [None] * RING

    def align(self):
        self.next = 0

    def add(self, src):
        s = self.next
        self.next = (s + 1) % RING
        self.count[s] += 1
        self.before.append(self.holder[s])
        self.holder[s] = len(self.slots)
        self.slots.append(s)
        self.nth.append(self.count[s])
        self.src.append(src)
        return len(self.slots) - 1

    def view(self, n):
        return self.buf[:, self.slots[n], :]


def plan(k):
    r, d = k.ring, k.dram
    k.tiles = {}

    def group(name, src, align=False):
        if align:
            r.align()
        k.tiles[name] = len(r.slots)
        for i in range(src.shape[0]):
            r.add(src[i])

    for name in ("in_t", "in_fv", "in_vv", "cmp_w1", "branch", "out1", "wq", "subk"):
        group(name, d[name])
    r.align()
    k.tiles["u"] = len(r.slots)
    for j in range(NKEY):
        r.add(d["peer_u"][j])
    r.align()
    k.tiles["v"] = len(r.slots)
    for j in range(NKEY):
        r.add(d["peer_v"][j])
    r.align()
    for name in [n for n in ("attn_t", "attn_v", "attn_out", "dn_qkv", "dn_ba", "dn_z", "dn_out") if n in d]:
        group(name, d[name])
    k.tiles["end"] = len(r.slots)


def load_tiles(sp, k, upto):
    r = k.ring
    while k.loaded < min(upto, k.tiles["end"]):
        n = k.loaded
        if r.before[n] is not None:
            if r.before[n] >= upto - RING:
                break
            sp.wait_ge(r.used.sem, r.before[n] + 1)
        sp.dma_start(r.view(n), r.src[n]).then_inc(r.landed[r.slots[n]], 16)
        k.loaded += 1


def landed(pe, k, n):
    pe.wait_ge(k.ring.landed[k.ring.slots[n]], 16 * k.ring.nth[n])


def tile_used(ins, k, n):
    assert k.ring.used.total == n, (k.ring.used.total, n)
    ins.then_inc(*k.ring.used.up())


def norm_stage(k, tiles, weight, out):
    nc, ps = k.nc, k.ps
    summed, meaned, rooted, scaled, turned = k.start("norm_summed", "norm_meaned", "norm_rooted",
                                                     "norm_scaled", "norm_turned")
    copied, = k.start("norm_copied")
    r = k.small[:, 0:16]
    xn = k.mid[:, 0:3 * D].rearrange("p (t n) -> p t n", t=3)
    with nc.Block() as block:

        @block.sync
        def _(sp):
            load_tiles(sp, k, k.prefetch)

        @block.scalar
        def _(act):
            for i, (h, rows, _) in enumerate(tiles):
                nc.scalar.activation(xn[0:rows, i, :], h, ACT.Square,
                                     accum_out=r[0:rows, i:i + 1]).then_inc(*summed.up())
            for i, (h, rows, _) in enumerate(tiles):
                act.wait_ge(*meaned.at(i + 1))
                nc.scalar.activation(r[0:rows, 6 + i:7 + i], r[0:rows, 3 + i:4 + i],
                                     ACT.Sqrt).then_inc(*rooted.up())

        @block.vector
        def _(dve):
            for i, (h, rows, _) in enumerate(tiles):
                dve.wait_ge(*summed.at(i + 1))
                nc.vector.tensor_scalar(r[0:rows, 3 + i:4 + i], r[0:rows, i:i + 1], 1.0 / D, EPS,
                                        ALU.mult, ALU.add).then_inc(*meaned.up())
            for i, (h, rows, _) in enumerate(tiles):
                dve.wait_ge(*rooted.at(i + 1))
                nc.vector.reciprocal(r[0:rows, 9 + i:10 + i], r[0:rows, 6 + i:7 + i]).then_inc(*meaned.up())
                dve.wait_ge(*meaned.last())
                y, inv, step = (r[0:rows, a + i:a + i + 1] for a in (3, 9, 12))
                nc.vector.scalar_tensor_tensor(step, inv, inv, y, ALU.mult, ALU.mult).then_inc(*meaned.up())
                dve.wait_ge(*meaned.last())
                nc.vector.tensor_scalar(step, step, -0.5, 1.5, ALU.mult, ALU.add).then_inc(*meaned.up())
                dve.wait_ge(*meaned.last())
                nc.vector.tensor_tensor(inv, inv, step, ALU.mult).then_inc(*meaned.up())
                dve.wait_ge(*meaned.last())
                nc.vector.tensor_scalar(xn[0:rows, i, :], h, inv, None, ALU.mult).then_inc(*scaled.up())
            for i, (_, rows, c0) in enumerate(tiles):
                for half in range(2):
                    dve.wait_ge(*turned.at(2 * i + half + 1))
                    turn = ps[:, 2 * i + half, 0:4 * rows].rearrange("p (c t) -> p c t", c=4)
                    w = weight[:, 4 * half:4 * half + 4].unsqueeze(2).broadcast_to([P, 4, rows])
                    nc.vector.tensor_tensor(out[:, 4 * half:4 * half + 4, c0:c0 + rows], turn, w,
                                            ALU.mult).then_inc(*copied.up())

        @block.tensor
        def _(pe):
            for i, (_, rows, _) in enumerate(tiles):
                pe.wait_ge(*scaled.at(i + 1))
                for c in range(KC):
                    ins = nc.tensor.transpose(ps[:, 2 * i + c // 4, (c % 4) * rows:(c % 4 + 1) * rows],
                                              xn[0:rows, i, c * P:(c + 1) * P], k.ident[0:rows, 0:rows])
                    if c % 4 == 3:
                        ins.then_inc(*turned.up())


def project_T(k, name, chunks, n, rhs, write, prefetch):
    nc, ps, first = k.nc, k.ps, k.tiles[name]
    engine, put = write
    by = {e: k.start("evacuated_" + e)[0] for e in ("vector", "scalar")}
    nth = [sum(engine(j) == engine(i) for j in range(i + 1)) for i in range(chunks)]
    with nc.Block() as block:

        @block.sync
        def _(sp):
            load_tiles(sp, k, prefetch)

        @block.tensor
        def _(pe):
            for i in range(chunks):
                t = k.ring.view(first + i).rearrange("p (c m) -> p c m", c=KC)
                landed(pe, k, first + i)
                if i >= 8:
                    pe.wait_ge(*by[engine(i - 8)].at(nth[i - 8]))
                for c in range(KC):
                    ins = nc.tensor.matmul(ps[:, i % 8, 0:n], t[:, c, :], rhs(c), start=c == 0, stop=c == KC - 1)
                tile_used(ins, k, first + i)

        @block.vector
        def _(dve):
            for i in range(chunks):
                if engine(i) == "vector":
                    dve.wait_ge(k.ring.used.sem, first + i + 1)
                    put(dve, i, ps[:, i % 8, 0:n]).then_inc(*by["vector"].up())

        @block.scalar
        def _(act):
            for i in range(chunks):
                if engine(i) == "scalar":
                    act.wait_ge(k.ring.used.sem, first + i + 1)
                    put(act, i, ps[:, i % 8, 0:n]).then_inc(*by["scalar"].up())


def project_N(k, name, lhs, groups, prefetch, pre=None):
    nc, first = k.nc, k.tiles[name]
    out, = k.start("rows_out")
    with nc.Block() as block:

        @block.sync
        def _(sp):
            load_tiles(sp, k, prefetch)

        @block.tensor
        def _(pe):
            n = first
            for tiles, per, cols, outs, _ in groups:
                for q in range(tiles):
                    t = k.ring.view(n).rearrange("p (c m) -> p c m", c=per)
                    landed(pe, k, n)
                    for c in range(per):
                        for o, i in outs:
                            ins = nc.tensor.matmul(o, lhs(q * per + c, i), t[:, c, 0:cols],
                                                   start=q + c == 0, stop=q == tiles - 1 and c == per - 1)
                    tile_used(ins, k, n)
                    n += 1

        @block.vector
        def _(dve):
            n = first
            for tiles, _, _, _, finish in groups:
                n += tiles
                dve.wait_ge(k.ring.used.sem, n)
                for ins in finish():
                    ins.then_inc(*out.up())


def input_stage(k):
    nc = k.nc
    got, = k.start("inputs_landed")
    with nc.Block() as block:

        @block.sync
        def _(sp):
            for dst, src in ((k.h, k.dram["x"]), (k.common[:, :], k.dram["const_common"]),
                             (k.param[:, :], k.dram["param"]), (k.hm[0:META, :], k.dram["meta"]),
                             (k.const1, k.dram["const_first"])):
                sp.dma_start(dst, src).then_inc(*got.up(16))
            load_tiles(sp, k, RING)
            sp.wait_ge(*got.last())


def prepare_stage(k):
    nc, ps, T = k.nc, k.ps, k.T
    vec, turned, filled, acted = k.start("prep_vector", "prep_product", "prep_gelu", "prep_act")
    first = k.tiles["cmp_w1"]
    f = k.mid[0:PH, 0:4 * S].rearrange("p (a n) -> p a n", a=4)
    blocks = k.cmp_in
    rot = k.rot
    gl = k.gelu
    with nc.Block() as block:

        @block.sync
        def _(sp):
            load_tiles(sp, k, k.tiles["cmp_w1"] + 8 + RING)

        @block.scalar
        def _(act):
            gate = T[GATE_ROW:GATE_ROW + 24, MISC, :]
            nc.scalar.activation(gate, gate, ACT.Sigmoid).then_inc(*acted.up())
            act.wait_ge(*vec.at(4))
            nc.scalar.activation(f[:, 1, :], f[:, 1, :], ACT.Exp).then_inc(*acted.up())
            act.wait_ge(*acted.last())
            nc.scalar.activation(f[:, 2, :], f[:, 1, :], ACT.Ln, bias=1.0).then_inc(*acted.up())
            for j in range(2):
                act.wait_ge(k.ring.used.sem, first + 4 * j + 4)
                for g in range(2):
                    nc.scalar.activation(gl[:, j, g, :], ps[:, 2 * j + g, 0:N_CMP],
                                         ACT.Gelu).then_inc(*filled.up())

        @block.vector
        def _(dve):
            for j in range(2):
                src = T[:, KCMP + j, :]
                src = bass.AP(src.tensor, src.offset, [list(src.ap[0]), [16, N_CMP], [1, 32]])
                pos = k.p("pos")[:, 32 * j:32 * j + 32].unsqueeze(1).broadcast_to([P, N_CMP, 32])
                nc.vector.tensor_tensor(blocks[:, j, :, :], src, pos, ALU.add).then_inc(*vec.up())
            nc.vector.tensor_scalar(f[:, 0, :], T[0:PH, MISC, :], k.p("fbias")[0:PH, :], None,
                                    ALU.add).then_inc(*vec.up())
            dve.wait_ge(*vec.last())
            nc.vector.scalar_tensor_tensor(f[:, 1, :], f[:, 0, :], -1.0, f[:, 0, :], ALU.mult,
                                           ALU.min).then_inc(*vec.up())
            dve.wait_ge(*acted.at(3))
            nc.vector.scalar_tensor_tensor(f[:, 3, :], f[:, 0, :], 0.0, f[:, 2, :], ALU.min,
                                           ALU.subtract).then_inc(*vec.up())
            dve.wait_ge(*vec.last())
            nc.vector.tensor_tensor_scan(f[:, 1, :], k.c("ones")[0:PH, 0:1].broadcast_to([PH, S]), f[:, 3, :], 0.0,
                                         ALU.mult, ALU.add).then_inc(*vec.up())
            dve.wait_ge(*vec.last())
            for base in (0, HD):
                nc.vector.tensor_scalar(k.negc[base:base + PH, :], f[:, 1, :], -8.0, None,
                                        ALU.mult).then_inc(*vec.up())
            dve.wait_ge(*turned.at(1))
            nc.vector.tensor_copy(k.gates, ps[:, 4:6, 0:24]).then_inc(*vec.up())
            for b, c0 in enumerate((NQ, KSL)):
                dve.wait_ge(*turned.at(2 + b))
                x, y = T[:, c0:c0 + 4, :], rot[:, :, :]
                sin = k.c("sin").unsqueeze(1).broadcast_to([P, 4, S])
                cos = k.c("cos").unsqueeze(1).broadcast_to([P, 4, S])
                swapped = ps[:, 6:8, :].rearrange("p b (c n) -> p (b c) n", c=2)
                nc.vector.tensor_tensor(y, swapped, sin, ALU.mult).then_inc(*vec.up())
                nc.vector.tensor_tensor(x, x, cos, ALU.mult).then_inc(*vec.up())
                dve.wait_ge(*vec.last())
                nc.vector.tensor_tensor(x, x, y, ALU.add).then_inc(*vec.up())
                dve.wait_ge(*vec.last())
            dve.wait_ge(*turned.at(4))
            nc.vector.tensor_copy(k.kcmp, ps[:, 4, 0:2 * N_CMP]).then_inc(*vec.up())
            nc.vector.tensor_copy(k.vcmp, ps[0:N_CMP, 5, 0:P]).then_inc(*vec.up())
            dve.wait_ge(*vec.last())
            kc = k.kcmp.rearrange("p (g n) -> p g n", g=2)
            tmp = rot[:, 0, 0:2 * N_CMP].rearrange("p (g n) -> p g n", g=2)
            cos = k.c("ccos")[:, 0:N_CMP].unsqueeze(1).broadcast_to([P, 2, N_CMP])
            sin = k.c("csin")[:, 0:N_CMP].unsqueeze(1).broadcast_to([P, 2, N_CMP])
            dve.wait_ge(*turned.at(5))
            nc.vector.tensor_tensor(tmp, ps[:, 6, 0:2 * N_CMP].rearrange("p (g n) -> p g n", g=2), sin,
                                    ALU.mult).then_inc(*vec.up())
            nc.vector.tensor_tensor(kc, kc, cos, ALU.mult).then_inc(*vec.up())
            dve.wait_ge(*vec.last())
            nc.vector.tensor_tensor(kc, kc, tmp, ALU.add).then_inc(*vec.up())

        @block.tensor
        def _(pe):
            pe.wait_ge(*acted.at(1))
            for tt in range(NT):
                ins = nc.tensor.transpose(ps[:, 4 + tt, 0:24], T[GATE_ROW:GATE_ROW + 24, MISC, tt * P:tt * P + P],
                                          k.ident[GATE_ROW:GATE_ROW + 24, GATE_ROW:GATE_ROW + 24])
            ins.then_inc(*turned.up())
            for b, c0 in enumerate((NQ, KSL)):
                if b:
                    pe.wait_ge(*vec.at(10))
                for c in range(4):
                    ins = nc.tensor.matmul(ps[:, 6 + c // 2, (c % 2) * S:(c % 2) * S + S], k.c("perm"),
                                           T[:, c0 + c, :], start=True, stop=True)
                ins.then_inc(*turned.up())
            pe.wait_ge(*vec.at(2))
            for j in range(2):
                for q in range(4):
                    n = first + 4 * j + q
                    landed(pe, k, n)
                    w = k.ring.view(n).rearrange("p (l m) -> p l m", l=8)
                    for g in range(2):
                        for l in range(8):
                            rows = slice(HD * g, HD * g + HD)
                            ins = nc.tensor.matmul(ps[:, 2 * j + g, 0:N_CMP], w[rows, l, :],
                                                   blocks[rows, j, :, 8 * q + l], start=q + l == 0,
                                                   stop=q == 3 and l == 7)
                    tile_used(ins, k, n)
            pe.wait_ge(*vec.at(9))
            pe.wait_ge(*filled.at(4))
            for g in range(2):
                nc.tensor.matmul(ps[:, 4, g * N_CMP:(g + 1) * N_CMP], k.p("w2k"), gl[:, 0, g, :],
                                 start=True, stop=True)
                ins = nc.tensor.matmul(ps[0:N_CMP, 5, g * HD:(g + 1) * HD], gl[:, 1, g, :], k.p("w2v"),
                                       start=True, stop=True)
            ins.then_inc(*turned.up())
            pe.wait_ge(*vec.at(17))
            nc.tensor.matmul(ps[:, 6, 0:2 * N_CMP], k.c("perm"), k.kcmp, start=True,
                             stop=True).then_inc(*turned.up())


def attention_stage(k):
    nc, ps, T = k.nc, k.ps, k.T
    scored, masked, peaked, exped = k.start("att_scored", "att_masked", "att_peaked", "att_exped")
    scaled, turned, unturned, summed = k.start("att_scaled", "att_turned", "att_copied", "att_valued")
    stored, stats = k.start("att_stored", "att_stats")
    units = []
    for tt in range(NT):
        units += [(tt, "fox", 0), (tt, "fox", 1), (tt, "cmp", 0)]
        units += [(tt, b, g) for g in range(2) for b in ("slc", "win")]
    n_exp = [0]
    for _, kind, _ in units:
        n_exp.append(n_exp[-1] + (1 if kind == "cmp" else 4))
    valued = [u for u, (_, kind, _) in enumerate(units) if kind in ("fox", "win")]
    done_by = lambda u: sum(v <= u for v in valued)
    soft = k.soft
    pt, ptc, st = k.pt, k.ptc, k.small[:, 0:96].rearrange("p (s a h) -> p s a h", s=2, a=6)
    few = lambda ap: ap.rearrange("p a b -> p (a b)")[:, 0:PH * 16].rearrange("p (h n) -> p h n", h=PH)[:, :, 0:N_CMP]
    wide = lambda ap, n, m: ap.unsqueeze(2).broadcast_to([P, n, m])
    place = lambda j: 2 * (j % 2) + j // 2
    place_few = lambda h: 4 * (h % 2) + h // 2
    few_scores = lambda s: ps[:, 2 * s:2 * s + 2, 0:4 * 16].rearrange("p b (c n) -> p b c n", n=16)[:, :, :, 0:N_CMP]
    with nc.Block() as block:

        @block.sync
        def _(sp):
            load_tiles(sp, k, k.tiles["branch"] + RING)

        @block.tensor
        def _(pe):
            def scores(u):
                tt, kind, a = units[u]
                if u >= 2:
                    pe.wait_ge(*masked.at(u - 1))
                q = slice(tt * P, tt * P + P)
                n = (tt + 1) * P
                out = ps[:, 2 * (u % 2):2 * (u % 2) + 2, :].rearrange("p b (h n) -> p (b h) n", h=2)
                if kind == "cmp":
                    out = few_scores(u % 2)
                    for h in range(PH):
                        g = h // 4
                        rows = slice(HD * (h % 2), HD * (h % 2) + HD)
                        ins = nc.tensor.matmul(out[:, h % 2, h // 2, :], T[rows, NQ + h // 2, q],
                                               k.kcmp[rows, g * N_CMP:(g + 1) * N_CMP], start=True, stop=True)
                else:
                    for j in range(4):
                        h = 4 * a + j
                        rows = slice(HD * (h % 2), HD * (h % 2) + HD)
                        if kind == "fox":
                            nc.tensor.matmul(out[:, place(j), 0:n], T[rows, FQ + h // 2, q],
                                             T[rows, FK + h // 2, 0:n], start=True, stop=False)
                            head = slice(HD * (h % 2), HD * (h % 2) + PH)
                            ins = nc.tensor.matmul(out[:, place(j), 0:n], k.ident[head, head.start + h:head.start + h + 1].broadcast_to([PH, P]),
                                                   k.negc[head, 0:n], start=False, stop=True)
                        else:
                            keys = (KSL if kind == "slc" else KWN) + a
                            ins = nc.tensor.matmul(out[:, place(j), 0:n], T[rows, NQ + h // 2, q],
                                                   T[rows, keys, 0:n], start=True, stop=True)
                ins.then_inc(*scored.up())

            def turn(u):
                tt, kind, _ = units[u]
                pe.wait_ge(*scaled.at(u + 1))
                if u:
                    pe.wait_ge(*unturned.at(u))
                if kind == "cmp":
                    src = few(soft[:, u % 2, :, :])
                    for h in range(PH):
                        ins = nc.tensor.transpose(ps[0:N_CMP, 4 + h // 4, (h % 4) * P:(h % 4) * P + P],
                                                  src[:, h, :], k.ident)
                else:
                    for kt in range(tt + 1):
                        for j in range(4):
                            ins = nc.tensor.transpose(ps[:, 4 + kt, j * P:j * P + P],
                                                      soft[:, u % 2, j, kt * P:kt * P + P], k.ident)
                ins.then_inc(*turned.up())

            def values(u):
                tt, kind, a = units[u]
                if kind not in ("fox", "win"):
                    return
                m = done_by(u) - 1
                pe.wait_ge(*unturned.at(u + 1))
                if m >= 2:
                    pe.wait_ge(*stored.at(m - 1))
                for j in range(4):
                    h = 4 * a + j
                    out = ps[HD * (j % 2):HD * (j % 2) + HD, 6 + m % 2, (j // 2) * P:(j // 2) * P + P]
                    terms = []
                    if kind == "fox":
                        for kt in range(tt + 1):
                            terms.append((k.fv[:, kt, h * HD:(h + 1) * HD], pt[:, u % 3, kt, place(j), :]))
                    else:
                        terms.append((k.vcmp[:, a * HD:(a + 1) * HD], ptc[0:N_CMP, place_few(h), :]))
                        for b in range(2):
                            for kt in range(tt + 1):
                                terms.append((k.vv[:, kt, b * P + a * HD:b * P + (a + 1) * HD],
                                              pt[:, (u - 1 + b) % 3, kt, place(j), :]))
                    for i, (v, p) in enumerate(terms):
                        ins = nc.tensor.matmul(out, v, p, start=i == 0, stop=i == len(terms) - 1)
                ins.then_inc(*summed.up())

            scores(0)
            for u in range(len(units) + 1):
                if u + 1 < len(units):
                    scores(u + 1)
                if u < len(units):
                    turn(u)
                if u:
                    values(u - 1)

        @block.vector
        def _(dve):
            def peaks(u):
                tt, kind, _ = units[u]
                n = (tt + 1) * P
                dve.wait_ge(*scored.at(u + 1))
                if u >= 2:
                    dve.wait_ge(*turned.at(u - 1))
                s = u % 2
                out = ps[:, 2 * s:2 * s + 2, :].rearrange("p b (h n) -> p (b h) n", h=2)
                if kind == "cmp":
                    src, dst = few_scores(s), few(soft[:, s, :, :]).rearrange("p (b c) n -> p b c n", b=2)
                    mask = k.c("cmask")[:, 16 * tt:16 * tt + N_CMP].unsqueeze(1).broadcast_to([P, 4, N_CMP])
                    heads = PH
                else:
                    src, dst = out[:, :, 0:n], soft[:, s, :, 0:n]
                    mask = k.c("mask")[:, S * tt:S * tt + n].unsqueeze(1).broadcast_to([P, 4, n])
                    heads = 4
                if kind == "cmp":
                    nc.vector.scalar_tensor_tensor(dst[:, 0, :, :], src[:, 0, :, :], HD ** -0.5, mask,
                                                   ALU.mult, ALU.add).then_inc(*stats.up())
                    dve.wait_ge(*stats.last())
                    dst, src = dst[:, 1, :, :], src[:, 1, :, :]
                nc.vector.scalar_tensor_tensor(dst, src, HD ** -0.5, mask, ALU.mult, ALU.add).then_inc(*masked.up())
                dve.wait_ge(*masked.last())
                if kind == "cmp":
                    dst = few(soft[:, s, :, :])
                nc.vector.tensor_reduce(st[:, s, 0, 0:heads], dst, AX.X, ALU.max).then_inc(*stats.up())
                dve.wait_ge(*stats.last())
                if kind == "cmp":
                    nc.vector.tensor_tensor(dst, dst, wide(st[:, s, 0, 0:heads], heads, N_CMP),
                                            ALU.subtract).then_inc(*peaked.up())
                else:
                    nc.vector.tensor_scalar(st[:, s, 1, 0:4], st[:, s, 0, 0:4], -1.0, None,
                                            ALU.mult).then_inc(*peaked.up())

            def scale(u):
                tt, kind, a = units[u]
                s = u % 2
                n = (tt + 1) * P
                dve.wait_ge(*exped.at(n_exp[u + 1]))
                if kind == "cmp":
                    dst, heads, n = few(soft[:, s, :, :]), PH, N_CMP
                    nc.vector.tensor_reduce(st[:, s, 2, :], dst, AX.X, ALU.add).then_inc(*stats.up())
                    dve.wait_ge(*stats.last())
                else:
                    dst, heads = soft[:, s, :, 0:n], 4
                nc.vector.reciprocal(st[:, s, 3, 0:heads], st[:, s, 2, 0:heads]).then_inc(*stats.up())
                dve.wait_ge(*stats.last())
                w = st[:, s, 3, 0:heads]
                if kind != "fox":
                    b = ("cmp", "slc", "win").index(kind)
                    gate = k.gates[:, tt, 12 * a:12 * a + 3 * heads].rearrange("p (c o r) -> p o c r", o=2, r=3)[:, :, :, b]
                    nc.vector.tensor_tensor(st[:, s, 4, 0:heads].rearrange("p (o c) -> p o c", o=2),
                                            w.rearrange("p (o c) -> p o c", o=2), gate, ALU.mult).then_inc(*stats.up())
                    dve.wait_ge(*stats.last())
                    w = st[:, s, 4, 0:heads]
                if kind == "cmp":
                    keep = k.c("ckeep")[:, 16 * tt:16 * tt + N_CMP].unsqueeze(1).broadcast_to([P, PH, N_CMP])
                    nc.vector.tensor_tensor(dst, dst, keep, ALU.mult).then_inc(*stats.up())
                    dve.wait_ge(*stats.last())
                nc.vector.tensor_tensor(dst, dst, wide(w, heads, n), ALU.mult).then_inc(*scaled.up())

            for u in range(len(units) + 1):
                if u < len(units):
                    peaks(u)
                if u:
                    scale(u - 1)

        @block.scalar
        def _(act):
            def exps(u):
                tt, kind, _ = units[u]
                s = u % 2
                act.wait_ge(*peaked.at(u + 1))
                if kind == "cmp":
                    dst = few(soft[:, s, :, :])
                    nc.scalar.activation(dst, dst, ACT.Exp).then_inc(*exped.up())
                    return
                for j in range(4):
                    p = soft[:, s, j, 0:(tt + 1) * P]
                    nc.scalar.activation(p, p, ACT.Exp, bias=st[:, s, 1, j:j + 1],
                                         accum_out=st[:, s, 2, j:j + 1]).then_inc(*exped.up())

            def copy_turned(u):
                tt, kind, _ = units[u]
                act.wait_ge(*turned.at(u + 1))
                if u >= 3 and done_by(u - 2):
                    act.wait_ge(*summed.at(done_by(u - 2)))
                if kind == "cmp":
                    nc.scalar.activation(ptc[0:N_CMP, :, :].rearrange("p (a h) n -> p a (h n)", a=2),
                                         ps[0:N_CMP, 4:6, :], ACT.Copy).then_inc(*unturned.up())
                else:
                    nc.scalar.activation(pt[:, u % 3, 0:tt + 1, :, :].rearrange("p t h n -> p t (h n)"),
                                         ps[:, 4:5 + tt, :], ACT.Copy).then_inc(*unturned.up())

            def store(u):
                tt, kind, a = units[u]
                if kind not in ("fox", "win"):
                    return
                m = done_by(u) - 1
                act.wait_ge(*summed.at(m + 1))
                y = k.yfox if kind == "fox" else k.ynsa
                nc.scalar.activation(y[:, 2 * a:2 * a + 2, tt * P:tt * P + P],
                                     ps[:, 6 + m % 2, 0:2 * P].rearrange("p (c n) -> p c n", c=2),
                                     ACT.Copy).then_inc(*stored.up())

            for u in range(len(units) + 2):
                if u < len(units):
                    exps(u)
                if 1 <= u <= len(units):
                    copy_turned(u - 1)
                if u >= 2:
                    store(u - 2)


def merge_stage(k):
    nc, ps = k.nc, k.ps
    first = k.tiles["branch"]
    gated, merged = k.start("merge_gated", "merged")
    t = k.mid[:, 0:4 * S].rearrange("p (a n) -> p a n", a=4)
    with nc.Block() as block:

        @block.sync
        def _(sp):
            load_tiles(sp, k, k.tiles["out1"] + RING)

        @block.tensor
        def _(pe):
            for c in range(KC):
                landed(pe, k, first + c)
                w = k.ring.view(first + c).rearrange("p (b c m) -> p b c m", b=2, c=4)
                if c >= 4:
                    pe.wait_ge(*gated.at(2 * (c - 3)))
                for b, y in enumerate((k.yfox, k.ynsa)):
                    for q in range(4):
                        ins = nc.tensor.matmul(ps[:, 2 * (c % 4) + b, 0:S], w[:, b, q, :], y[:, q, :],
                                               start=q == 0, stop=q == 3)
                tile_used(ins, k, first + c)

        @block.vector
        def _(dve):
            for c in range(KC):
                dve.wait_ge(k.ring.used.sem, first + c + 1)
                if c >= 2:
                    dve.wait_ge(*merged.at(c - 1))
                for b in range(2):
                    nc.vector.tensor_tensor(t[:, 2 * (c % 2) + b, :], ps[:, 2 * (c % 4) + b, 0:S],
                                            k.T[:, MERGE + KC * b + c, :], ALU.mult).then_inc(*gated.up())
                dve.wait_ge(*gated.last())
                nc.vector.tensor_tensor(k.mergedT[:, c, :], t[:, 2 * (c % 2), :], t[:, 2 * (c % 2) + 1, :],
                                        ALU.add).then_inc(*merged.up())




def scores_stage(k):
    nc, ps = k.nc, k.ps
    first = k.tiles["subk"]
    taken, = k.start("scores_taken")
    with nc.Block() as block:

        @block.sync
        def _(sp):
            load_tiles(sp, k, k.tiles["u"] + RING)

        @block.tensor
        def _(pe):
            for q in range(2):
                landed(pe, k, first + q)
                keys = k.ring.view(first + q).rearrange("p (a n) -> p a n", a=8)
                for a in range(8):
                    for tt in range(NT):
                        ins = nc.tensor.matmul(ps[:, 4 * tt + 2 * q + a // 4, (a % 4) * P:(a % 4) * P + P],
                                               k.qT[:, 8 * q + a, tt * P:tt * P + P], keys[:, a, :],
                                               start=True, stop=True)
                tile_used(ins, k, first + q)

        @block.vector
        def _(dve):
            for q in range(2):
                dve.wait_ge(k.ring.used.sem, first + q + 1)
                for tt in range(NT):
                    src = ps[:, 4 * tt + 2 * q:4 * tt + 2 * q + 2, :].rearrange("p b n -> p (b n)")
                    nc.vector.tensor_copy(k.score[:, tt, 8 * q:8 * q + 8, :].rearrange("p a n -> p (a n)"),
                                          src).then_inc(*taken.up())


def top16(nc, dve, sig, values, top, index):
    for half in range(2):
        best, at = top[:, 8 * half:8 * half + 8], index[:, 8 * half:8 * half + 8]
        nc.vector.max(best, values).then_inc(*sig.up())
        dve.wait_ge(*sig.last())
        nc.vector.max_index(at, best, values).then_inc(*sig.up())
        if half == 0:
            dve.wait_ge(*sig.last())
            nc.vector.match_replace(values, best, values, -3e38).then_inc(*sig.up())
            dve.wait_ge(*sig.last())


def experts_in_stage(k):
    nc, ps = k.nc, k.ps
    first = k.tiles["u"]
    gelu, pick, = k.start("gelu_stored", "top_picked")
    ring, src = k.ring, k.dram["peer_u"]
    used = ring.used
    rounds = NKEY // RING
    n0 = [16 * (ring.nth[first + j] - 1) for j in range(RING)]
    assert k.loaded == first + RING and used.total == first
    with nc.Block() as block:

        @block.sync
        def _(sp):
            with sp.Fori(1, rounds) as i:
                for j in range(RING):
                    sp.wait_ge(used.sem, i * RING + (first + j - RING + 1))
                    sp.dma_start(ring.buf[:, j, :], src[bass.ds(i * RING + j, 1), :, :].rearrange("a p n -> (a p) n")
                                 ).then_inc(ring.landed[j], 16)
            k.loaded = first + NKEY
            for j in range(RING):
                sp.wait_ge(used.sem, k.loaded - RING + 1)
                sp.dma_start(ring.buf[:, j, :], ring.src[k.loaded]).then_inc(ring.landed[j], 16)
                k.loaded += 1

        @block.tensor
        def _(pe):
            def one_round(i):
                for j in range(RING):
                    w = ring.buf[:, j, :].rearrange("p (c m) -> p c m", c=KC)
                    pe.wait_ge(ring.landed[j], i * 16 + (n0[j] + 16))
                    if type(i) is not int:
                        pe.wait_ge(gelu.sem, i * RING + (gelu.base + j - RING + 1))
                    for c in range(KC):
                        ins = nc.tensor.matmul(ps[:, j, 0:S], w[:, c, :], k.hT[:, c, 0:S],
                                               start=c == 0, stop=c == KC - 1)
                    ins.then_inc(used.sem, 1)
            one_round(0)
            with pe.Fori(1, rounds) as i:
                one_round(i)

        @block.scalar
        def _(act):
            def one_round(i):
                for j in range(RING):
                    act.wait_ge(used.sem, i * RING + (first + j + 1))
                    out = k.coef[:, j, :] if type(i) is int else k.coef[:, bass.ds(i * RING + j, 1), :].rearrange("p a t -> p (a t)")
                    nc.scalar.activation(out, ps[:, j, 0:S], ACT.Gelu).then_inc(gelu.sem, 1)
            one_round(0)
            with act.Fori(1, rounds) as i:
                one_round(i)

        @block.vector
        def _(dve):
            def wait():
                dve.wait_ge(*pick.last())
            for tt in range(NT):
                for a in range(2 * PH):
                    top16(nc, dve, pick, k.score[:, tt, a, :], k.top[:, a, :], k.at[:, a, :])
                wait()
                nc.vector.tensor_copy(k.atf, k.at).then_inc(*pick.up())
                cand = k.score[:, tt, :, :].rearrange("p a n -> p (a n)").rearrange("p (h a b) -> p h a b", h=PH, a=TOPK)
                halves = k.top.rearrange("p (h o) a -> p o h a", o=2)
                nc.vector.tensor_tensor(cand, halves[:, 0].unsqueeze(3).broadcast_to([P, PH, TOPK, TOPK]),
                                        halves[:, 1].unsqueeze(2).broadcast_to([P, PH, TOPK, TOPK]),
                                        ALU.add).then_inc(*pick.up())
                wait()
                for h in range(PH):
                    top16(nc, dve, pick, cand[:, h].rearrange("p a b -> p (a b)"), k.best[:, tt, h, :], k.pos[:, h, :])
                wait()
                flat = lambda ap: ap.rearrange("p h a -> p (h a)")
                for o, (op, operand) in enumerate(((ALU.logical_shift_right, 4), (ALU.bitwise_and, 15))):
                    nc.vector.tensor_scalar(flat(k.part), flat(k.pos), operand, None, op).then_inc(*pick.up())
                    wait()
                    nc.vector.tensor_copy(k.partf, k.part).then_inc(*pick.up())
                    wait()
                    eq = k.score[:, tt, :, :].rearrange("p a n -> p (a n)").rearrange("p (h a b) -> p h a b", h=PH, a=TOPK)
                    eq3 = eq.rearrange("p h a b -> p (h a) b")
                    nc.vector.tensor_tensor(eq3, flat(k.partf).unsqueeze(2).broadcast_to([P, P, TOPK]),
                                            k.c("iota")[:, 0:TOPK].unsqueeze(1).broadcast_to([P, P, TOPK]),
                                            ALU.is_equal).then_inc(*pick.up())
                    wait()
                    table = k.atf.rearrange("p (h o) a -> p o h a", o=2)[:, o].unsqueeze(2).broadcast_to([P, PH, TOPK, TOPK])
                    nc.vector.tensor_tensor(eq, eq, table, ALU.mult).then_inc(*pick.up())
                    wait()
                    nc.vector.tensor_reduce(k.chosen[:, tt, o, :], eq3, AX.X, ALU.add).then_inc(*pick.up())
    used.total += NKEY
    gelu.total += NKEY


def choice_stage(k):
    nc, ps = k.nc, k.ps
    vec, exped, turned = k.start("choice_vector", "choice_exped", "choice_turned")
    best = k.best.rearrange("p t h a -> p (t h) a")
    lead, total, inverse = (k.small[:, 16 * i:16 * i + 16] for i in range(3))
    wide = lambda ap: ap.unsqueeze(2).broadcast_to([P, NT * PH, TOPK])
    with nc.Block() as block:

        @block.vector
        def _(dve):
            nc.vector.tensor_copy(lead, best[:, :, 0]).then_inc(*vec.up())
            dve.wait_ge(*vec.last())
            nc.vector.tensor_tensor(best, best, wide(lead), ALU.subtract).then_inc(*vec.up())
            dve.wait_ge(*exped.at(1))
            nc.vector.tensor_reduce(total, best, AX.X, ALU.add).then_inc(*vec.up())
            dve.wait_ge(*vec.last())
            nc.vector.reciprocal(inverse, total).then_inc(*vec.up())
            dve.wait_ge(*vec.last())
            nc.vector.tensor_tensor(best, best, wide(inverse), ALU.mult).then_inc(*vec.up())
            for o in range(3):
                dve.wait_ge(*turned.at(o + 1))
                nc.vector.tensor_copy(k.chosenT[:, o, :], ps[:, o, 0:S]).then_inc(*vec.up())

        @block.scalar
        def _(act):
            act.wait_ge(*vec.at(2))
            nc.scalar.activation(best, best, ACT.Exp).then_inc(*exped.up())

        @block.tensor
        def _(pe):
            for o in range(3):
                if o == 2:
                    pe.wait_ge(*vec.at(5))
                for tt in range(NT):
                    src = k.chosen[:, tt, o, :] if o < 2 else k.best[:, tt].rearrange("p h a -> p (h a)")
                    ins = nc.tensor.transpose(ps[:, o, tt * P:tt * P + P], src, k.ident)
                ins.then_inc(*turned.up())


def weight_stage(k):
    nc, ps = k.nc, k.ps
    hot, spread, folded = k.start("hot_made", "weights_spread", "coef_made")
    Q = 4
    G = 2
    rounds = S // (Q * G)
    row = k.onehot
    iota = k.c("iota")
    with nc.Block() as block:

        @block.vector
        def _(dve):
            def make(i, g):
                if type(i) is not int:
                    dve.wait_ge(spread.sem, i * G + (spread.base + g - G + 1))
                for q in range(Q):
                    t = i * (Q * G) + (g * Q + q)
                    at = lambda o: k.chosenT[:, o, t:t + 1] if type(i) is int else k.chosenT[:, o, bass.ds(t, 1)]
                    nc.vector.tensor_scalar(row[:, g, 0, q, :], iota, at(0), None, ALU.is_equal).then_inc(hot.sem, 1)
                    nc.vector.tensor_scalar(row[:, g, 1, q, :], iota, at(1), at(2), ALU.is_equal,
                                            ALU.mult).then_inc(hot.sem, 1)

            def fold(i, g):
                t = i * (Q * G) + g * Q
                c = k.coef[:, :, t:t + Q] if type(i) is int else k.coef[:, :, bass.ds(t, Q)]
                c = c.rearrange("p j t -> p t j")
                dve.wait_ge(spread.sem, i * G + (spread.base + g + 1))
                nc.vector.tensor_tensor(c, ps[:, g, :].rearrange("p (t j) -> p t j", t=Q), c,
                                        ALU.mult).then_inc(folded.sem, 1)

            def one_round(i):
                for g in range(G):
                    make(i, g)
                for g in range(G):
                    fold(i, g)
            one_round(0)
            with dve.Fori(1, rounds) as i:
                one_round(i)

        @block.tensor
        def _(pe):
            def one_round(i):
                for g in range(G):
                    pe.wait_ge(hot.sem, i * (2 * Q * G) + (hot.base + 2 * Q * (g + 1)))
                    if type(i) is not int:
                        pe.wait_ge(folded.sem, i * G + (folded.base + g - G + 1))
                    for q in range(Q):
                        ins = nc.tensor.matmul(ps[:, g, q * P:(q + 1) * P], row[:, g, 0, q, :], row[:, g, 1, q, :],
                                               start=True, stop=True)
                    ins.then_inc(spread.sem, 1)
            one_round(0)
            with pe.Fori(1, rounds) as i:
                one_round(i)
    hot.total += 2 * S
    spread.total += S // Q
    folded.total += S // Q


def experts_out_stage(k):
    nc, ps = k.nc, k.ps
    first = k.tiles["v"]
    staged, added = k.start("coef_staged", "experts_added")
    ring, src = k.ring, k.dram["peer_v"]
    used = ring.used
    rounds = NKEY // RING
    n0 = [16 * (ring.nth[first + j] - 1) for j in range(RING)]
    assert k.loaded == first + RING and used.total == first
    stage = k.stage
    with nc.Block() as block:

        @block.sync
        def _(sp):
            with sp.Fori(1, rounds) as i:
                for j in range(RING):
                    sp.wait_ge(used.sem, i * RING + (first + j - RING + 1))
                    sp.dma_start(ring.buf[:, j, :], src[bass.ds(i * RING + j, 1), :, :].rearrange("a p n -> (a p) n")
                                 ).then_inc(ring.landed[j], 16)
            k.loaded = first + NKEY
            load_tiles(sp, k, k.loaded + RING)

        @block.scalar
        def _(act):
            def one_round(i):
                for j in range(RING):
                    if type(i) is int:
                        c = k.coef[:, j, :]
                    else:
                        act.wait_ge(used.sem, i * RING + (first + j - RING + 1))
                        c = k.coef[:, bass.ds(i * RING + j, 1), :].rearrange("p a t -> p (a t)")
                    nc.scalar.activation(stage[:, j, :], c, ACT.Copy).then_inc(staged.sem, 1)
            one_round(0)
            with act.Fori(1, rounds) as i:
                one_round(i)

        @block.tensor
        def _(pe):
            def one_round(i, head=False, tail=False):
                for j in range(RING):
                    pe.wait_ge(ring.landed[j], i * 16 + (n0[j] + 16))
                    pe.wait_ge(staged.sem, i * RING + (staged.base + j + 1))
                    for tt in range(NT):
                        for half in range(2):
                            ins = nc.tensor.matmul(ps[:, 2 * tt + half, :], stage[:, j, tt * P:tt * P + P],
                                                   ring.buf[:, j, half * 512:(half + 1) * 512],
                                                   start=head and j == 0, stop=tail and j == RING - 1,
                                                   skip_group_check=True)
                    ins.then_inc(used.sem, 1)
            one_round(0, head=True)
            with pe.Fori(1, rounds - 1) as i:
                one_round(i)
            one_round(rounds - 1, tail=True)

        @block.vector
        def _(dve):
            dve.wait_ge(used.sem, first + NKEY)
            for tt in range(NT):
                h = k.h[:, tt, :]
                nc.vector.tensor_tensor(h, h, ps[:, 2 * tt:2 * tt + 2, :].rearrange("p b n -> p (b n)"),
                                        ALU.add).then_inc(*added.up())
    used.total += NKEY
    staged.total += NKEY


def peer(k, stop):
    k.prefetch = k.tiles["wq"] + RING
    norm_stage(k, [(k.h[:, tt, :], P, tt * P) for tt in range(NT)], k.p("norm_ffn"), k.hT)
    k.qT, = k.carve(k.big, (2 * PH, S))
    project_T(k, "wq", 2 * PH, S, lambda c: k.hT[:, c, 0:S],
              (lambda i: "vector", lambda eng, i, src: k.nc.vector.tensor_copy(k.qT[:, i, :], src)),
              k.tiles["subk"] + RING)
    k.score, = k.carve(k.mid, (NT, 2 * PH, NKEY))
    scores_stage(k)
    if stop <= 6: return
    k.coef, = k.carve(k.big, (NKEY, S))
    (_, k.top, k.at, k.atf, k.pos, k.part, k.partf) = k.carve(
        k.mid, (NT, 2 * PH, NKEY), (2 * PH, TOPK), (2 * PH, TOPK), (2 * PH, TOPK), (PH, TOPK), (PH, TOPK), (PH, TOPK))
    k.at, k.pos, k.part = (ap.bitcast(U32) for ap in (k.at, k.pos, k.part))
    k.best, k.chosen = k.carve(k.kept, (NT, PH, TOPK), (NT, 2, P))
    experts_in_stage(k)
    if stop <= 7: return
    k.chosenT, k.onehot = k.carve(k.mid, (3, S), (2, 2, 4, NKEY))
    choice_stage(k)
    weight_stage(k)
    if stop <= 8: return
    k.stage, = k.carve(k.mid, (RING, S))
    experts_out_stage(k)


def final_norm_stage(k):
    nc = k.nc
    landed_row, summed, vec, rooted = k.start("row_landed", "final_summed", "final_vector", "final_rooted")
    r = k.small[:, 0:12]
    k.wide, k.squares = k.carve(k.mid, (D,), (NT, D))
    with nc.Block() as block:

        @block.sync
        def _(sp):
            sp.dma_start(k.wide, k.dram["norm_final"]).then_inc(*landed_row.up(16))
            sp.dma_start(k.const2, k.dram["const_second"]).then_inc(*landed_row.up(16))
            sp.wait_ge(*landed_row.last())

        @block.scalar
        def _(act):
            for tt in range(NT):
                nc.scalar.activation(k.squares[:, tt, :], k.h[:, tt, :], ACT.Square,
                                     accum_out=r[:, tt:tt + 1]).then_inc(*summed.up())
            act.wait_ge(*vec.at(1))
            nc.scalar.activation(r[:, 4:6], r[:, 2:4], ACT.Sqrt).then_inc(*rooted.up())

        @block.vector
        def _(dve):
            dve.wait_ge(*summed.at(NT))
            nc.vector.tensor_scalar(r[:, 2:4], r[:, 0:2], 1.0 / D, EPS, ALU.mult, ALU.add).then_inc(*vec.up())
            dve.wait_ge(*rooted.at(1))
            newton(nc, dve, vec, r[:, 2:4], r[:, 4:6], r[:, 6:8], r[:, 8:10])
            dve.wait_ge(*landed_row.at(32))
            for tt in range(NT):
                nc.vector.scalar_tensor_tensor(k.h[:, tt, :], k.h[:, tt, :], r[:, 6 + tt:7 + tt], k.wide,
                                               ALU.mult, ALU.mult).then_inc(*vec.up())


def newton(nc, dve, sig, y, root, inv, step):
    nc.vector.reciprocal(inv, root).then_inc(*sig.up())
    dve.wait_ge(*sig.last())
    nc.vector.tensor_tensor(step, inv, inv, ALU.mult).then_inc(*sig.up())
    dve.wait_ge(*sig.last())
    nc.vector.tensor_tensor(step, step, y, ALU.mult).then_inc(*sig.up())
    dve.wait_ge(*sig.last())
    nc.vector.tensor_scalar(step, step, -0.5, 1.5, ALU.mult, ALU.add).then_inc(*sig.up())
    dve.wait_ge(*sig.last())
    nc.vector.tensor_tensor(inv, inv, step, ALU.mult).then_inc(*sig.up())
    dve.wait_ge(*sig.last())


def head_norm_stage(k, chunks, heads, gather, spread, scale, eps, finish):
    nc, ps, xs = k.nc, k.ps, chunks
    n = len(xs)
    squared, summed, vec, rooted, wide, applied = k.start("head_squared", "head_summed", "head_vector",
                                                          "head_rooted", "head_spread", "head_applied")
    sq = k.squares2
    r = k.factors[0:heads]
    with nc.Block() as block:

        @block.sync
        def _(sp):
            load_tiles(sp, k, k.prefetch)

        @block.scalar
        def _(act):
            for c in range(n):
                if c >= 2:
                    act.wait_ge(*summed.at(c - 1))
                nc.scalar.activation(sq[:, c % 2, :], xs[c], ACT.Square).then_inc(*squared.up())
            act.wait_ge(*vec.at(1))
            nc.scalar.activation(r[:, 1, :], r[:, 0, :], ACT.Sqrt).then_inc(*rooted.up())

        @block.tensor
        def _(pe):
            for c in range(n):
                pe.wait_ge(*squared.at(c + 1))
                nc.tensor.matmul(ps[0:heads, 7, 0:L], gather(c), sq[:, c % 2, :], start=c == 0,
                                 stop=c == n - 1).then_inc(*summed.up())
            pe.wait_ge(*vec.at(6))
            for c in range(n):
                if c >= 7:
                    pe.wait_ge(*applied.at(c - 6))
                for lhsT, rows in spread(c):
                    ins = nc.tensor.matmul(ps[rows, c % 7, 0:L], lhsT, r[:, 2, :], start=True, stop=True)
                ins.then_inc(*wide.up())

        @block.vector
        def _(dve):
            dve.wait_ge(*summed.at(n))
            nc.vector.tensor_scalar(r[:, 0, :], ps[0:heads, 7, 0:L], scale, eps, ALU.mult,
                                    ALU.add).then_inc(*vec.up())
            dve.wait_ge(*rooted.at(1))
            newton(nc, dve, vec, r[:, 0, :], r[:, 1, :], r[:, 2, :], r[:, 3, :])
            for c in range(n):
                dve.wait_ge(*wide.at(c + 1))
                ins = list(finish(c, ps[:, c % 7, 0:L]))
                for i in ins:
                    i.then_inc(*(applied if i is ins[-1] else vec).up())


def sink_attention_stage(k):
    nc, ps, T = k.nc, k.ps, k.T2
    AK, GATE = 8, 10
    scored, masked, peaked, exped = k.start("att_scored", "att_masked", "att_peaked", "att_exped")
    scaled, turned, unturned, summed = k.start("att_scaled", "att_turned", "att_copied", "att_valued")
    stored, stats = k.start("att_stored", "att_stats")
    units = [(tt, a) for tt in range(NT) for a in range(AH // 2)]
    keys = lambda tt: META + (tt + 1) * P
    soft, pt = k.soft2, k.pt2
    st = k.small[:, 0:24].rearrange("p (s a h) -> p s a h", s=2, a=6)
    slope = [2.0 ** (-8.0 * (h + 1) / AH) for h in range(AH)]
    sinks = k.p("sinks")

    def key_tiles(tt):
        return [(0, META)] + [(META + i * P, P) for i in range(tt + 1)]

    with nc.Block() as block:

        @block.sync
        def _(sp):
            load_tiles(sp, k, k.tiles["attn_out"] + RING)

        @block.tensor
        def _(pe):
            def scores(u):
                tt, a = units[u]
                if u >= 2:
                    pe.wait_ge(*masked.at(u - 1))
                for j in range(2):
                    h = 2 * a + j
                    rows = slice(HD * j, HD * j + HD)
                    ins = nc.tensor.matmul(ps[:, 2 * (u % 2) + j, 0:keys(tt)],
                                           T[rows, a, META + tt * P:META + tt * P + P],
                                           T[rows, AK + h // 8, 0:keys(tt)], start=True, stop=True)
                ins.then_inc(*scored.up())

            def turn(u):
                tt, _ = units[u]
                pe.wait_ge(*scaled.at(u + 1))
                if u:
                    pe.wait_ge(*unturned.at(u))
                for i, (c0, n) in enumerate(key_tiles(tt)):
                    for j in range(2):
                        ins = nc.tensor.transpose(ps[0:n, 4 + i // 2, (2 * (i % 2) + j) * P:(2 * (i % 2) + j) * P + P],
                                                  soft[:, u % 2, j, c0:c0 + n], k.ident)
                ins.then_inc(*turned.up())

            def values(u):
                tt, a = units[u]
                pe.wait_ge(*unturned.at(u + 1))
                if u >= 2:
                    pe.wait_ge(*stored.at(u - 1))
                tiles = key_tiles(tt)
                for j in range(2):
                    g = (2 * a + j) // 8
                    for i, (_, n) in enumerate(tiles):
                        ins = nc.tensor.matmul(ps[HD * j:HD * j + HD, 6 + u % 2, 0:P], k.v2[0:n, i, g * HD:(g + 1) * HD],
                                               pt[0:n, u % 2, i, j, :], start=i == 0, stop=i == len(tiles) - 1)
                ins.then_inc(*summed.up())

            scores(0)
            for u in range(len(units) + 1):
                if u + 1 < len(units):
                    scores(u + 1)
                if u < len(units):
                    turn(u)
                if u:
                    values(u - 1)

        @block.vector
        def _(dve):
            def peaks(u):
                tt, a = units[u]
                s, n = u % 2, keys(tt)
                dve.wait_ge(*scored.at(u + 1))
                if u >= 2:
                    dve.wait_ge(*turned.at(u - 1))
                dist = k.c("dist")[:, L * tt:L * tt + n]
                for j in range(2):
                    nc.vector.scalar_tensor_tensor(soft[:, s, j, 0:n], dist, -slope[2 * a + j],
                                                   ps[:, 2 * s + j, 0:n], ALU.mult,
                                                   ALU.add).then_inc(*(masked if j else stats).up())
                dve.wait_ge(*masked.last())
                dve.wait_ge(*stats.last())
                nc.vector.tensor_reduce(st[:, s, 0, :], soft[:, s, :, 0:n], AX.X, ALU.max).then_inc(*stats.up())
                dve.wait_ge(*stats.last())
                nc.vector.tensor_tensor(st[:, s, 0, :], st[:, s, 0, :], sinks[:, 2 * a:2 * a + 2],
                                        ALU.max).then_inc(*stats.up())
                dve.wait_ge(*stats.last())
                nc.vector.tensor_tensor(st[:, s, 3, :], sinks[:, 2 * a:2 * a + 2], st[:, s, 0, :],
                                        ALU.subtract).then_inc(*stats.up())
                dve.wait_ge(*stats.last())
                nc.vector.tensor_scalar(st[:, s, 1, :], st[:, s, 0, :], -1.0, None, ALU.mult).then_inc(*peaked.up())

            def scale(u):
                tt, a = units[u]
                s, n = u % 2, keys(tt)
                dve.wait_ge(*exped.at(3 * (u + 1)))
                nc.vector.tensor_tensor(st[:, s, 2, :], st[:, s, 2, :], st[:, s, 3, :], ALU.add).then_inc(*stats.up())
                dve.wait_ge(*stats.last())
                nc.vector.reciprocal(st[:, s, 4, :], st[:, s, 2, :]).then_inc(*stats.up())
                dve.wait_ge(*stats.last())
                for j in range(2):
                    nc.vector.tensor_scalar(soft[:, s, j, 0:n], soft[:, s, j, 0:n], st[:, s, 4, j:j + 1], None,
                                            ALU.mult).then_inc(*(scaled if j else stats).up())

            def store(u):
                tt, a = units[u]
                dve.wait_ge(*summed.at(u + 1))
                cols = slice(META + tt * P, META + tt * P + P)
                nc.vector.tensor_tensor(k.y2[:, a, cols], ps[:, 6 + u % 2, 0:P], T[:, GATE + a, cols],
                                        ALU.mult).then_inc(*stored.up())

            for u in range(len(units) + 2):
                if u < len(units):
                    peaks(u)
                if 1 <= u <= len(units):
                    scale(u - 1)
                if u >= 2:
                    store(u - 2)

        @block.scalar
        def _(act):
            def exps(u):
                tt, _ = units[u]
                s = u % 2
                act.wait_ge(*peaked.at(u + 1))
                nc.scalar.activation(st[:, s, 3, :], st[:, s, 3, :], ACT.Exp).then_inc(*exped.up())
                for j in range(2):
                    p = soft[:, s, j, 0:keys(tt)]
                    nc.scalar.activation(p, p, ACT.Exp, bias=st[:, s, 1, j:j + 1],
                                         accum_out=st[:, s, 2, j:j + 1]).then_inc(*exped.up())

            def copy_turned(u):
                tt, _ = units[u]
                act.wait_ge(*turned.at(u + 1))
                if u >= 2:
                    act.wait_ge(*summed.at(u - 1))
                nc.scalar.activation(pt[0:META, u % 2, 0, :, :].rearrange("p j n -> p (j n)"), ps[0:META, 4, 0:2 * P],
                                     ACT.Copy).then_inc(*stats2.up())
                act.wait_ge(*stats2.last())
                nc.scalar.activation(pt[:, u % 2, 1:2 + tt, :, :].rearrange("p i j n -> p (i j n)"),
                                     k.flat[:, 4 * 512 + 2 * P:4 * 512 + (4 + 2 * tt) * P],
                                     ACT.Copy).then_inc(*unturned.up())

            stats2, = k.start("att_meta_copied")
            for u in range(len(units) + 1):
                if u < len(units):
                    exps(u)
                if u:
                    copy_turned(u - 1)


def meta_attention_stage(k):
    nc, ps, T = k.nc, k.ps, k.T2
    AK, GATE = 8, 10
    pe_done, vec, exped = k.start("meta_product", "meta_vector", "meta_exped")
    m = META
    k.meta_soft, k.meta_turned = k.carve(k.mid, (AH, META), (AH, META))
    soft, turned = k.meta_soft[0:m], k.meta_turned[0:m]
    st = k.small[0:m, 24:24 + 4 * AH].rearrange("p (a h) -> p a h", a=4)
    wide = lambda ap: ap.unsqueeze(2).broadcast_to([m, AH, m])
    with nc.Block() as block:

        @block.tensor
        def _(pe):
            for h in range(AH):
                rows = slice(HD * (h % 2), HD * (h % 2) + HD)
                ins = nc.tensor.matmul(ps[0:m, h % 2, (h // 2) * m:(h // 2) * m + m], T[rows, h // 2, 0:m],
                                       T[rows, AK + h // 8, 0:m], start=True, stop=True)
            ins.then_inc(*pe_done.up())
            pe.wait_ge(*vec.at(10))
            for h in range(AH):
                ins = nc.tensor.transpose(ps[0:m, 2, h * m:(h + 1) * m], soft[:, h, :], k.ident[0:m, 0:m])
            ins.then_inc(*pe_done.up())
            pe.wait_ge(*vec.at(11))
            for i in range(AH):
                h = 2 * (i % 8) + i // 8
                g = h // 8
                ins = nc.tensor.matmul(ps[HD * (h % 2):HD * (h % 2) + HD, 3, (h // 2) * m:(h // 2) * m + m],
                                       k.v2[0:m, 0, g * HD:(g + 1) * HD], turned[:, i, :], start=True, stop=True)
            ins.then_inc(*pe_done.up())

        @block.vector
        def _(dve):
            def done(ins):
                ins.then_inc(*vec.up())
                dve.wait_ge(*vec.last())
            sinks = k.p("sinks_placed")[0:m, :]
            dve.wait_ge(*pe_done.at(1))
            for o in range(2):
                done(nc.vector.tensor_tensor(soft[:, 8 * o:8 * o + 8, :], ps[0:m, o, 0:8 * m].rearrange("p (h n) -> p h n", h=8),
                                             k.c("meta_bias")[0:m, 8 * m * o:8 * m * (o + 1)].rearrange("p (h n) -> p h n", h=8),
                                             ALU.add))
            done(nc.vector.tensor_reduce(st[:, 0, :], soft, AX.X, ALU.max))
            done(nc.vector.tensor_tensor(st[:, 0, :], st[:, 0, :], sinks, ALU.max))
            done(nc.vector.tensor_tensor(st[:, 1, :], sinks, st[:, 0, :], ALU.subtract))
            done(nc.vector.tensor_tensor(soft, soft, wide(st[:, 0, :]), ALU.subtract))
            dve.wait_ge(*exped.at(2))
            done(nc.vector.tensor_reduce(st[:, 2, :], soft, AX.X, ALU.add))
            done(nc.vector.tensor_tensor(st[:, 2, :], st[:, 2, :], st[:, 1, :], ALU.add))
            done(nc.vector.reciprocal(st[:, 3, :], st[:, 2, :]))
            done(nc.vector.tensor_tensor(soft, soft, wide(st[:, 3, :]), ALU.mult))
            dve.wait_ge(*pe_done.at(2))
            done(nc.vector.tensor_copy(turned.rearrange("p h n -> p (h n)"), ps[0:m, 2, 0:AH * m]))
            dve.wait_ge(*pe_done.at(3))
            done(nc.vector.tensor_tensor(k.y2[:, :, 0:m], ps[:, 3, 0:8 * m].rearrange("p (c n) -> p c n", c=8),
                                         T[:, GATE:GATE + 8, 0:m], ALU.mult))

        @block.scalar
        def _(act):
            act.wait_ge(*vec.at(6))
            nc.scalar.activation(st[:, 1, :], st[:, 1, :], ACT.Exp).then_inc(*exped.up())
            nc.scalar.activation(soft, soft, ACT.Exp).then_inc(*exped.up())


def second_block(k, stop):
    nc, ps = k.nc, k.ps
    n_const = sum(n for _, n in k.const_cols["second"][0])
    (k.const2, k.T2, k.v2, k.squares2, k.factors, k.soft2, k.pt2, k.y2) = k.carve(
        k.big, (n_const,), (18, L), (3, P), (2, L), (4, L), (2, 2, L), (2, 3, 2, P), (KC, L))
    k.bind("second", k.const2)
    k.flat = ps[:, :, :].rearrange("p b n -> p (b n)")
    final_norm_stage(k)
    if stop <= 21: return
    tiles = [(k.hm[0:META, :], META, 0)] + [(k.h[:, tt, :], P, META + tt * P) for tt in range(NT)]
    k.prefetch = k.tiles["attn_t"] + RING
    norm_stage(k, tiles, k.p("attn_norm"), k.hT)
    rhs = lambda c: k.hT[:, c, :]

    def put(eng, i, src):
        if i < 10:
            return nc.vector.tensor_copy(k.T2[:, i, :], src)
        return nc.scalar.activation(k.T2[:, i, :], src, ACT.Silu)
    project_T(k, "attn_t", 18, L, rhs, (lambda i: "vector" if i < 10 else "scalar", put), k.tiles["attn_v"] + RING)
    spans = [(0, META)] + [(META + tt * P, P) for tt in range(NT)]
    def keep_v():
        for i, (_, n) in enumerate(spans):
            yield nc.vector.tensor_copy(k.v2[0:n, i, :], ps[0:n, i, 0:P])
    project_N(k, "attn_v", lambda c, i: k.hT[:, c, spans[i][0]:spans[i][0] + spans[i][1]],
              [(1, 8, P, [(ps[0:n, i, 0:P], i) for i, (_, n) in enumerate(spans)], keep_v)],
              k.tiles["attn_out"] + RING)
    if stop <= 22: return

    def apply_qk(c, wide):
        w = k.p("q_norm") if c < 8 else k.p("k_norm")
        yield nc.vector.scalar_tensor_tensor(k.T2[:, c, :], wide, w, k.T2[:, c, :], ALU.mult, ALU.mult)
    two = slice(0, HD), slice(HD, P)
    head_norm_stage(k, [k.T2[:, c, :] for c in range(10)], 20,
                    lambda c: k.c("pair")[:, 18 - 2 * c:38 - 2 * c],
                    lambda c: [(k.ident[0:20, 2 * c + o:2 * c + o + 1].broadcast_to([20, HD]), two[o]) for o in range(2)],
                    8.0 / HD, 8.0 * EPS, apply_qk)
    if stop <= 23: return
    meta_attention_stage(k)
    sink_attention_stage(k)
    if stop <= 24: return
    out_rows(k, "attn_out", [(k.hm, 0, META, 0)] + [(k.h[:, tt, :], 2 + 2 * tt, P, META + tt * P) for tt in range(NT)],
             KC, lambda c, c0, rows: k.y2[:, c, c0:c0 + rows], k.tiles.get("dn_qkv", k.tiles["end"]) + RING)
    if stop <= 25: return
    deltanet(k, tiles, stop)


def conv_stage(k):
    nc, ps = k.nc, k.ps
    first = k.tiles["dn_qkv"]
    n = 2 * DNK + DNV
    conv, chain, silu, cleared = k.start("conv_done", "conv_chain", "conv_silu", "pads_cleared")
    silu2, = k.start("conv_silu_meta")
    taps = k.p("conv").rearrange("p (c s) -> p c s", s=4)
    acc = k.squares2
    with nc.Block() as block:

        @block.sync
        def _(sp):
            load_tiles(sp, k, k.tiles["dn_ba"] + RING)

        @block.gpsimd
        def _(pool):
            for ap in (k.vT[:, :, 0, :, 0:PAD], k.kT[:, :, 0, :, 0:PAD], k.dq[:, :, 0, 0:PAD], k.state):
                nc.gpsimd.memset(ap, 0.0).then_inc(*cleared.up())
            pool.wait_ge(*cleared.last())

        @block.tensor
        def _(pe):
            for i in range(n):
                t = k.ring.view(first + i).rearrange("p (c m) -> p c m", c=KC)
                landed(pe, k, first + i)
                if i >= 8:
                    pe.wait_ge(*conv.at(i - 7))
                for c in range(KC):
                    ins = nc.tensor.matmul(ps[:, i % 8, 0:L], t[:, c, :], k.hT[:, c, :], start=c == 0, stop=c == KC - 1)
                tile_used(ins, k, first + i)

        @block.vector
        def _(dve):
            for i in range(n):
                dve.wait_ge(k.ring.used.sem, first + i + 1)
                if i >= 2:
                    dve.wait_ge(*silu.at(i - 1))
                x, y = ps[:, i % 8, 0:L], acc[:, i % 2, :]
                nc.vector.tensor_scalar(y, x, taps[:, i, 3:4], None, ALU.mult).then_inc(*chain.up())
                for s in range(1, 4):
                    dve.wait_ge(*chain.last())
                    nc.vector.scalar_tensor_tensor(y[:, s:L], x[:, 0:L - s], taps[:, i, 3 - s:4 - s], y[:, s:L],
                                                   ALU.mult, ALU.add).then_inc(*(conv if s == 3 else chain).up())

        @block.scalar
        def _(act):
            for i in range(n):
                act.wait_ge(*conv.at(i + 1))
                y = acc[:, i % 2, :]
                if i < 2 * DNK:
                    nc.scalar.activation(k.qk[:, i, :], y, ACT.Silu).then_inc(*silu.up())
                else:
                    h = i - 2 * DNK
                    v = k.vT[:, h // 2, :, h % 2, :]
                    nc.scalar.activation(v[:, 0, PAD:CH], y[:, 0:META], ACT.Silu).then_inc(*silu2.up())
                    nc.scalar.activation(v[:, 1:NCH, :], y[:, META:L].rearrange("p (c s) -> p c s", c=NCH - 1),
                                         ACT.Silu).then_inc(*silu.up())


def delta_gates_stage(k):
    nc, ps = k.nc, k.ps
    vec, acted, made, clear = k.start("gate_vector", "gate_act", "gate_product", "gate_cleared")
    b, a = slice(0, 16), slice(32, 48)
    sp, ba = k.soft_plus, k.ba
    dup = k.dup
    n = NCH * DNK
    col = lambda ap: ap.rearrange("p (c i) -> p c i", c=NCH)
    with nc.Block() as block:

        @block.sync
        def _(sync):
            load_tiles(sync, k, k.prefetch)

        @block.gpsimd
        def _(pool):
            nc.gpsimd.memset(dup[0:48], 0.0).then_inc(*clear.up())

        @block.scalar
        def _(act):
            nc.scalar.activation(ba[b, :], ba[b, :], ACT.Sigmoid).then_inc(*acted.up())
            nc.scalar.activation(k.small[a, 0:1], k.p("a_log")[a, :], ACT.Exp).then_inc(*acted.up())
            act.wait_ge(*vec.at(2))
            nc.scalar.activation(sp[a, 1, :], sp[a, 1, :], ACT.Exp).then_inc(*acted.up())
            act.wait_ge(*acted.last())
            nc.scalar.activation(sp[a, 1, :], sp[a, 1, :], ACT.Ln, bias=1.0).then_inc(*acted.up())
            act.wait_ge(*vec.at(14))
            nc.scalar.activation(k.eG, k.G, ACT.Exp).then_inc(*acted.up())
            nc.scalar.activation(k.eGL, k.eGL, ACT.Exp).then_inc(*acted.up())
            nc.scalar.activation(k.egl, ps[:, 2, 0:2 * n], ACT.Exp).then_inc(*acted.up())

        @block.vector
        def _(dve):
            def done(ins):
                ins.then_inc(*vec.up())
                dve.wait_ge(*vec.last())
            done(nc.vector.tensor_scalar(sp[a, 0, :], ba[a, :], k.p("dt_bias")[a, :], None, ALU.add))
            done(nc.vector.scalar_tensor_tensor(sp[a, 1, :], sp[a, 0, :], -1.0, sp[a, 0, :], ALU.mult, ALU.min))
            dve.wait_ge(*acted.at(4))
            done(nc.vector.scalar_tensor_tensor(sp[a, 0, :], sp[a, 0, :], 0.0, sp[a, 1, :], ALU.max, ALU.add))
            done(nc.vector.tensor_scalar(ba[a, :], sp[a, 0, :], k.small[a, 0:1], -1.0, ALU.mult, ALU.mult))
            dve.wait_ge(*clear.at(1))
            done(nc.vector.tensor_copy(dup[0:48, 0, :, PAD:CH], ba[0:48, 0:META].unsqueeze(1).broadcast_to([48, 2, META])))
            done(nc.vector.tensor_copy(dup[0:48, 1:NCH], ba[0:48, META:L].rearrange("p (c s) -> p c s", c=NCH - 1)
                                       .unsqueeze(2).broadcast_to([48, NCH - 1, 2, CH])))
            dve.wait_ge(*made.at(1))
            turned = ps[:, 0, 0:48 * NCH].rearrange("p (c r) -> p c r", c=NCH)
            for j, (dst, c0) in enumerate(((k.beta, 0), (k.g, 32))):
                for o in range(2):
                    rows = slice(CH * o, CH * o + CH)
                    done(nc.vector.tensor_copy(col(dst)[rows], turned[rows, :, c0 + 8 * o:c0 + 8 * o + 8]))
            for o in range(2):
                done(nc.vector.tensor_scalar(k.gm[:, n * o:n * (o + 1)], k.g, k.c("half")[:, o:o + 1], None, ALU.mult))
            dve.wait_ge(*made.at(2))
            done(nc.vector.tensor_copy(k.G, ps[:, 1, 0:n]))
            done(nc.vector.tensor_tensor(k.eGL, ps[:, 1, n:2 * n], k.G, ALU.subtract))
            done(nc.vector.tensor_scalar(k.negG, k.G, -1.0, None, ALU.mult))
            dve.wait_ge(*acted.at(7))
            done(nc.vector.tensor_tensor(k.be, k.beta, k.eG, ALU.mult))

        @block.tensor
        def _(pe):
            pe.wait_ge(*vec.at(6))
            pe.wait_ge(*acted.at(1))
            for c in range(NCH):
                ins = nc.tensor.transpose(ps[:, 0, 48 * c:48 * c + 48], dup[0:48, c].rearrange("p o s -> p (o s)"),
                                          k.ident[0:48, 0:48])
            ins.then_inc(*made.up())
            pe.wait_ge(*vec.at(12))
            nc.tensor.matmul(ps[:, 1, 0:n], k.c("upper"), k.g, start=True, stop=True)
            nc.tensor.matmul(ps[:, 1, n:2 * n], k.c("block"), k.g, start=True, stop=True)
            nc.tensor.matmul(ps[:, 2, 0:2 * n], k.c("ones"), k.gm, start=True, stop=True).then_inc(*made.up())


LEVELS = 5


def delta_stage(k):
    nc, ps = k.nc, k.ps
    gr, kk, kq, kr, vr, mt = k.start("d_sums", "d_kk", "d_kq", "d_krows", "d_vrows", "d_turned")
    power, grown, us, ws = k.start("d_power", "d_product", "d_u", "d_w")
    masked, m_done, attn, krows, vrows = k.start("d_masked", "d_m", "d_attn", "d_kscaled", "d_vscaled")
    rinit, ptaken, rtaken, decay, mtaken = k.start("d_rinit", "d_ptaken", "d_rtaken", "d_decay", "d_mtaken")
    p2taken, utaken, wtaken = k.start("d_p2taken", "d_utaken", "d_wtaken")
    old, inter, intra, grow_s, oturn = k.start("d_old", "d_inter", "d_intra", "d_state", "d_oturned")
    vnew, oscaled, summed, state, squared = k.start("d_vnew", "d_oscaled", "d_osum", "d_state_new", "d_squared")
    rooted, normed, stored, chain, mean = k.start("d_rooted", "d_normed", "d_stored", "d_chain", "d_mean")
    H = 4
    half = lambda ap, b: ap[:, H * b:H * b + H, :]
    flat = lambda ap: ap.rearrange("p i n -> p (i n)")
    bank = lambda b, n=1: k.flat[:, 512 * b:512 * (b + n)]
    quad = lambda b: ps[:, b, :].rearrange("p (i n) -> p i n", i=H)
    wide = lambda ap: ap.unsqueeze(2).broadcast_to([P, H, P])
    kT = lambda c, i: k.kT[:, i, c].rearrange("p o s -> p (o s)")
    vT = lambda c, i: k.vT[:, i, c].rearrange("p o s -> p (o s)")
    at = lambda c, i: DNK * c + i
    low, up_ = k.c("low"), k.c("up")
    lvl = lambda c, l, b: 2 * LEVELS * c + 2 * (l - 1) + b + 1
    lvl4 = lambda c, l, b: 2 * (LEVELS - 1) * c + 2 * (l - 1) + b + 1
    with nc.Block() as block:

        @block.sync
        def _(sp):
            load_tiles(sp, k, k.prefetch)

        @block.tensor
        def _(pe):
            for c in range(NCH):
                if c:
                    pe.wait_ge(*state.at(16 * c))
                    pe.wait_ge(*summed.at(c))
                    pe.wait_ge(*stored.at(2 * (c - 1)) if c > 1 else summed.at(c))
                for b in range(2):
                    n = 2 * c + b
                    if b:
                        pe.wait_ge(*masked.at(n))
                    for i in range(H):
                        g = k.g[:, at(c, H * b + i):at(c, H * b + i) + 1].broadcast_to([P, P])
                        ins = nc.tensor.matmul(quad(0)[:, i, :], g, k.c("upper"), start=True, stop=True)
                    ins.then_inc(*gr.up())
                    if b:
                        pe.wait_ge(*krows.at(n))
                    for i in range(H):
                        ins = nc.tensor.transpose(quad(3)[:, i, :], kT(c, H * b + i), k.ident)
                    ins.then_inc(*kr.up())
                    if b:
                        pe.wait_ge(*vrows.at(n))
                    for i in range(H):
                        ins = nc.tensor.transpose(quad(4)[:, i, :], vT(c, H * b + i), k.ident)
                    ins.then_inc(*vr.up())
                    if b:
                        pe.wait_ge(*m_done.at(n))
                    for i in range(H):
                        ins = nc.tensor.matmul(quad(1)[:, i, :], kT(c, H * b + i), kT(c, H * b + i), start=True, stop=True)
                    ins.then_inc(*kk.up())
                    if b:
                        pe.wait_ge(*attn.at(n))
                    for i in range(H):
                        q = k.dq[:, H * b + i, c, :].unsqueeze(1).broadcast_to([P, 2, CH])
                        ins = nc.tensor.matmul(quad(2)[:, i, :].rearrange("p (o s) -> p o s", o=2), kT(c, H * b + i), q,
                                               start=True, stop=True)
                    ins.then_inc(*kq.up())
                for b in range(2):
                    n = 2 * c + b
                    pe.wait_ge(*m_done.at(n + 1))
                    for i in range(H):
                        ins = nc.tensor.transpose(quad(6 + b)[:, i, :], half(k.pw, b)[:, i, :], k.ident)
                    ins.then_inc(*mt.up())
                pe.wait_ge(*attn.at(2 * c + 2))
                pe.wait_ge(*krows.at(2 * c + 2))
                pe.wait_ge(*vrows.at(2 * c + 2))
                for l in range(1, LEVELS + 1):
                    for b in range(2):
                        n = 2 * c + b
                        if l == 1:
                            pe.wait_ge(*mtaken.at(n + 1))
                        else:
                            pe.wait_ge(*ptaken.at(lvl(c, l - 1, b)))
                            pe.wait_ge(*p2taken.at(lvl4(c, l - 1, b)))
                        for i in range(H):
                            m, t = half(k.pw, b)[:, i, :], half(k.pwT, b)[:, i, :]
                            ins = nc.tensor.matmul(quad(b)[:, i, :], t, m, start=True, stop=True)
                            if l < LEVELS:
                                ins = nc.tensor.matmul(quad(2 + b)[:, i, :], m, t, start=True, stop=True)
                        ins.then_inc(*power.up())
                    for b in range(2):
                        pe.wait_ge(*ptaken.at(lvl(c, l, b)))
                        pe.wait_ge(*rinit.at(2 * c + b + 1))
                        if l > 1:
                            pe.wait_ge(*rtaken.at(lvl(c, l - 1, b)))
                        for i in range(H):
                            ins = nc.tensor.matmul(quad(4 + b)[:, i, :], half(k.pw, b)[:, i, :], half(k.R, b)[:, i, :],
                                                   start=True, stop=True)
                        ins.then_inc(*grown.up())
                for b in range(2):
                    pe.wait_ge(*rtaken.at(lvl(c, LEVELS, b)))
                    for i in range(H):
                        ins = nc.tensor.matmul(quad(b)[:, i, :], half(k.R, b)[:, i, :], half(k.vb, b)[:, i, :], start=True, stop=True)
                    ins.then_inc(*us.up())
                    for i in range(H):
                        ins = nc.tensor.matmul(quad(2 + b)[:, i, :], half(k.kbg, b)[:, i, :], half(k.R, b)[:, i, :], start=True, stop=True)
                    ins.then_inc(*ws.up())
                if c:
                    pe.wait_ge(*wtaken.at(2 * c + 2))
                    for dst, lhs, sig in ((4, lambda i, o: k.wT[:, i, CH * o:CH * o + CH], old),
                                          (6, lambda i, o: k.dq[:, i, c, :], inter)):
                        for i in range(DNK):
                            for o in range(2):
                                ins = nc.tensor.matmul(ps[CH * o:CH * o + CH, dst + i // H, (i % H) * P:(i % H) * P + P],
                                                       lhs(i, o), k.state[:, 2 * i + o, :], start=True, stop=True)
                        ins.then_inc(*sig.up())
                pe.wait_ge(*vnew.at(c + 1))
                pe.wait_ge(*wtaken.at(2 * c + 2))
                for i in range(DNK):
                    ins = nc.tensor.matmul(ps[:, i // H, (i % H) * P:(i % H) * P + P], k.attnT[:, i, :], k.vn[:, i, :],
                                           start=True, stop=True)
                ins.then_inc(*intra.up())
                for i in range(DNK):
                    for o in range(2):
                        rows = slice(CH * o, CH * o + CH)
                        ins = nc.tensor.matmul(ps[:, 2 + 2 * o + i // H, (i % H) * P:(i % H) * P + P],
                                               k.kst[rows, i, :], k.vn[rows, i, :], start=True, stop=True)
                ins.then_inc(*grow_s.up())
                if c:
                    pe.wait_ge(*normed.at(c))
                    for i in range(DNK):
                        ins = nc.tensor.transpose(ps[:, 6 + i // H, (i % H) * P:(i % H) * P + P], k.o1[:, i, :], k.ident)
                    ins.then_inc(*oturn.up())

        @block.vector
        def _(dve):
            for c in range(NCH):
                def mask(b):
                    n = 2 * c + b
                    dve.wait_ge(*gr.at(n + 1))
                    nc.vector.tensor_tensor(half(k.E, b), quad(0), low.unsqueeze(1).broadcast_to([P, H, P]),
                                            ALU.subtract).then_inc(*chain.up())
                    nc.vector.tensor_tensor(half(k.ET, b), quad(0), up_.unsqueeze(1).broadcast_to([P, H, P]),
                                            ALU.add).then_inc(*masked.up())

                def rows(b):
                    n = 2 * c + b
                    cols = lambda ap: wide(ap[:, at(c, H * b):at(c, H * b) + H])
                    dve.wait_ge(*kr.at(n + 1))
                    nc.vector.tensor_tensor(half(k.kbg, b), quad(3), cols(k.be), ALU.mult).then_inc(*chain.up())
                    nc.vector.tensor_tensor(half(k.kst, b), quad(3), cols(k.eGL), ALU.mult).then_inc(*krows.up())
                    dve.wait_ge(*vr.at(n + 1))
                    nc.vector.tensor_tensor(half(k.vb, b), quad(4), cols(k.beta), ALU.mult).then_inc(*vrows.up())

                def products(b):
                    n = 2 * c + b
                    dve.wait_ge(*decay.at(8 * (n + 1)))
                    dve.wait_ge(*kk.at(n + 1))
                    for i in range(H):
                        j = at(c, H * b + i)
                        nc.vector.scalar_tensor_tensor(half(k.pw, b)[:, i, :], quad(1)[:, i, :], k.beta[:, j:j + 1],
                                                       half(k.E, b)[:, i, :], ALU.mult,
                                                       ALU.mult).then_inc(*(m_done if i == H - 1 else chain).up())
                    dve.wait_ge(*kq.at(n + 1))
                    nc.vector.tensor_tensor(half(k.attnT, b), quad(2), half(k.ET, b), ALU.mult).then_inc(*attn.up())
                    dve.wait_ge(*chain.last())

                if c:
                    dve.wait_ge(*grow_s.at(c))
                mask(0)
                rows(0)
                mask(1)
                rows(1)
                products(0)
                products(1)
                for b in range(2):
                    dve.wait_ge(*mtaken.at(2 * c + b + 1))
                    nc.vector.scalar_tensor_tensor(half(k.R, b), half(k.pwT, b), -1.0, k.ident.unsqueeze(1).broadcast_to([P, H, P]),
                                                   ALU.mult, ALU.add).then_inc(*rinit.up())
                for l in range(1, LEVELS + 1):
                    for b in range(2):
                        if l < LEVELS:
                            dve.wait_ge(*power.at(lvl(c, l, b)))
                            dve.wait_ge(*rinit.at(2 * c + b + 1))
                            nc.vector.tensor_copy(flat(half(k.pwT, b)), bank(2 + b)).then_inc(*p2taken.up())
                    for b in range(2):
                        dve.wait_ge(*grown.at(lvl(c, l, b)))
                        if l == 1:
                            dve.wait_ge(*rinit.at(2 * c + b + 1))
                        else:
                            dve.wait_ge(*rtaken.at(lvl(c, l - 1, b)))
                        nc.vector.tensor_tensor(half(k.R, b), half(k.R, b), quad(4 + b), ALU.add).then_inc(*rtaken.up())
                dve.wait_ge(*utaken.at(2 * c + 2))
                if c:
                    dve.wait_ge(*old.at(c))
                    nc.vector.tensor_tensor(flat(k.vn), flat(k.u), bank(4, 2), ALU.subtract).then_inc(*vnew.up())
                else:
                    nc.vector.tensor_copy(flat(k.vn), flat(k.u)).then_inc(*vnew.up())
                dve.wait_ge(*intra.at(c + 1))
                if c:
                    dve.wait_ge(*oscaled.at(8 * c))
                    nc.vector.tensor_tensor(flat(k.o1), flat(k.o1), bank(0, 2), ALU.add).then_inc(*summed.up())
                else:
                    nc.vector.tensor_copy(k.small[:, 0:1], bank(0, 2)[:, 0:1]).then_inc(*summed.up())
                dve.wait_ge(*grow_s.at(c + 1))
                for i in range(DNK):
                    for o in range(2):
                        j = NCH * DNK * o + at(c, i)
                        nc.vector.scalar_tensor_tensor(k.state[:, 2 * i + o, :], k.state[:, 2 * i + o, :], k.egl[:, j:j + 1],
                                                       ps[:, 2 + 2 * o + i // H, (i % H) * P:(i % H) * P + P],
                                                       ALU.mult, ALU.add).then_inc(*state.up())
                if c:
                    st = k.small[:, 8:48].rearrange("p (a i) -> p a i", a=5)
                    dve.wait_ge(*squared.at(8 * c))
                    nc.vector.tensor_scalar(st[:, 1, :], st[:, 0, :], 1.0 / P, EPS, ALU.mult, ALU.add).then_inc(*mean.up())
                    dve.wait_ge(*rooted.at(c))
                    newton(nc, dve, chain, st[:, 1, :], st[:, 2, :], st[:, 3, :], st[:, 4, :])
                    nc.vector.tensor_tensor(k.o1, k.o1, st[:, 3, :].unsqueeze(2).broadcast_to([P, DNK, P]),
                                            ALU.mult).then_inc(*normed.up())
                    dve.wait_ge(*oturn.at(c))
                    for b in range(2):
                        cols = slice(META + CH * (c - 1), META + CH * c)
                        heads = slice(2 * H * b, 2 * H * (b + 1))
                        nc.vector.scalar_tensor_tensor(k.dy[:, heads, CH * (c - 1):CH * c],
                                                       bank(6 + b).rearrange("p (h s) -> p h s", s=CH), k.p("o_norm"),
                                                       k.z[:, heads, cols], ALU.mult, ALU.mult).then_inc(*stored.up())

        @block.scalar
        def _(act):
            for c in range(NCH):
                for b in range(2):
                    act.wait_ge(*masked.at(2 * c + b + 1))
                    for i in range(H):
                        j = at(c, H * b + i)
                        e, t = half(k.E, b)[:, i, :], half(k.ET, b)[:, i, :]
                        nc.scalar.activation(e, e, ACT.Exp, bias=k.G[:, j:j + 1], scale=-1.0).then_inc(*decay.up())
                        nc.scalar.activation(t, t, ACT.Exp, bias=k.negG[:, j:j + 1]).then_inc(*decay.up())
                for b in range(2):
                    act.wait_ge(*mt.at(2 * c + b + 1))
                    nc.scalar.activation(flat(half(k.pwT, b)), bank(6 + b), ACT.Copy).then_inc(*mtaken.up())
                for l in range(1, LEVELS + 1):
                    for b in range(2):
                        act.wait_ge(*power.at(lvl(c, l, b)))
                        nc.scalar.activation(flat(half(k.pw, b)), bank(b), ACT.Copy).then_inc(*ptaken.up())
                for b in range(2):
                    act.wait_ge(*us.at(2 * c + b + 1))
                    nc.scalar.activation(flat(half(k.u, b)), bank(b), ACT.Copy).then_inc(*utaken.up())
                    act.wait_ge(*ws.at(2 * c + b + 1))
                    nc.scalar.activation(flat(half(k.wT, b)), bank(2 + b), ACT.Copy).then_inc(*wtaken.up())
                if c:
                    act.wait_ge(*inter.at(c))
                    if c > 1:
                        act.wait_ge(*oturn.at(c - 1))
                    for i in range(DNK):
                        nc.scalar.activation(k.o1[:, i, :], ps[:, 6 + i // H, (i % H) * P:(i % H) * P + P], ACT.Copy,
                                             scale=k.eG[:, at(c, i):at(c, i) + 1]).then_inc(*oscaled.up())
                    act.wait_ge(*summed.at(c + 1))
                    st = k.small[:, 8:48].rearrange("p (a i) -> p a i", a=5)
                    for i in range(DNK):
                        nc.scalar.activation(k.E[:, i, :], k.o1[:, i, :], ACT.Square,
                                             accum_out=st[:, 0, i:i + 1]).then_inc(*squared.up())
                    act.wait_ge(*mean.at(c))
                    nc.scalar.activation(st[:, 2, :], st[:, 1, :], ACT.Sqrt).then_inc(*rooted.up())


def deltanet(k, tiles, stop):
    nc = k.nc
    k.prefetch = k.tiles["dn_qkv"] + RING
    norm_stage(k, tiles, k.p("dn_norm"), k.hT)
    n_const = sum(n for _, n in k.const_cols["second"][0])
    shapes = [(n_const,), (2 * DNK, L), (DNK, NCH, 2, CH), (DNK, NCH, 2, CH), (DNK, NCH, CH), (DNV, L), (DNV, S),
              (DNV, P)]
    k.const2, k.qk, k.vT, k.kT, k.dq, k.z, k.dy, k.state = k.carve(k.big, *shapes)
    k.squares2, = k.carve(k.mid, (2, L))
    conv_stage(k)
    if stop <= 26: return
    k.ba, k.soft_plus, k.dup = k.carve(k.mid, (L,), (2, L), (NCH, 2, CH))

    def put(eng, i, src):
        if i == 0:
            return nc.vector.tensor_copy(k.ba, src)
        return nc.scalar.activation(k.z[:, i - 1, :], src, ACT.Silu)
    project_T(k, "dn_ba", 1 + DNV, L, lambda c: k.hT[:, c, :],
              (lambda i: "scalar" if i else "vector", put), k.tiles["dn_out"] + RING)
    n = NCH * DNK
    (k.beta, k.g, k.G, k.negG, k.eG, k.eGL, k.be, k.gm, k.egl) = k.carve(
        k.kept, (n,), (n,), (n,), (n,), (n,), (n,), (n,), (2 * n,), (2 * n,))
    k.prefetch = k.tiles["dn_out"] + RING
    delta_gates_stage(k)
    k.squares2, k.factors = k.carve(k.mid, (2, L), (4, L))

    def unit(c, wide):
        x = k.qk[:, c, :]
        chunked = lambda ap: ap[:, META:L].rearrange("p (c s) -> p c s", c=NCH - 1)
        if c < DNK:
            for dst, w, s in ((k.dq[:, c, 0, PAD:CH], wide[:, 0:META], x[:, 0:META]),
                              (k.dq[:, c, 1:NCH, :], chunked(wide), chunked(x))):
                yield nc.vector.scalar_tensor_tensor(dst, w, DNK_SCALE, s, ALU.mult, ALU.mult)
        else:
            i = c - DNK
            two = lambda ap: ap.unsqueeze(1).broadcast_to([P, 2, META])
            four = lambda ap: chunked(ap).unsqueeze(2).broadcast_to([P, NCH - 1, 2, CH])
            yield nc.vector.tensor_tensor(k.kT[:, i, 0, :, PAD:CH], two(wide[:, 0:META]), two(x[:, 0:META]), ALU.mult)
            yield nc.vector.tensor_tensor(k.kT[:, i, 1:NCH, :, :], four(wide), four(x), ALU.mult)
    head_norm_stage(k, [k.qk[:, c, :] for c in range(2 * DNK)], 2 * DNK,
                    lambda c: k.c("one")[:, 15 - c:31 - c],
                    lambda c: [(k.ident[0:16, c:c + 1].broadcast_to([16, P]), slice(0, P))], 1.0, EPS, unit)
    if stop <= 27: return
    k.vn, k.o1, k.E, k.ET, k.R = k.carve(k.mid, (DNK, P), (DNK, P), (DNK, P), (DNK, P), (DNK, P))
    k.const2, k.kbg, k.kst, k.vb, k.attnT = k.carve(k.big, (n_const,), (DNK, P), (DNK, P), (DNK, P), (DNK, P))
    assert 4 * DNK * P <= 2 * DNK * L
    start = sum(int(np.prod(s)) for s in shapes)
    k.pw, k.pwT, k.u = k.carve(k.big[:, start:32768], (DNK, P), (DNK, P), (DNK, P))
    k.wT, = k.carve(k.hT.rearrange('p c n -> p (c n)'), (DNK, P))
    delta_stage(k)
    if stop <= 28: return
    out_rows(k, "dn_out", [(k.h[:, tt, :], 2 * tt, P, tt * P) for tt in range(NT)], DNV,
             lambda c, c0, rows: k.dy[:, c, c0:c0 + rows], k.tiles["end"] + RING)
    sent, = k.start("output_sent")
    with nc.Block() as block:

        @block.sync
        def _(sp):
            for tt in range(NT):
                sp.dma_start(k.out[tt], k.h[:, tt, :]).then_inc(*sent.up(16))
            sp.wait_ge(*sent.last())


DNK_SCALE = P ** -0.5


def dn_lay_out(a):
    w = a["dn_w_in_2"][0]
    z, b, aa = w[:, 4096:6144], w[:, 6144:6160], w[:, 6160:6176]
    ba = np.zeros((D, P), w.dtype)
    order = [0, 2, 4, 6, 8, 10, 12, 14, 1, 3, 5, 7, 9, 11, 13, 15]
    ba[:, 0:16], ba[:, 32:48] = b[:, order], aa[:, order]
    return {"dn_qkv": chunks_T(w[:, :4096]), "dn_z": chunks_T(z), "dn_ba": chunks_T(ba),
            "dn_out": chunks_N(a["dn_w_out_2"][0], 512)}


def dn_params(a):
    order = [0, 2, 4, 6, 8, 10, 12, 14, 1, 3, 5, 7, 9, 11, 13, 15]

    def rows(v):
        out = np.zeros((P, 1), v.dtype)
        out[32:48, 0] = v[order]
        return out
    return {"conv": a["dn_conv_w_2"][0].reshape(4, 32, P).transpose(2, 1, 0).reshape(P, -1),
            "a_log": rows(a["dn_a_log_2"][0]), "dt_bias": rows(a["dn_dt_bias_2"][0]),
            "o_norm": a["dn_o_norm_w_2"][0][:, None]}


def dn_consts():
    r = np.arange(P)
    same = (r[:, None] // CH) == (r[None, :] // CH)
    one = np.zeros((P, 31))
    one[:, 15] = 1
    half = np.stack([r < CH, r >= CH], 1)
    return {"upper": same & (r[:, None] <= r[None, :]), "block": same, "half": half, "one": one,
            "low": np.where(same & (r[:, None] > r[None, :]), 0, NEG),
            "up": np.where(same & (r[:, None] <= r[None, :]), 0, NEG)}


def second_constants():
    f = np.float32
    r = np.arange(P)
    q = r[:, None]
    dist = []
    for tt in range(NT):
        pos_q = META + tt * P + q
        pos = np.arange(L)[None, :]
        d = pos_q - pos
        ok = (d >= 0) & ((pos < META) | (d < P))
        dist.append(np.where(ok, np.minimum(d, P), 1e34))
    meta = np.zeros((P, AH, META), f)
    for i in range(AH):
        h = 2 * (i % 8) + i // 8
        d = np.arange(META)[:, None] - np.arange(META)[None, :]
        meta[:META, i] = np.where(d >= 0, -2.0 ** (-8.0 * (h + 1) / AH) * d, NEG)
    pair = np.zeros((P, 38), f)
    pair[:HD, 18] = pair[HD:, 19] = 1
    return {"dist": np.concatenate(dist, 1), "meta_bias": meta.reshape(P, -1), "pair": pair, **dn_consts()}


def lay_out_second(a):
    w = a["attn_w_in_2"][0]
    q, kk, v, gate = w[:, :1024], w[:, 1024:1152], w[:, 1152:1280], w[:, 1280:]
    twice = lambda m: np.concatenate([m[:, :HD], m[:, :HD], m[:, HD:], m[:, HD:]], 1)
    return {"attn_t": chunks_T(np.concatenate([q, twice(kk), gate], 1)), "attn_v": chunks_N(v, P),
            "attn_out": chunks_N(a["attn_w_out_2"][0], 512),
            "norm_final": np.broadcast_to(a["norm_final"], (P, D)), **dn_lay_out(a)}


def params_second(a):
    col = lambda v: v.reshape(-1, P).T
    both = lambda v: np.concatenate([v, v])[:, None]
    sinks = np.broadcast_to(a["attn_sinks_2"], (P, AH))
    return {"attn_norm": col(a["attn_norm_w_2"][0]), "dn_norm": col(a["dn_norm_w_2"][0]),
            "q_norm": both(a["attn_q_norm_w_2"][0]), "k_norm": both(a["attn_k_norm_w_2"][0]),
            "sinks": sinks, "sinks_placed": np.concatenate([sinks[:, 0::2], sinks[:, 1::2]], 1), **dn_params(a)}


class Build:

    def __init__(self, nc, ctx, dram, const_cols, param_cols):
        self.nc, self.ctx, self.dram = nc, ctx, dram
        self.signals, self.loaded, self.prefetch = {}, 0, RING
        sb = lambda name, cols: ctx.enter_context(nc.sbuf_tensor(name, [P, cols], F32))
        self.ps = ctx.enter_context(nc.psum_tensor("banks", [P, 8, 512], F32))
        self.big, self.mid, self.small = sb("big", 32768), sb("mid", 5248), sb("small", 96)
        self.kept = sb("kept", 2 * NT * PH * TOPK + NT * P)
        self.hbuf = sb("residual", 3 * D)
        self.h = self.hbuf[:, 0:2 * D].rearrange("p (t n) -> p t n", t=NT)
        self.hm = self.hbuf[:, 2 * D:3 * D]
        self.hT = sb("normed", KC * L)[:, :].rearrange("p (c n) -> p c n", c=KC)
        self.const = {}
        self.const_cols = const_cols
        common = const_cols["common"]
        self.common = sb("const", common[1])
        self.bind("common", self.common[:, :])
        self.param_cols = param_cols[0]
        self.param = sb("param", param_cols[1])
        ring = sb("weights", RING * TILE)[:, :].rearrange("p (s n) -> p s n", s=RING)
        sem = lambda name: ctx.enter_context(nc.semaphore(name))
        self.ring = Ring(ring, [sem(f"tile_landed_{s}") for s in range(RING)], Signal(sem("tile_used")))
        self.ident = self.c("ident")

    def bind(self, part, view):
        at = 0
        for name, cols in self.const_cols[part][0]:
            self.const[name] = view[:, at:at + cols]
            at += cols

    def c(self, name):
        return self.const[name]

    def p(self, name):
        a, n = self.param_cols[name]
        return self.param[:, a:a + n]

    def start(self, *names):
        for name in names:
            if name not in self.signals:
                self.signals[name] = Signal(self.ctx.enter_context(self.nc.semaphore(name)))
            self.signals[name].start()
        return [self.signals[name] for name in names]

    def carve(self, region, *shapes):
        at, pieces = 0, []
        for shape in shapes:
            n = int(np.prod(shape))
            piece = region[:, at:at + n]
            if len(shape) > 1:
                names = "abcd"[:len(shape)]
                piece = piece.rearrange(f"p ({' '.join(names)}) -> p {' '.join(names)}", **dict(zip(names, shape)))
            pieces.append(piece)
            at += n
        assert at <= region.shape[1], (at, region.shape)
        return pieces


def program(nc, dram, out, const_cols, param_cols, stop=99):
    with ExitStack() as ctx:
        k = Build(nc, ctx, dram, const_cols, param_cols)
        k.out = out
        plan(k)
        first_block(k, stop)
        if stop > 20:
            second_block(k, stop)
        drain(k)


def drain(k):
    with k.nc.Block() as block:

        @block.sync
        def _(sp):
            for s in range(RING):
                n = sum(k.ring.slots[i] == s for i in range(k.loaded))
                if n:
                    sp.wait_ge(k.ring.landed[s], 16 * n)


def first_block(k, stop):
    ps = k.ps
    (k.T, k.fv, k.vv, k.cmp_in, k.rot, k.gelu, k.kcmp, k.vcmp, k.negc, k.gates, k.soft, k.pt, k.ptc, k.yfox, k.ynsa,
     k.mergedT, k.const1) = k.carve(
        k.big, (N_IN_T, S), (NT, 512), (NT, 256), (2, N_CMP, 32), (4, S), (2, 2, N_CMP), (2 * N_CMP,), (P,), (S,), (NT, 24),
        (2, 4, S), (3, 2, 4, P), (PH, P), (4, S), (4, S), (KC, S),
        (sum((n for _, n in k.const_cols['first'][0])),))
    k.vcmp = k.vcmp[0:N_CMP, :]
    k.bind("first", k.const1)
    input_stage(k)
    norm_stage(k, [(k.h[:, tt, :], P, tt * P) for tt in range(NT)], k.p("norm_mix"), k.hT)
    if stop <= 1: return
    def put(eng, i, src):
        if i < MERGE:
            return k.nc.vector.tensor_copy(k.T[:, i, :], src)
        return k.nc.scalar.activation(k.T[:, i, :], src, ACT.Sigmoid)
    project_T(k, "in_t", N_IN_T, S, lambda c: k.hT[:, c, 0:S],
              (lambda i: "vector" if i < MERGE else "scalar", put), k.tiles["in_fv"] + RING)
    def copy(dst, banks):
        def finish():
            for tt in range(NT):
                yield k.nc.vector.tensor_copy(dst[:, tt, :], ps[:, banks + tt, 0:dst.shape[2]])
        return finish
    lhs = lambda c, tt: k.hT[:, c, tt * P:tt * P + P]
    project_N(k, "in_fv", lhs, [
        (4, 2, 512, [(ps[:, tt, :], tt) for tt in range(NT)], copy(k.fv, 0)),
        (2, 4, 256, [(ps[:, 2 + tt, 0:256], tt) for tt in range(NT)], copy(k.vv, 2))],
        k.tiles["cmp_w1"] + RING)
    if stop <= 2: return
    prepare_stage(k)
    if stop <= 3: return
    attention_stage(k)
    if stop <= 4: return
    merge_stage(k)
    out_rows(k, "out1", [(k.h[:, tt, :], 2 * tt, P, tt * P) for tt in range(NT)], KC,
             lambda c, c0, rows: k.mergedT[:, c, c0:c0 + rows], k.tiles["wq"] + RING)
    if stop <= 5: return
    peer(k, stop)


def out_rows(k, name, tiles, chunks, lhs, prefetch):
    def finish(half):
        def add():
            for h, bank, rows, _ in tiles:
                dst = h[0:rows, half * 512:(half + 1) * 512]
                yield k.nc.vector.tensor_tensor(dst, dst, k.ps[0:rows, bank + half, :], ALU.add)
        return add
    groups = [(chunks // 2, 2, 512, [(k.ps[0:rows, bank + half, :], (c0, rows)) for _, bank, rows, c0 in tiles],
               finish(half)) for half in range(2)]
    project_N(k, name, lambda c, i: lhs(c, *i), groups, prefetch)


def constants():
    f = np.float32
    r = np.arange(P)
    q, s = r[:, None], np.arange(S)[None, :]
    eye = np.eye(P, dtype=f)
    common = {"ident": eye, "ones": np.ones((P, P), f), "iota": np.tile(r[None, :].astype(f), (P, 1))}
    mask = np.concatenate([np.where(s <= q + P * tt, 0, NEG) for tt in range(NT)], 1)
    ends = np.where(np.arange(16) < N_CMP, np.arange(16) * 16 + 31, 10 ** 6)[None, :]
    keep = np.concatenate([ends <= q + P * tt for tt in range(NT)], 1)
    inv = (np.float32(500000.0) ** (-np.arange(0, 16, 2, dtype=f) / f(16))).astype(f)
    row = r % HD
    freq = np.where(row < 16, inv[row % 8], 0).astype(f)[:, None]

    def rope(pos):
        ang = (np.asarray(pos, f)[None, :] * freq).astype(f)
        sin = np.where(row[:, None] < 16, np.sin(ang), 0)
        return np.cos(ang), sin

    cos, sin = rope(np.arange(S))
    ccos, csin = rope(np.arange(16) * 16 + 31)
    perm = np.zeros((P, P), f)
    for m in range(P):
        if m % HD < 8:
            perm[m + 8, m] = -1
        elif m % HD < 16:
            perm[m - 8, m] = 1
    first = {"mask": mask, "cmask": np.where(keep, 0, NEG), "ckeep": keep, "cos": cos, "sin": sin,
             "ccos": ccos, "csin": csin, "perm": perm}
    return {"common": common, "first": first, "second": second_constants()}


def pack(parts):
    cols, arrays = {}, {}
    for part, named in parts.items():
        cols[part] = ([(n, a.shape[1]) for n, a in named.items()], sum(a.shape[1] for a in named.values()))
        arrays["const_" + part] = np.concatenate([a.astype(np.float32) for a in named.values()], 1)
    return cols, arrays


def chunks_T(w):
    n = w.shape[1] // P
    return w.reshape(KC, P, n, P).transpose(2, 1, 0, 3).reshape(n, P, TILE)


def chunks_N(w, cols):
    per = TILE // cols
    c, n = w.shape[0] // P, w.shape[1] // cols
    return w.reshape(c // per, per, P, n, cols).transpose(3, 0, 2, 1, 4).reshape(n * (c // per), P, TILE)


def lay_out(a):
    w = a["w_in"][0]
    at = np.cumsum([0, 512, 512, 512, 8, 512, 128, 128, 128, 128, 128, 128, 24, 2048])
    part = [w[:, at[i]:at[i + 1]] for i in range(13)]
    fq, fk, fv, fl, nq, kc, vc, ksl, vsl, kwn, vwn, gate, merge = part
    twice = lambda m: np.concatenate([m[:, :HD], m[:, :HD], m[:, HD:], m[:, HD:]], 1)
    misc = np.zeros((D, P), w.dtype)
    misc[:, 0:8], misc[:, GATE_ROW:GATE_ROW + 24] = fl, gate
    out = {"in_t": chunks_T(np.concatenate([fq, fk, nq, kc, vc, twice(ksl), twice(kwn), misc, merge], 1)),
           "in_fv": chunks_N(fv, 512),
           "in_vv": chunks_N(np.concatenate([vsl, vwn], 1), 256)}
    w1 = a["nsa_cmp_w1"][0].reshape(2, 32, HD, P).transpose(0, 2, 1, 3)
    w1 = np.concatenate([w1, w1], 1).reshape(2, P, 4, 8 * P).transpose(0, 2, 1, 3)
    out["cmp_w1"] = w1.reshape(8, P, TILE)
    out["branch"] = a["w_branch"][0].reshape(2, 4, P, KC, P).transpose(3, 2, 0, 1, 4).reshape(KC, P, TILE)
    out["out1"] = chunks_N(a["w_out"][0], 512)
    out["wq"] = chunks_T(a["peer_wq"][0])
    out["subk"] = a["peer_subkeys"][0].reshape(16, NKEY, P).transpose(2, 0, 1).reshape(P, 2, TILE).transpose(1, 0, 2)
    u = a["peer_u"][0].reshape(NKEY, NKEY, KC, P)
    out["peer_u"] = u.transpose(1, 3, 2, 0).reshape(NKEY, P, TILE)
    out["peer_v"] = a["peer_v"][0].reshape(NKEY, NKEY, D).transpose(1, 0, 2)
    out["x"] = a["x"][0].reshape(NT, P, D).transpose(1, 0, 2)
    out["meta"] = a["meta_tokens_2"]
    out.update(lay_out_second(a))

    col = lambda v: v.reshape(-1, P).T
    rows = lambda v: np.concatenate([v.reshape(-1, 1), np.zeros((P - v.size, 1), v.dtype)])
    both = lambda v: np.concatenate([v, v])
    params = {"norm_mix": col(a["norm_mix"][0]), "norm_ffn": col(a["norm_ffn"][0]),
              "fbias": rows(a["fox_f_bias"][0]),
              "pos": both(a["nsa_cmp_pos"][0].transpose(2, 0, 1).reshape(HD, 64)),
              "w2k": np.concatenate([a["nsa_cmp_w2"][0, 0]] * 2, 1), "w2v": a["nsa_cmp_w2"][0, 1]}
    params.update(params_second(a))
    cols, at = {}, 0
    for n, v in params.items():
        cols[n] = (at, v.shape[1])
        at += v.shape[1]
    out["param"] = np.concatenate(list(params.values()), 1)
    return out, (cols, at)


def launch(nc, inputs, stop=99):
    arrays, param_cols = lay_out({n: np.asarray(v) for n, v in inputs.items()})
    const_cols, consts = pack(constants())
    arrays.update(consts)
    dram, given = {}, {}
    for name, v in arrays.items():
        given["in_" + name] = v = np.ascontiguousarray(v)
        dram[name] = nc.dram_tensor("in_" + name, v.shape, mybir.dt.from_np(v.dtype), kind="ExternalInput").ap()
    out = nc.dram_tensor("out", (NT, P, D), F32, kind="ExternalOutput").ap()
    program(nc, dram, out, const_cols, param_cols, stop)
    return given


def kernel(**inputs):
    import concourse.bacc as _bacc
    from concourse.bass_utils import run_bass_kernel_spmd as _run

    nc = _bacc.Bacc("TRN2", target_bir_lowering=False, num_devices=1)
    given = launch(nc, inputs)
    return _run(nc, [given], core_ids=[0]).results[0]["out"].reshape(1, S, D)
```

```python
from contextlib import ExitStack

import numpy as np
import concourse.bass as bass
from concourse import mybir

ALU = mybir.AluOpType
ACT = mybir.ActivationFunctionType
AX = mybir.AxisListType
F32 = mybir.dt.float32
F32R = mybir.dt.float32r
U32 = mybir.dt.uint32

P = 128
D = 1024
KC = D // P
S = 256
NT = S // P
META = 16
L = META + S
HD = 64
NEG = -1e30
EPS = 1e-6
RING = 4
BODY = 8
TILE = 1024

FQ, FK, NQ, KCMP, VCMP, KSL, KWN, MISC, MERGE = 0, 4, 8, 12, 13, 14, 16, 18, 19
N_IN_T = 35
GATE_ROW = 32
N_CMP = (S - 32) // 16 + 1
PH, TOPK = 8, 16
NKEY = 128
AH = 16
DNK, DNV = 8, 16
CH = 64
AHEAD = 2
NCH = 5
PAD = NCH * CH - L


class Signal:

    def __init__(self, sem):
        self.sem, self.total, self.base = sem, 0, 0

    def up(self, n=1):
        self.total += n
        return self.sem, n

    def start(self):
        self.base = self.total

    def at(self, k):
        return self.sem, self.base + k

    def last(self):
        return self.sem, self.total


class Ring:

    def __init__(self, buf, landed, used):
        self.buf, self.landed, self.used = buf, landed, used
        self.slots, self.src, self.nth, self.count, self.next = [], [], [], [0] * RING, 0
        self.before, self.holder = [], [None] * RING

    def align(self):
        self.next = 0

    def add(self, src):
        s = self.next
        self.next = (s + 1) % RING
        self.count[s] += 1
        self.before.append(self.holder[s])
        self.holder[s] = len(self.slots)
        self.slots.append(s)
        self.nth.append(self.count[s])
        self.src.append(src)
        return len(self.slots) - 1

    def view(self, n):
        return self.buf[:, self.slots[n], :]


def plan(k):
    r, d = k.ring, k.dram
    k.tiles = {}

    def group(name, src, align=False):
        if align:
            r.align()
        k.tiles[name] = len(r.slots)
        for i in range(src.shape[0]):
            r.add(src[i])

    for name in ("in_t", "in_fv", "in_vv", "cmp_w1", "branch", "out1", "wq", "subk"):
        group(name, d[name])
    r.align()
    k.tiles["u"] = len(r.slots)
    for j in range(NKEY):
        r.add(d["peer_u"][j])
    r.align()
    k.tiles["v"] = len(r.slots)
    for j in range(NKEY):
        r.add(d["peer_v"][j])
    r.align()
    for name in [n for n in ("attn_t", "attn_out", "dn_qkv", "dn_ba", "dn_z", "dn_out") if n in d]:
        group(name, d[name])
    k.tiles["end"] = len(r.slots)
    plain = [n for name in ("cmp_w1", "subk") for n in range(k.tiles[name], k.tiles[name] + d[name].shape[0])]
    k.split, k.low_nth, made = [], [], {"vector": 0, "gpsimd": 0}
    for n in range(len(r.slots)):
        k.split.append(None if n in plain else n - sum(q < n for q in plain))
        engine = "gpsimd" if k.tiles["dn_qkv"] + AHEAD <= n < k.tiles["dn_ba"] and n % 2 else "vector"
        made[engine] += n not in plain
        k.low_nth.append((engine, made[engine]))


def load_tiles(sp, k, upto):
    r = k.ring
    while k.loaded < min(upto, k.tiles["end"]):
        n = k.loaded
        if r.before[n] is not None:
            if r.before[n] >= upto - RING:
                break
            if k.split[r.before[n]] is None:
                sp.wait_ge(r.used.sem, r.before[n] + 1)
            else:
                await_low(sp, k, r.before[n])
        sp.dma_start(r.view(n), r.src[n]).then_inc(r.landed[r.slots[n]], 16)
        k.loaded += 1


def landed(pe, k, n):
    pe.wait_ge(k.ring.landed[k.ring.slots[n]], 16 * k.ring.nth[n])



def make_high(act, k, n):
    if n in k.split_early:
        return
    m = k.split[n]
    landed(act, k, n)
    if m >= 2:
        act.wait_ge(k.high_used.sem, m - 1)
        await_low(act, k, k.split.index(m - 2))
    k.nc.scalar.activation(k.high[:, m % 2, :], k.ring.view(n), ACT.Copy).then_inc(*k.high_made.up())


def make_low(dve, k, n):
    if n in k.split_early:
        return
    m = k.split[n]
    dve.wait_ge(k.high_made.sem, m + 1)
    if m >= 2:
        dve.wait_ge(k.ring.used.sem, k.split.index(m - 2) + 1)
    engine, _ = k.low_nth[n]
    unit = {"vector": k.nc.vector, "gpsimd": k.nc.gpsimd}[engine]
    unit.tensor_tensor(k.low[:, m % 2, :], k.ring.view(n), k.high[:, m % 2, :].bitcast(F32),
                       ALU.subtract).then_inc(*k.low_made[engine].up())


def early(k, name):
    return () if k.tiles[name] == 0 else range(k.tiles[name], k.tiles[name] + AHEAD)


def end_early(k, name):
    k.split_early.update(early(k, name))


def parts(k, n, chunks):
    return [ap[:, k.split[n] % 2, :].rearrange("p (c m) -> p c m", c=chunks) for ap in (k.high, k.low)]


def await_high(pe, k, n):
    pe.wait_ge(k.high_made.sem, k.split[n] + 1)


def await_low(pe, k, n):
    engine, nth = k.low_nth[n]
    pe.wait_ge(k.low_made[engine].sem, nth)


def tile_T(pe, k, n, out, rhs, chunks=KC):
    nc = k.nc
    high, low = parts(k, n, chunks)
    await_high(pe, k, n)
    for part in range(2):
        for c in range(chunks):
            ins = nc.tensor.matmul(out, high[:, c, :], rhs(c)[part], start=part + c == 0, stop=False)
    ins.then_inc(*k.high_used.up())
    await_low(pe, k, n)
    for c in range(chunks):
        ins = nc.tensor.matmul(out, low[:, c, :], rhs(c)[0], start=False, stop=c == chunks - 1)
    tile_used(ins, k, n)


def tile_used(ins, k, n):
    assert k.ring.used.total == n, (k.ring.used.total, n)
    ins.then_inc(*k.ring.used.up())


def norm_stage(k, tiles, weight, cols, following):
    nc, ps = k.nc, k.ps
    summed, meaned, rooted, scaled, turned = k.start("norm_summed", "norm_meaned", "norm_rooted",
                                                     "norm_scaled", "norm_turned")
    copied, parted, left = k.start("norm_copied", "norm_high", "norm_low")
    high, low = k.pair(cols)
    starts = [sum(rows for _, rows in tiles[:i]) for i in range(len(tiles))]
    steps = [(i, half) for i in range(len(tiles)) for half in range(2)]

    def views(i, half):
        rows, c0 = tiles[i][1], starts[i]
        x = xn[:, i, 4 * rows * half:4 * rows * (half + 1)].rearrange("p (c t) -> p c t", c=4)
        return x, *[ap[:, 4 * half:4 * half + 4, c0:c0 + rows] for ap in (high, low)]
    r = k.small[:, 0:16]
    xn = k.mid[:, (3 - len(tiles)) * D:3 * D].rearrange("p (t n) -> p t n", n=D)
    with nc.Block() as block:

        @block.sync
        def _(sp):
            load_tiles(sp, k, k.prefetch)

        @block.scalar
        def _(act):
            for i, (h, rows) in enumerate(tiles):
                nc.scalar.activation(xn[0:rows, i, :], h, ACT.Square,
                                     accum_out=r[0:rows, i:i + 1]).then_inc(*summed.up())
            for i, (h, rows) in enumerate(tiles):
                act.wait_ge(*meaned.at(i + 1))
                nc.scalar.activation(r[0:rows, 6 + i:7 + i], r[0:rows, 3 + i:4 + i],
                                     ACT.Sqrt).then_inc(*rooted.up())
            for n in early(k, following):
                make_high(act, k, n)
            for j, step in enumerate(steps):
                act.wait_ge(*copied.at(j + 1))
                x, hi, _ = views(*step)
                nc.scalar.activation(hi, x, ACT.Copy).then_inc(*parted.up())

        @block.vector
        def _(dve):
            for i, (h, rows) in enumerate(tiles):
                dve.wait_ge(*summed.at(i + 1))
                nc.vector.tensor_scalar(r[0:rows, 3 + i:4 + i], r[0:rows, i:i + 1], 1.0 / D, EPS,
                                        ALU.mult, ALU.add).then_inc(*meaned.up())
            for i, (h, rows) in enumerate(tiles):
                dve.wait_ge(*rooted.at(i + 1))
                nc.vector.reciprocal(r[0:rows, 9 + i:10 + i], r[0:rows, 6 + i:7 + i]).then_inc(*meaned.up())
                dve.wait_ge(*meaned.last())
                y, inv, step = (r[0:rows, a + i:a + i + 1] for a in (3, 9, 12))
                nc.vector.scalar_tensor_tensor(step, inv, inv, y, ALU.mult, ALU.mult).then_inc(*meaned.up())
                dve.wait_ge(*meaned.last())
                nc.vector.tensor_scalar(step, step, -0.5, 1.5, ALU.mult, ALU.add).then_inc(*meaned.up())
                dve.wait_ge(*meaned.last())
                nc.vector.tensor_tensor(inv, inv, step, ALU.mult).then_inc(*meaned.up())
                dve.wait_ge(*meaned.last())
                nc.vector.tensor_scalar(xn[0:rows, i, :], h, inv, None, ALU.mult).then_inc(*scaled.up())
            for n in early(k, following):
                make_low(dve, k, n)

            def subtract(j):
                dve.wait_ge(*parted.at(j + 1))
                x, hi, lo = views(*steps[j])
                nc.vector.tensor_tensor(lo, x, hi.bitcast(F32), ALU.subtract).then_inc(*left.up())
            for j, (i, half) in enumerate(steps):
                rows = tiles[i][1]
                dve.wait_ge(*turned.at(2 * i + 2))
                turn = ps[:, 2 * i + half, 0:4 * rows].rearrange("p (c t) -> p c t", c=4)
                w = weight[:, 4 * half:4 * half + 4].unsqueeze(2).broadcast_to([P, 4, rows])
                nc.vector.tensor_tensor(views(i, half)[0], turn, w, ALU.mult).then_inc(*copied.up())
                if j:
                    subtract(j - 1)
            subtract(len(steps) - 1)

        @block.tensor
        def _(pe):
            for i, (_, rows) in enumerate(tiles):
                pe.wait_ge(*scaled.at(i + 1))
                for c in range(KC):
                    ins = nc.tensor.transpose(ps[:, 2 * i + c // 4, (c % 4) * rows:(c % 4 + 1) * rows],
                                              xn[0:rows, i, c * P:(c + 1) * P], k.ident[0:rows, 0:rows])
                    if c % 4 == 3:
                        ins.then_inc(*turned.up())


def project_T(k, name, chunks, n, write, prefetch):
    nc, ps, first = k.nc, k.ps, k.tiles[name]
    engine, put = write
    high, low = k.pair(n)
    by = {e: k.start("evacuated_" + e)[0] for e in ("vector", "scalar")}
    nth = [sum(engine(j) == engine(i) for j in range(i + 1)) for i in range(chunks)]
    with nc.Block() as block:

        @block.sync
        def _(sp):
            load_tiles(sp, k, prefetch)

        @block.tensor
        def _(pe):
            for i in range(chunks):
                if i >= 8:
                    pe.wait_ge(*by[engine(i - 8)].at(nth[i - 8]))
                tile_T(pe, k, first + i, ps[:, i % 8, 0:n], lambda c: (high[:, c, :], low[:, c, :]))

        @block.vector
        def _(dve):
            for i in range(-AHEAD, chunks):
                if i + AHEAD < chunks:
                    make_low(dve, k, first + i + AHEAD)
                if i >= 0 and engine(i) == "vector":
                    dve.wait_ge(k.ring.used.sem, first + i + 1)
                    put(dve, i, ps[:, i % 8, 0:n]).then_inc(*by["vector"].up())

        @block.scalar
        def _(act):
            for i in range(-AHEAD, chunks):
                if i + AHEAD < chunks:
                    make_high(act, k, first + i + AHEAD)
                if i >= 0 and engine(i) == "scalar":
                    act.wait_ge(k.ring.used.sem, first + i + 1)
                    put(act, i, ps[:, i % 8, 0:n]).then_inc(*by["scalar"].up())


def project_N(k, name, lhs, groups, prefetch):
    nc, first = k.nc, k.tiles[name]
    out, = k.start("rows_out")
    count = sum(g[0] for g in groups)
    with nc.Block() as block:

        @block.sync
        def _(sp):
            load_tiles(sp, k, prefetch)

        @block.tensor
        def _(pe):
            n = first
            for tiles, per, cols, outs, _ in groups:
                for q in range(tiles):
                    high, low = parts(k, n, per)
                    await_high(pe, k, n)
                    for c in range(per):
                        for part in range(2):
                            for o, i in outs:
                                ins = nc.tensor.matmul(o, lhs(q * per + c, i)[part], high[:, c, 0:cols],
                                                       start=q + c + part == 0, stop=False)
                    ins.then_inc(*k.high_used.up())
                    await_low(pe, k, n)
                    for c in range(per):
                        for o, i in outs:
                            ins = nc.tensor.matmul(o, lhs(q * per + c, i)[0], low[:, c, 0:cols], start=False,
                                                   stop=q == tiles - 1 and c == per - 1)
                    tile_used(ins, k, n)
                    n += 1

        @block.scalar
        def _(act):
            for n in range(count):
                make_high(act, k, first + n)

        @block.vector
        def _(dve):
            n = made = 0
            for tiles, _, _, _, finish in groups:
                n += tiles
                for made in range(made, min(n + AHEAD, count)):
                    make_low(dve, k, first + made)
                made = min(n + AHEAD, count)
                dve.wait_ge(k.ring.used.sem, first + n)
                for ins in finish():
                    ins.then_inc(*out.up())


def input_stage(k):
    nc = k.nc
    got, = k.start("inputs_landed")
    with nc.Block() as block:

        @block.sync
        def _(sp):
            for dst, src in ((k.h, k.dram["x"]), (k.common[:, :], k.dram["const_common"]),
                             (k.param[:, :], k.dram["param"]),
                             (k.const1, k.dram["const_first"])):
                sp.dma_start(dst, src).then_inc(*got.up(16))
            load_tiles(sp, k, RING)
            sp.wait_ge(*got.last())


def prepare_stage(k):
    nc, ps, T = k.nc, k.ps, k.T
    vec, turned, filled, acted = k.start("prep_vector", "prep_product", "prep_gelu", "prep_act")
    blocked, = k.start("blocks_made")
    first = k.tiles["cmp_w1"]
    f = k.mid[0:PH, 0:4 * S].rearrange("p (a n) -> p a n", a=4)
    blocks = k.cmp_in
    rot = k.rot
    gl = k.gelu
    with nc.Block() as block:

        @block.sync
        def _(sp):
            load_tiles(sp, k, k.tiles["branch"] + RING)

        @block.scalar
        def _(act):
            gate = T[GATE_ROW:GATE_ROW + 24, MISC, :]
            nc.scalar.activation(gate, gate, ACT.Sigmoid).then_inc(*acted.up())
            act.wait_ge(*vec.at(2))
            nc.scalar.activation(f[:, 1, :], f[:, 1, :], ACT.Exp).then_inc(*acted.up())
            act.wait_ge(*acted.last())
            nc.scalar.activation(f[:, 2, :], f[:, 1, :], ACT.Ln, bias=1.0).then_inc(*acted.up())
            for j in range(2):
                act.wait_ge(k.ring.used.sem, first + 2 * j + 2)
                nc.scalar.activation(gl[:, j].rearrange("p g n -> p (g n)"), ps[:, j, 0:2 * N_CMP],
                                     ACT.Gelu).then_inc(*filled.up())

        @block.vector
        def _(dve):
            for j in range(2):
                for g in range(2):
                    rows = slice(HD * g, HD * g + HD)
                    for s in range(2):
                        src = T[rows, KCMP + j, 16 * s:S]
                        src = bass.AP(src.tensor, src.offset, [list(src.ap[0]), [16, N_CMP], [1, 16]])
                        pos = k.p("pos")[rows, 32 * j + 16 * s:32 * j + 16 * s + 16]
                        nc.vector.tensor_tensor(blocks[HD * s:HD * s + HD, j, g, :, :], src,
                                                pos.unsqueeze(1).broadcast_to([HD, N_CMP, 16]),
                                                ALU.add).then_inc(*blocked.up())
            nc.vector.tensor_scalar(f[:, 0, :], T[0:PH, MISC, :], k.p("fbias")[0:PH, :], None,
                                    ALU.add).then_inc(*vec.up())
            dve.wait_ge(*vec.last())
            nc.vector.scalar_tensor_tensor(f[:, 1, :], f[:, 0, :], -1.0, f[:, 0, :], ALU.mult,
                                           ALU.min).then_inc(*vec.up())
            dve.wait_ge(*acted.at(3))
            nc.vector.scalar_tensor_tensor(f[:, 3, :], f[:, 0, :], 0.0, f[:, 2, :], ALU.min,
                                           ALU.subtract).then_inc(*vec.up())
            dve.wait_ge(*vec.last())
            nc.vector.tensor_tensor_scan(f[:, 1, :], k.c("ones")[0:PH, 0:1].broadcast_to([PH, S]), f[:, 3, :], 0.0,
                                         ALU.mult, ALU.add).then_inc(*vec.up())
            dve.wait_ge(*vec.last())
            for base in (0, HD):
                nc.vector.tensor_scalar(k.negc[base:base + PH, :], f[:, 1, :], -8.0, None,
                                        ALU.mult).then_inc(*vec.up())
            dve.wait_ge(*turned.at(1))
            nc.vector.tensor_copy(k.gates, ps[:, 4:6, 0:24]).then_inc(*vec.up())
            for b, c0 in enumerate((NQ, KSL)):
                dve.wait_ge(*turned.at(2 + b))
                x, y = T[:, c0:c0 + 4, :], rot[:, :, :]
                sin = k.c("sin").unsqueeze(1).broadcast_to([P, 4, S])
                cos = k.c("cos").unsqueeze(1).broadcast_to([P, 4, S])
                swapped = ps[:, 6:8, :].rearrange("p b (c n) -> p (b c) n", c=2)
                nc.vector.tensor_tensor(y, swapped, sin, ALU.mult).then_inc(*vec.up())
                nc.vector.tensor_tensor(x, x, cos, ALU.mult).then_inc(*vec.up())
                dve.wait_ge(*vec.last())
                nc.vector.tensor_tensor(x, x, y, ALU.add).then_inc(*vec.up())
                dve.wait_ge(*vec.last())
            dve.wait_ge(*turned.at(4))
            nc.vector.tensor_copy(k.kcmp, ps[:, 4, 0:2 * N_CMP]).then_inc(*vec.up())
            nc.vector.tensor_copy(k.vcmp, ps[0:N_CMP, 5, 0:P]).then_inc(*vec.up())
            dve.wait_ge(*vec.last())
            kc = k.kcmp.rearrange("p (g n) -> p g n", g=2)
            tmp = rot[:, 0, 0:2 * N_CMP].rearrange("p (g n) -> p g n", g=2)
            cos = k.c("ccos")[:, 0:N_CMP].unsqueeze(1).broadcast_to([P, 2, N_CMP])
            sin = k.c("csin")[:, 0:N_CMP].unsqueeze(1).broadcast_to([P, 2, N_CMP])
            dve.wait_ge(*turned.at(5))
            nc.vector.tensor_tensor(tmp, ps[:, 6, 0:2 * N_CMP].rearrange("p (g n) -> p g n", g=2), sin,
                                    ALU.mult).then_inc(*vec.up())
            nc.vector.tensor_tensor(kc, kc, cos, ALU.mult).then_inc(*vec.up())
            dve.wait_ge(*vec.last())
            nc.vector.tensor_tensor(kc, kc, tmp, ALU.add).then_inc(*vec.up())

        @block.tensor
        def _(pe):
            pe.wait_ge(*acted.at(1))
            for tt in range(NT):
                ins = nc.tensor.transpose(ps[:, 4 + tt, 0:24], T[GATE_ROW:GATE_ROW + 24, MISC, tt * P:tt * P + P],
                                          k.ident[GATE_ROW:GATE_ROW + 24, GATE_ROW:GATE_ROW + 24])
            ins.then_inc(*turned.up())
            for b, c0 in enumerate((NQ, KSL)):
                if b:
                    pe.wait_ge(*vec.at(8))
                for c in range(4):
                    ins = nc.tensor.matmul(ps[:, 6 + c // 2, (c % 2) * S:(c % 2) * S + S], k.c("perm"),
                                           T[:, c0 + c, :], start=True, stop=True)
                ins.then_inc(*turned.up())
            for j in range(2):
                pe.wait_ge(*blocked.at(4 * j + 4))
                for q in range(2):
                    n = first + 2 * j + q
                    landed(pe, k, n)
                    w = k.ring.view(n).rearrange("p (l m) -> p l m", l=8)
                    for l in range(8):
                        ins = nc.tensor.matmul(ps[:, j, 0:2 * N_CMP].rearrange("p (g n) -> p g n", g=2), w[:, l, :],
                                               blocks[:, j, :, :, 8 * q + l], start=q + l == 0, stop=q == 1 and l == 7)
                    tile_used(ins, k, n)
            pe.wait_ge(*vec.at(7))
            pe.wait_ge(*filled.at(2))
            for g in range(2):
                nc.tensor.matmul(ps[:, 4, g * N_CMP:(g + 1) * N_CMP], k.p("w2k"), gl[:, 0, g, :],
                                 start=True, stop=True)
                ins = nc.tensor.matmul(ps[0:N_CMP, 5, g * HD:(g + 1) * HD], gl[:, 1, g, :], k.p("w2v"),
                                       start=True, stop=True)
            ins.then_inc(*turned.up())
            pe.wait_ge(*vec.at(15))
            nc.tensor.matmul(ps[:, 6, 0:2 * N_CMP], k.c("perm"), k.kcmp, start=True,
                             stop=True).then_inc(*turned.up())


def attention_stage(k):
    nc, ps, T = k.nc, k.ps, k.T
    scored, masked, peaked, exped = k.start("att_scored", "att_masked", "att_peaked", "att_exped")
    scaled, turned, unturned, summed = k.start("att_scaled", "att_turned", "att_copied", "att_valued")
    stored, stats = k.start("att_stored", "att_stats")
    units = []
    for tt in range(NT):
        units += [(tt, "fox", 0), (tt, "fox", 1), (tt, "cmp", 0)]
        units += [(tt, b, g) for g in range(2) for b in ("slc", "win")]
    n_exp = [0]
    for _, kind, _ in units:
        n_exp.append(n_exp[-1] + (1 if kind == "cmp" else 4))
    valued = [u for u, (_, kind, _) in enumerate(units) if kind in ("fox", "win")]
    done_by = lambda u: sum(v <= u for v in valued)
    soft = k.soft
    pt, ptc, st = k.pt, k.ptc, k.small[:, 0:96].rearrange("p (s a h) -> p s a h", s=2, a=6)
    few = lambda ap: ap.rearrange("p a b -> p (a b)")[:, 0:PH * 16].rearrange("p (h n) -> p h n", h=PH)[:, :, 0:N_CMP]
    wide = lambda ap, n, m: ap.unsqueeze(2).broadcast_to([P, n, m])
    place = lambda j: 2 * (j % 2) + j // 2
    place_few = lambda h: 4 * (h % 2) + h // 2
    few_scores = lambda s: ps[:, 2 * s:2 * s + 2, 0:4 * 16].rearrange("p b (c n) -> p b c n", n=16)[:, :, :, 0:N_CMP]
    with nc.Block() as block:

        @block.sync
        def _(sp):
            load_tiles(sp, k, k.tiles["branch"] + RING)

        @block.tensor
        def _(pe):
            def scores(u):
                tt, kind, a = units[u]
                if u >= 2:
                    pe.wait_ge(*masked.at(u - 1))
                q = slice(tt * P, tt * P + P)
                n = (tt + 1) * P
                out = ps[:, 2 * (u % 2):2 * (u % 2) + 2, :].rearrange("p b (h n) -> p (b h) n", h=2)
                if kind == "cmp":
                    out = few_scores(u % 2)
                    for h in range(PH):
                        g = h // 4
                        rows = slice(HD * (h % 2), HD * (h % 2) + HD)
                        ins = nc.tensor.matmul(out[:, h % 2, h // 2, :], T[rows, NQ + h // 2, q],
                                               k.kcmp[rows, g * N_CMP:(g + 1) * N_CMP], start=True, stop=True)
                else:
                    for j in range(4):
                        h = 4 * a + j
                        rows = slice(HD * (h % 2), HD * (h % 2) + HD)
                        if kind == "fox":
                            nc.tensor.matmul(out[:, place(j), 0:n], T[rows, FQ + h // 2, q],
                                             T[rows, FK + h // 2, 0:n], start=True, stop=False)
                            head = slice(HD * (h % 2), HD * (h % 2) + PH)
                            ins = nc.tensor.matmul(out[:, place(j), 0:n], k.ident[head, head.start + h:head.start + h + 1].broadcast_to([PH, P]),
                                                   k.negc[head, 0:n], start=False, stop=True)
                        else:
                            keys = (KSL if kind == "slc" else KWN) + a
                            ins = nc.tensor.matmul(out[:, place(j), 0:n], T[rows, NQ + h // 2, q],
                                                   T[rows, keys, 0:n], start=True, stop=True)
                ins.then_inc(*scored.up())

            def turn(u):
                tt, kind, _ = units[u]
                pe.wait_ge(*scaled.at(u + 1))
                if u:
                    pe.wait_ge(*unturned.at(u))
                if kind == "cmp":
                    src = few(soft[:, u % 3, :, :])
                    for h in range(PH):
                        ins = nc.tensor.transpose(ps[0:N_CMP, 4 + h // 4, (h % 4) * P:(h % 4) * P + P],
                                                  src[:, h, :], k.ident)
                else:
                    for kt in range(tt + 1):
                        for j in range(4):
                            ins = nc.tensor.transpose(ps[:, 4 + kt, j * P:j * P + P],
                                                      soft[:, u % 3, j, kt * P:kt * P + P], k.ident)
                ins.then_inc(*turned.up())

            def values(u):
                tt, kind, a = units[u]
                if kind not in ("fox", "win"):
                    return
                m = done_by(u) - 1
                pe.wait_ge(*unturned.at(u + 1))
                if m >= 2:
                    pe.wait_ge(*stored.at(m - 1))
                for j in range(4):
                    h = 4 * a + j
                    out = ps[HD * (j % 2):HD * (j % 2) + HD, 6 + m % 2, (j // 2) * P:(j // 2) * P + P]
                    terms = []
                    if kind == "fox":
                        for kt in range(tt + 1):
                            terms.append((k.fv[:, kt, h * HD:(h + 1) * HD], pt[:, u % 3, kt, place(j), :]))
                    else:
                        terms.append((k.vcmp[:, a * HD:(a + 1) * HD], ptc[0:N_CMP, place_few(h), :]))
                        for b in range(2):
                            for kt in range(tt + 1):
                                terms.append((k.vv[:, kt, b * P + a * HD:b * P + (a + 1) * HD],
                                              pt[:, (u - 1 + b) % 3, kt, place(j), :]))
                    for i, (v, p) in enumerate(terms):
                        ins = nc.tensor.matmul(out, v, p, start=i == 0, stop=i == len(terms) - 1)
                ins.then_inc(*summed.up())

            scores(0)
            scores(1)
            for u in range(len(units) + 1):
                if u + 2 < len(units):
                    scores(u + 2)
                if u:
                    values(u - 1)
                if u < len(units):
                    turn(u)

        @block.vector
        def _(dve):
            def peaks(u):
                tt, kind, _ = units[u]
                n = (tt + 1) * P
                dve.wait_ge(*scored.at(u + 1))
                if u >= 3:
                    dve.wait_ge(*turned.at(u - 2))
                s, b = u % 2, u % 3
                out = ps[:, 2 * s:2 * s + 2, :].rearrange("p b (h n) -> p (b h) n", h=2)
                if kind == "cmp":
                    src, dst = few_scores(s), few(soft[:, b, :, :]).rearrange("p (b c) n -> p b c n", b=2)
                    mask = k.c("cmask")[:, 16 * tt:16 * tt + N_CMP].unsqueeze(1).broadcast_to([P, 4, N_CMP])
                    heads = PH
                else:
                    src, dst = out[:, :, 0:n], soft[:, b, :, 0:n]
                    mask = k.c("mask")[:, S * tt:S * tt + n].unsqueeze(1).broadcast_to([P, 4, n])
                    heads = 4
                if kind == "cmp":
                    nc.vector.scalar_tensor_tensor(dst[:, 0, :, :], src[:, 0, :, :], HD ** -0.5, mask,
                                                   ALU.mult, ALU.add).then_inc(*stats.up())
                    dve.wait_ge(*stats.last())
                    dst, src = dst[:, 1, :, :], src[:, 1, :, :]
                nc.vector.scalar_tensor_tensor(dst, src, HD ** -0.5, mask, ALU.mult, ALU.add).then_inc(*masked.up())
                dve.wait_ge(*masked.last())
                if kind == "cmp":
                    dst = few(soft[:, b, :, :])
                nc.vector.tensor_reduce(st[:, s, 0, 0:heads], dst, AX.X, ALU.max).then_inc(*stats.up())
                dve.wait_ge(*stats.last())
                if kind == "cmp":
                    nc.vector.tensor_tensor(dst, dst, wide(st[:, s, 0, 0:heads], heads, N_CMP),
                                            ALU.subtract).then_inc(*peaked.up())
                else:
                    nc.vector.tensor_scalar(st[:, s, 1, 0:4], st[:, s, 0, 0:4], -1.0, None,
                                            ALU.mult).then_inc(*peaked.up())

            def scale(u):
                tt, kind, a = units[u]
                s = u % 2
                n = (tt + 1) * P
                dve.wait_ge(*exped.at(n_exp[u + 1]))
                if kind == "cmp":
                    dst, heads, n = few(soft[:, u % 3, :, :]), PH, N_CMP
                    nc.vector.tensor_reduce(st[:, s, 2, :], dst, AX.X, ALU.add).then_inc(*stats.up())
                    dve.wait_ge(*stats.last())
                else:
                    dst, heads = soft[:, u % 3, :, 0:n], 4
                nc.vector.reciprocal(st[:, s, 3, 0:heads], st[:, s, 2, 0:heads]).then_inc(*stats.up())
                dve.wait_ge(*stats.last())
                w = st[:, s, 3, 0:heads]
                if kind != "fox":
                    b = ("cmp", "slc", "win").index(kind)
                    gate = k.gates[:, tt, 12 * a:12 * a + 3 * heads].rearrange("p (c o r) -> p o c r", o=2, r=3)[:, :, :, b]
                    nc.vector.tensor_tensor(st[:, s, 4, 0:heads].rearrange("p (o c) -> p o c", o=2),
                                            w.rearrange("p (o c) -> p o c", o=2), gate, ALU.mult).then_inc(*stats.up())
                    dve.wait_ge(*stats.last())
                    w = st[:, s, 4, 0:heads]
                if kind == "cmp":
                    keep = k.c("ckeep")[:, 16 * tt:16 * tt + N_CMP].unsqueeze(1).broadcast_to([P, PH, N_CMP])
                    nc.vector.tensor_tensor(dst, dst, keep, ALU.mult).then_inc(*stats.up())
                    dve.wait_ge(*stats.last())
                nc.vector.tensor_tensor(dst, dst, wide(w, heads, n), ALU.mult).then_inc(*scaled.up())

            for u in range(len(units) + 1):
                if u < len(units):
                    peaks(u)
                if u:
                    scale(u - 1)
                if u == 2:
                    for n in early(k, "branch"):
                        make_low(dve, k, n)

        @block.scalar
        def _(act):
            def exps(u):
                tt, kind, _ = units[u]
                s = u % 2
                act.wait_ge(*peaked.at(u + 1))
                if kind == "cmp":
                    dst = few(soft[:, u % 3, :, :])
                    nc.scalar.activation(dst, dst, ACT.Exp).then_inc(*exped.up())
                    return
                for j in range(4):
                    p = soft[:, u % 3, j, 0:(tt + 1) * P]
                    nc.scalar.activation(p, p, ACT.Exp, bias=st[:, s, 1, j:j + 1],
                                         accum_out=st[:, s, 2, j:j + 1]).then_inc(*exped.up())

            def copy_turned(u):
                tt, kind, _ = units[u]
                act.wait_ge(*turned.at(u + 1))
                if u >= 3 and done_by(u - 2):
                    act.wait_ge(*summed.at(done_by(u - 2)))
                if kind == "cmp":
                    nc.scalar.activation(ptc[0:N_CMP, :, :].rearrange("p (a h) n -> p a (h n)", a=2),
                                         ps[0:N_CMP, 4:6, :], ACT.Copy).then_inc(*unturned.up())
                else:
                    nc.scalar.activation(pt[:, u % 3, 0:tt + 1, :, :].rearrange("p t h n -> p t (h n)"),
                                         ps[:, 4:5 + tt, :], ACT.Copy).then_inc(*unturned.up())

            def store(u):
                tt, kind, a = units[u]
                if kind not in ("fox", "win"):
                    return
                m = done_by(u) - 1
                act.wait_ge(*summed.at(m + 1))
                y = k.yfox if kind == "fox" else k.ynsa
                nc.scalar.activation(y[:, 2 * a:2 * a + 2, tt * P:tt * P + P],
                                     ps[:, 6 + m % 2, 0:2 * P].rearrange("p (c n) -> p c n", c=2),
                                     ACT.Copy).then_inc(*stored.up())

            for u in range(len(units) + 2):
                if u < len(units):
                    exps(u)
                if 1 <= u <= len(units):
                    copy_turned(u - 1)
                if u == 2:
                    for n in early(k, "branch"):
                        make_high(act, k, n)
                if u >= 2:
                    store(u - 2)


def merge_stage(k):
    nc, ps = k.nc, k.ps
    first = k.tiles["branch"]
    gated, merged, y_high, y_low = k.start("merge_gated", "merged", "branch_high", "branch_low")
    t = k.mid[:, 0:4 * S].rearrange("p (a n) -> p a n", a=4)
    high_y, low_y = (ap.rearrange("p (b c) n -> p b c n", b=2) for ap in k.pair(S))
    ys = (k.yfox, k.ynsa)
    with nc.Block() as block:

        @block.sync
        def _(sp):
            load_tiles(sp, k, k.tiles["out1"] + RING)

        @block.tensor
        def _(pe):
            for c in range(KC):
                n = first + c
                high, low = parts(k, n, 8)
                await_high(pe, k, n)
                if c >= 4:
                    pe.wait_ge(*gated.at(2 * (c - 3)))
                for b in range(2):
                    for part, (y, ready) in enumerate(((high_y, y_high), (low_y, y_low))):
                        if c == 0:
                            pe.wait_ge(*ready.at(b + 1))
                        for q in range(4):
                            ins = nc.tensor.matmul(ps[:, 2 * (c % 4) + b, 0:S], high[:, 4 * b + q, :],
                                                   y[:, b, q, :], start=part + q == 0, stop=False)
                ins.then_inc(*k.high_used.up())
                await_low(pe, k, n)
                for b in range(2):
                    for q in range(4):
                        ins = nc.tensor.matmul(ps[:, 2 * (c % 4) + b, 0:S], low[:, 4 * b + q, :],
                                               high_y[:, b, q, :], start=False, stop=q == 3)
                tile_used(ins, k, n)

        @block.scalar
        def _(act):
            for b in range(2):
                nc.scalar.activation(high_y[:, b], ys[b], ACT.Copy).then_inc(*y_high.up())
            for c in range(KC):
                make_high(act, k, first + c)

        @block.vector
        def _(dve):
            for b in range(2):
                dve.wait_ge(*y_high.at(b + 1))
                nc.vector.tensor_tensor(low_y[:, b], ys[b], high_y[:, b].bitcast(F32),
                                        ALU.subtract).then_inc(*y_low.up())
            for c in range(-AHEAD, KC):
                if c + AHEAD < KC:
                    make_low(dve, k, first + c + AHEAD)
                if c < 0:
                    continue
                dve.wait_ge(k.ring.used.sem, first + c + 1)
                if c >= 2:
                    dve.wait_ge(*merged.at(c - 1))
                for b in range(2):
                    nc.vector.tensor_tensor(t[:, 2 * (c % 2) + b, :], ps[:, 2 * (c % 4) + b, 0:S],
                                            k.T[:, MERGE + KC * b + c, :], ALU.mult).then_inc(*gated.up())
                dve.wait_ge(*gated.last())
                nc.vector.tensor_tensor(k.mergedT[:, c, :], t[:, 2 * (c % 2), :], t[:, 2 * (c % 2) + 1, :],
                                        ALU.add).then_inc(*merged.up())


def scores_stage(k):
    nc, ps = k.nc, k.ps
    first = k.tiles["subk"]
    taken, = k.start("scores_taken")
    with nc.Block() as block:

        @block.sync
        def _(sp):
            load_tiles(sp, k, k.tiles["u"] + RING)

        @block.tensor
        def _(pe):
            for q in range(2):
                landed(pe, k, first + q)
                keys = k.ring.view(first + q).rearrange("p (a n) -> p a n", a=8)
                for a in range(8):
                    for tt in range(NT):
                        ins = nc.tensor.matmul(ps[:, 4 * tt + 2 * q + a // 4, (a % 4) * P:(a % 4) * P + P],
                                               k.qT[:, 8 * q + a, tt * P:tt * P + P], keys[:, a, :],
                                               start=True, stop=True)
                tile_used(ins, k, first + q)

        @block.scalar
        def _(act):
            for n in early(k, "u"):
                make_high(act, k, n)

        @block.vector
        def _(dve):
            for n in early(k, "u"):
                make_low(dve, k, n)
            for q in range(2):
                dve.wait_ge(k.ring.used.sem, first + q + 1)
                for tt in range(NT):
                    src = ps[:, 4 * tt + 2 * q:4 * tt + 2 * q + 2, :].rearrange("p b n -> p (b n)")
                    nc.vector.tensor_copy(k.score[:, tt, 8 * q:8 * q + 8, :].rearrange("p a n -> p (a n)"),
                                          src).then_inc(*taken.up())


def top16(nc, dve, sig, values, top, index):
    for half in range(2):
        best, at = top[:, 8 * half:8 * half + 8], index[:, 8 * half:8 * half + 8]
        nc.vector.max(best, values).then_inc(*sig.up())
        dve.wait_ge(*sig.last())
        nc.vector.max_index(at, best, values).then_inc(*sig.up())
        if half == 0:
            dve.wait_ge(*sig.last())
            nc.vector.match_replace(values, best, values, -3e38).then_inc(*sig.up())
            dve.wait_ge(*sig.last())


def fori_load(sp, k, first, src, i, j):
    sp.wait_ge(k.low_made["vector"].sem, i * BODY + (k.low_nth[first][1] + j - RING))
    tile = src[j] if type(i) is int else src[bass.ds(i * BODY + j, 1), :, :].rearrange("a p n -> (a p) n")
    sp.dma_start(k.ring.buf[:, j % RING, :], tile).then_inc(k.ring.landed[j % RING], 16)


def fori_high(act, k, first, i, j):
    if type(i) is int and first + i * BODY + j in k.split_early:
        return
    s = k.split[first]
    act.wait_ge(k.ring.landed[j % RING], i * (16 * BODY // RING) + 16 * (k.ring.nth[first + j % RING] + j // RING))
    act.wait_ge(k.high_used.sem, i * BODY + (s + j - 1))
    act.wait_ge(k.low_made["vector"].sem, i * BODY + (k.low_nth[first][1] + j - 2))
    k.nc.scalar.activation(k.high[:, (s + j) % 2, :], k.ring.buf[:, j % RING, :], ACT.Copy).then_inc(k.high_made.sem, 1)


def fori_low(dve, k, first, i, j):
    if type(i) is int and first + i * BODY + j in k.split_early:
        return
    s = k.split[first]
    dve.wait_ge(k.high_made.sem, i * BODY + (s + j + 1))
    dve.wait_ge(k.ring.used.sem, i * BODY + (first + j - 1))
    k.nc.vector.tensor_tensor(k.low[:, (s + j) % 2, :], k.ring.buf[:, j % RING, :],
                              k.high[:, (s + j) % 2, :].bitcast(F32), ALU.subtract).then_inc(k.low_made["vector"].sem, 1)


def after_fori(k):
    k.high_used.total += NKEY
    k.high_made.total += NKEY - AHEAD
    k.low_made["vector"].total += NKEY - AHEAD


def experts_in_stage(k):
    nc, ps = k.nc, k.ps
    first = k.tiles["u"]
    gelu, pick, = k.start("gelu_stored", "top_picked")
    ring, src = k.ring, k.dram["peer_u"]
    used = ring.used
    rounds = NKEY // BODY
    s = k.split[first]
    low_made, low0 = k.low_made["vector"], k.low_nth[first][1] - 1
    assert k.loaded == first + RING and used.total == first
    with nc.Block() as block:

        @block.sync
        def _(sp):
            for j in range(RING, BODY):
                fori_load(sp, k, first, src, 0, j)
            with sp.Fori(1, rounds) as i:
                for j in range(BODY):
                    fori_load(sp, k, first, src, i, j)
            k.loaded = first + NKEY
            load_tiles(sp, k, k.loaded + RING)

        @block.tensor
        def _(pe):
            def one_round(i):
                for j in range(BODY):
                    high, low = parts(k, first + j, KC)
                    pe.wait_ge(k.high_made.sem, i * BODY + (s + j + 1))
                    if type(i) is not int:
                        pe.wait_ge(gelu.sem, i * BODY + (gelu.base + j - BODY + 1))
                    for part, x in enumerate(k.pair(S)):
                        for c in range(KC):
                            ins = nc.tensor.matmul(ps[:, j, 0:S], high[:, c, :], x[:, c, :],
                                                   start=part + c == 0, stop=False)
                    ins.then_inc(k.high_used.sem, 1)
                    pe.wait_ge(low_made.sem, i * BODY + (low0 + j + 1))
                    for c in range(KC):
                        ins = nc.tensor.matmul(ps[:, j, 0:S], low[:, c, :], k.pair(S)[0][:, c, :],
                                               start=False, stop=c == KC - 1)
                    ins.then_inc(used.sem, 1)
            one_round(0)
            with pe.Fori(1, rounds) as i:
                one_round(i)

        @block.scalar
        def _(act):
            def one_round(i):
                for j in range(BODY):
                    fori_high(act, k, first, i, j)
                    if j == 0 and type(i) is int:
                        continue
                    b = (j - 1) % BODY
                    act.wait_ge(used.sem, i * BODY + (first + j))
                    out = k.coef[:, b, :] if type(i) is int else \
                        k.coef[:, bass.ds(i * BODY + (j - 1), 1), :].rearrange("p a t -> p (a t)")
                    nc.scalar.activation(out, ps[:, b, 0:S], ACT.Gelu).then_inc(gelu.sem, 1)
            one_round(0)
            with act.Fori(1, rounds) as i:
                one_round(i)
            act.wait_ge(used.sem, first + NKEY)
            nc.scalar.activation(k.coef[:, NKEY - 1, :], ps[:, BODY - 1, 0:S], ACT.Gelu).then_inc(gelu.sem, 1)

        @block.vector
        def _(dve):
            def wait():
                dve.wait_ge(*pick.last())

            def picks(tt):
                for a in range(2 * PH):
                    top16(nc, dve, pick, k.score[:, tt, a, :], k.top[:, a, :], k.at[:, a, :])
                    yield
                wait()
                nc.vector.tensor_copy(k.atf, k.at).then_inc(*pick.up())
                cand = k.score[:, tt, :, :].rearrange("p a n -> p (a n)").rearrange("p (h a b) -> p h a b", h=PH, a=TOPK)
                halves = k.top.rearrange("p (h o) a -> p o h a", o=2)
                nc.vector.tensor_tensor(cand, halves[:, 0].unsqueeze(3).broadcast_to([P, PH, TOPK, TOPK]),
                                        halves[:, 1].unsqueeze(2).broadcast_to([P, PH, TOPK, TOPK]),
                                        ALU.add).then_inc(*pick.up())
                wait()
                for h in range(PH):
                    top16(nc, dve, pick, cand[:, h].rearrange("p a b -> p (a b)"), k.best[:, tt, h, :], k.pos[:, h, :])
                    yield
                wait()
                flat = lambda ap: ap.rearrange("p h a -> p (h a)")
                for o, (op, operand) in enumerate(((ALU.logical_shift_right, 4), (ALU.bitwise_and, 15))):
                    nc.vector.tensor_scalar(flat(k.part), flat(k.pos), operand, None, op).then_inc(*pick.up())
                    wait()
                    nc.vector.tensor_copy(k.partf, k.part).then_inc(*pick.up())
                    wait()
                    eq = k.score[:, tt, :, :].rearrange("p a n -> p (a n)").rearrange("p (h a b) -> p h a b", h=PH, a=TOPK)
                    eq3 = eq.rearrange("p h a b -> p (h a) b")
                    nc.vector.tensor_tensor(eq3, flat(k.partf).unsqueeze(2).broadcast_to([P, P, TOPK]),
                                            k.c("iota")[:, 0:TOPK].unsqueeze(1).broadcast_to([P, P, TOPK]),
                                            ALU.is_equal).then_inc(*pick.up())
                    yield
                    wait()
                    table = k.atf.rearrange("p (h o) a -> p o h a", o=2)[:, o].unsqueeze(2).broadcast_to([P, PH, TOPK, TOPK])
                    nc.vector.tensor_tensor(eq, eq, table, ALU.mult).then_inc(*pick.up())
                    yield
                    wait()
                    nc.vector.tensor_reduce(k.chosen[:, tt, o, :], eq3, AX.X, ALU.add).then_inc(*pick.up())
                    yield

            beside = 10 * BODY
            n = 0
            for n in range(AHEAD):
                fori_low(dve, k, first, n // BODY, n % BODY)
            n, step = AHEAD, 0
            for tt in range(NT):
                for _ in picks(tt):
                    step += 1
                    while n < min(beside, AHEAD + 4 * step // 3):
                        fori_low(dve, k, first, n // BODY, n % BODY)
                        n += 1
            for n in range(n, beside):
                fori_low(dve, k, first, n // BODY, n % BODY)
            with dve.Fori(beside // BODY, rounds) as i:
                for j in range(BODY):
                    fori_low(dve, k, first, i, j)
    after_fori(k)
    used.total += NKEY
    gelu.total += NKEY


def choice_stage(k):
    nc, ps = k.nc, k.ps
    vec, exped, turned = k.start("choice_vector", "choice_exped", "choice_turned")
    best = k.best.rearrange("p t h a -> p (t h) a")
    lead, total, inverse = (k.small[:, 16 * i:16 * i + 16] for i in range(3))
    wide = lambda ap: ap.unsqueeze(2).broadcast_to([P, NT * PH, TOPK])
    with nc.Block() as block:

        @block.vector
        def _(dve):
            nc.vector.tensor_copy(lead, best[:, :, 0]).then_inc(*vec.up())
            dve.wait_ge(*vec.last())
            nc.vector.tensor_tensor(best, best, wide(lead), ALU.subtract).then_inc(*vec.up())
            dve.wait_ge(*exped.at(1))
            nc.vector.tensor_reduce(total, best, AX.X, ALU.add).then_inc(*vec.up())
            dve.wait_ge(*vec.last())
            nc.vector.reciprocal(inverse, total).then_inc(*vec.up())
            dve.wait_ge(*vec.last())
            nc.vector.tensor_tensor(best, best, wide(inverse), ALU.mult).then_inc(*vec.up())
            for n in early(k, "v"):
                make_low(dve, k, n)
            for o in range(3):
                dve.wait_ge(*turned.at(o + 1))
                nc.vector.tensor_copy(k.chosenT[:, o, :], ps[:, o, 0:S]).then_inc(*vec.up())

        @block.scalar
        def _(act):
            act.wait_ge(*vec.at(2))
            nc.scalar.activation(best, best, ACT.Exp).then_inc(*exped.up())
            for n in early(k, "v"):
                make_high(act, k, n)

        @block.tensor
        def _(pe):
            for o in range(3):
                if o == 2:
                    pe.wait_ge(*vec.at(5))
                for tt in range(NT):
                    src = k.chosen[:, tt, o, :] if o < 2 else k.best[:, tt].rearrange("p h a -> p (h a)")
                    ins = nc.tensor.transpose(ps[:, o, tt * P:tt * P + P], src, k.ident)
                ins.then_inc(*turned.up())


def weight_stage(k):
    nc, ps = k.nc, k.ps
    first_made, scaled, second_made = k.start("first_hot_made", "first_hot_scaled", "second_hot_made")
    spread, folded = k.start("weights_spread", "coef_made")
    Q, A, B = 4, 4, 2
    groups, body, ahead = S // Q, 4, 2
    turns = groups // body
    first, second = k.first_hot, k.second_hot
    iota = k.c("iota")

    def choice(o, i, g, q, n):
        t = i * (body * Q) + (g * Q + q)
        return k.chosenT[:, o, t:t + n] if type(i) is int else k.chosenT[:, o, bass.ds(t, n)]

    def hot(out, o, i, g):
        return nc.vector.tensor_tensor(out, iota.unsqueeze(1).broadcast_to([P, Q, NKEY]),
                                       choice(o, i, g, 0, Q).unsqueeze(2).broadcast_to([P, Q, NKEY]), ALU.is_equal)

    def over_groups(engine, one_turn):
        one_turn(0)
        with engine.Fori(1, turns - 1) as i:
            one_turn(i)
        one_turn(turns - 1)

    with nc.Block() as block:

        @block.vector
        def _(dve):
            def make(i, g):
                if type(i) is not int or i * body + g >= A:
                    dve.wait_ge(spread.sem, i * body + (spread.base + g - A + 1))
                hot(first[:, g % A], 0, i, g).then_inc(first_made.sem, 1)
                if type(i) is not int or i * body + g >= B:
                    dve.wait_ge(spread.sem, i * body + (spread.base + g - B + 1))
                hot(second[:, g % B], 1, i, g).then_inc(second_made.sem, 1)

            def fold(i, g):
                t = i * (body * Q) + g * Q
                c = k.coef[:, :, t:t + Q] if type(i) is int else k.coef[:, :, bass.ds(t, Q)]
                c = c.rearrange("p j t -> p t j")
                dve.wait_ge(spread.sem, i * body + (spread.base + g + 1))
                nc.vector.tensor_tensor(c, ps[:, g, :].rearrange("p (t j) -> p t j", t=Q), c,
                                        ALU.mult).then_inc(folded.sem, 1)

            def one_turn(i):
                for g in range(body):
                    if type(i) is not int or i * body + g + ahead < groups:
                        make(i, g + ahead)
                    fold(i, g)
            for g in range(ahead):
                make(0, g)
            over_groups(dve, one_turn)

        @block.scalar
        def _(act):
            def one_turn(i):
                for g in range(body):
                    act.wait_ge(first_made.sem, i * body + (first_made.base + g + 1))
                    for q in range(Q):
                        nc.scalar.activation(first[:, g % A, q, :], first[:, g % A, q, :], ACT.Copy,
                                             scale=choice(2, i, g, q, 1)).then_inc(scaled.sem, 1)
            over_groups(act, one_turn)

        @block.tensor
        def _(pe):
            def one_turn(i):
                for g in range(body):
                    pe.wait_ge(scaled.sem, i * (Q * body) + (scaled.base + Q * (g + 1)))
                    pe.wait_ge(second_made.sem, i * body + (second_made.base + g + 1))
                    if type(i) is not int or i:
                        pe.wait_ge(folded.sem, i * body + (folded.base + g - body + 1))
                    for q in range(Q):
                        ins = nc.tensor.matmul(ps[:, g, q * P:(q + 1) * P], first[:, g % A, q, :],
                                               second[:, g % B, q, :], start=True, stop=True)
                    ins.then_inc(spread.sem, 1)
            over_groups(pe, one_turn)
    first_made.total += groups
    second_made.total += groups
    scaled.total += S
    spread.total += groups
    folded.total += groups


STAGES = 8


def experts_out_stage(k):
    nc, ps = k.nc, k.ps
    first = k.tiles["v"]
    staged, added = k.start("coef_staged", "experts_added")
    ring, src = k.ring, k.dram["peer_v"]
    used = ring.used
    rounds = NKEY // BODY
    s = k.split[first]
    low_made, low0 = k.low_made["vector"], k.low_nth[first][1] - 1
    assert k.loaded == first + RING and used.total == first
    stage, stage_low = k.stage, k.stage_low
    staged_low, = k.start("coef_low_staged")
    c_of = lambda i, j: k.coef[:, j, :] if type(i) is int else \
        k.coef[:, bass.ds(i * BODY + j, 1), :].rearrange("p a t -> p (a t)")
    with nc.Block() as block:

        @block.sync
        def _(sp):
            for j in range(RING, BODY):
                fori_load(sp, k, first, src, 0, j)
            with sp.Fori(1, rounds) as i:
                for j in range(BODY):
                    fori_load(sp, k, first, src, i, j)
            k.loaded = first + NKEY
            load_tiles(sp, k, k.loaded + RING)

        @block.scalar
        def _(act):
            def one_round(i):
                for j in range(BODY):
                    if type(i) is not int or j >= STAGES:
                        act.wait_ge(used.sem, i * BODY + (first + j - STAGES + 1))
                    nc.scalar.activation(stage[:, j % STAGES, :], c_of(i, j), ACT.Copy).then_inc(staged.sem, 1)
                    fori_high(act, k, first, i, j)
            one_round(0)
            with act.Fori(1, rounds) as i:
                one_round(i)

        @block.tensor
        def _(pe):
            def one_round(i, head=False, tail=False):
                for j in range(BODY):
                    high, low = parts(k, first + j, 2)
                    pe.wait_ge(k.high_made.sem, i * BODY + (s + j + 1))
                    pe.wait_ge(staged.sem, i * BODY + (staged.base + j + 1))
                    for part, (c, v) in enumerate(((stage, high), (stage_low, high), (stage, low))):
                        if part == 1:
                            pe.wait_ge(staged_low.sem, i * BODY + (staged_low.base + j + 1))
                        if part == 2:
                            pe.wait_ge(low_made.sem, i * BODY + (low0 + j + 1))
                        for tt in range(NT):
                            for half in range(2):
                                ins = nc.tensor.matmul(ps[:, 2 * tt + half, :], c[:, j % STAGES, tt * P:tt * P + P],
                                                       v[:, half, :], start=head and j + part == 0,
                                                       stop=tail and j == BODY - 1 and part == 2,
                                                       skip_group_check=True)
                        if part == 1:
                            ins.then_inc(k.high_used.sem, 1)
                    ins.then_inc(used.sem, 1)
            one_round(0, head=True)
            with pe.Fori(1, rounds - 1) as i:
                one_round(i)
            one_round(rounds - 1, tail=True)

        @block.vector
        def _(dve):
            def one_round(i):
                for j in range(BODY):
                    dve.wait_ge(staged.sem, i * BODY + (staged.base + j + 1))
                    nc.vector.tensor_tensor(stage_low[:, j % STAGES, :], c_of(i, j), stage[:, j % STAGES, :].bitcast(F32),
                                            ALU.subtract).then_inc(staged_low.sem, 1)
                    fori_low(dve, k, first, i, j)
            one_round(0)
            with dve.Fori(1, rounds) as i:
                one_round(i)
            dve.wait_ge(used.sem, first + NKEY)
            for tt in range(NT):
                h = k.h[:, tt, :]
                nc.vector.tensor_tensor(h, h, ps[:, 2 * tt:2 * tt + 2, :].rearrange("p b n -> p (b n)"),
                                        ALU.add).then_inc(*added.up())
    after_fori(k)
    used.total += NKEY
    staged.total += NKEY


def peer(k, stop):
    k.prefetch = k.tiles["wq"] + RING
    k.top, k.at, k.atf, k.pos, k.part, k.partf = k.carve(
        k.mid, (2 * PH, TOPK), (2 * PH, TOPK), (2 * PH, TOPK), (PH, TOPK), (PH, TOPK), (PH, TOPK))
    k.at, k.pos, k.part = (ap.bitcast(U32) for ap in (k.at, k.pos, k.part))
    norm_stage(k, [(k.h[:, tt, :], P) for tt in range(NT)], k.p("norm_ffn"), S, "wq")
    end_early(k, "wq")
    k.qT, = k.carve(k.big, (2 * PH, S))
    project_T(k, "wq", 2 * PH, S,
              (lambda i: "vector", lambda eng, i, src: k.nc.vector.tensor_copy(k.qT[:, i, :], src)),
              k.tiles["subk"] + RING)
    k.score, = k.carve(k.big[:, (NKEY - 16) * S:NKEY * S], (NT, 2 * PH, NKEY))
    scores_stage(k)
    end_early(k, "u")
    if stop <= 6: return
    k.coef, = k.carve(k.big, (NKEY, S))
    k.best, k.chosen = k.carve(k.kept, (NT, PH, TOPK), (NT, 2, P))
    experts_in_stage(k)
    if stop <= 7: return
    k.chosenT, k.first_hot, k.second_hot = k.carve(k.spare, (3, S), (4, 4, NKEY), (2, 4, NKEY))
    choice_stage(k)
    end_early(k, "v")
    weight_stage(k)
    if stop <= 8: return
    k.stage, k.stage_low = (k.parts[:, part, 0:STAGES * S].rearrange("p (s n) -> p s n", n=S) for part in range(2))
    experts_out_stage(k)


def final_norm_stage(k):
    nc = k.nc
    landed_row, summed, vec, rooted = k.start("row_landed", "final_summed", "final_vector", "final_rooted")
    r = k.small[:, 0:12]
    k.wide, k.squares = k.carve(k.mid, (D,), (NT, D))
    with nc.Block() as block:

        @block.sync
        def _(sp):
            sp.dma_start(k.wide, k.dram["norm_final"]).then_inc(*landed_row.up(16))
            sp.dma_start(k.const2, k.dram["const_second"]).then_inc(*landed_row.up(16))
            sp.dma_start(k.hm[0:META, :], k.dram["meta"]).then_inc(*landed_row.up(16))
            sp.wait_ge(*landed_row.last())

        @block.scalar
        def _(act):
            for tt in range(NT):
                nc.scalar.activation(k.squares[:, tt, :], k.h[:, tt, :], ACT.Square,
                                     accum_out=r[:, tt:tt + 1]).then_inc(*summed.up())
            act.wait_ge(*vec.at(1))
            nc.scalar.activation(r[:, 4:6], r[:, 2:4], ACT.Sqrt).then_inc(*rooted.up())

        @block.vector
        def _(dve):
            dve.wait_ge(*summed.at(NT))
            nc.vector.tensor_scalar(r[:, 2:4], r[:, 0:2], 1.0 / D, EPS, ALU.mult, ALU.add).then_inc(*vec.up())
            dve.wait_ge(*rooted.at(1))
            newton(nc, dve, vec, r[:, 2:4], r[:, 4:6], r[:, 6:8], r[:, 8:10])
            dve.wait_ge(*landed_row.at(48))
            for tt in range(NT):
                nc.vector.scalar_tensor_tensor(k.h[:, tt, :], k.h[:, tt, :], r[:, 6 + tt:7 + tt], k.wide,
                                               ALU.mult, ALU.mult).then_inc(*vec.up())


def newton(nc, dve, sig, y, root, inv, step):
    nc.vector.reciprocal(inv, root).then_inc(*sig.up())
    dve.wait_ge(*sig.last())
    nc.vector.tensor_tensor(step, inv, inv, ALU.mult).then_inc(*sig.up())
    dve.wait_ge(*sig.last())
    nc.vector.tensor_tensor(step, step, y, ALU.mult).then_inc(*sig.up())
    dve.wait_ge(*sig.last())
    nc.vector.tensor_scalar(step, step, -0.5, 1.5, ALU.mult, ALU.add).then_inc(*sig.up())
    dve.wait_ge(*sig.last())
    nc.vector.tensor_tensor(inv, inv, step, ALU.mult).then_inc(*sig.up())
    dve.wait_ge(*sig.last())


def head_norm_stage(k, chunks, heads, gather, spread, scale, eps, finish):
    nc, ps, xs = k.nc, k.ps, chunks
    n = len(xs)
    squared, summed, vec, rooted, wide, applied = k.start("head_squared", "head_summed", "head_vector",
                                                          "head_rooted", "head_spread", "head_applied")
    sq = k.squares2
    r = k.factors[0:heads]
    with nc.Block() as block:

        @block.sync
        def _(sp):
            load_tiles(sp, k, k.prefetch)

        @block.scalar
        def _(act):
            for c in range(n):
                if c >= 2:
                    act.wait_ge(*summed.at(c - 1))
                nc.scalar.activation(sq[:, c % 2, :], xs[c], ACT.Square).then_inc(*squared.up())
            act.wait_ge(*vec.at(1))
            nc.scalar.activation(r[:, 1, :], r[:, 0, :], ACT.Sqrt).then_inc(*rooted.up())

        @block.tensor
        def _(pe):
            for c in range(n):
                pe.wait_ge(*squared.at(c + 1))
                nc.tensor.matmul(ps[0:heads, 7, 0:L], gather(c), sq[:, c % 2, :], start=c == 0,
                                 stop=c == n - 1).then_inc(*summed.up())
            pe.wait_ge(*vec.at(6))
            for c in range(n):
                if c >= 7:
                    pe.wait_ge(*applied.at(c - 6))
                for lhsT, rows in spread(c):
                    ins = nc.tensor.matmul(ps[rows, c % 7, 0:L], lhsT, r[:, 2, :], start=True, stop=True)
                ins.then_inc(*wide.up())

        @block.vector
        def _(dve):
            dve.wait_ge(*summed.at(n))
            nc.vector.tensor_scalar(r[:, 0, :], ps[0:heads, 7, 0:L], scale, eps, ALU.mult,
                                    ALU.add).then_inc(*vec.up())
            dve.wait_ge(*rooted.at(1))
            newton(nc, dve, vec, r[:, 0, :], r[:, 1, :], r[:, 2, :], r[:, 3, :])
            for c in range(n):
                dve.wait_ge(*wide.at(c + 1))
                ins = list(finish(c, ps[:, c % 7, 0:L]))
                for i in ins:
                    i.then_inc(*(applied if i is ins[-1] else vec).up())


def sink_attention_stage(k):
    nc, ps, T = k.nc, k.ps, k.T2
    AK, GATE = 8, 10
    scored, masked, peaked, exped = k.start("att_scored", "att_masked", "att_peaked", "att_exped")
    scaled, turned, unturned, summed = k.start("att_scaled", "att_turned", "att_copied", "att_valued")
    stored, stats = k.start("att_stored", "att_stats")
    units = [(tt, a) for tt in range(NT) for a in range(AH // 2)]
    keys = lambda tt: META + (tt + 1) * P
    soft, pt = k.soft2, k.pt2
    st = k.small[:, 0:24].rearrange("p (s a h) -> p s a h", s=2, a=6)
    slope = [2.0 ** (-8.0 * (h + 1) / AH) for h in range(AH)]
    sinks = k.p("sinks")

    def key_tiles(tt):
        return [(0, META)] + [(META + i * P, P) for i in range(tt + 1)]

    with nc.Block() as block:

        @block.sync
        def _(sp):
            load_tiles(sp, k, k.tiles["attn_out"] + RING)

        @block.tensor
        def _(pe):
            def scores(u):
                tt, a = units[u]
                if u >= 2:
                    pe.wait_ge(*masked.at(u - 1))
                for j in range(2):
                    h = 2 * a + j
                    rows = slice(HD * j, HD * j + HD)
                    ins = nc.tensor.matmul(ps[:, 2 * (u % 2) + j, 0:keys(tt)],
                                           T[rows, a, META + tt * P:META + tt * P + P],
                                           T[rows, AK + h // 8, 0:keys(tt)], start=True, stop=True)
                ins.then_inc(*scored.up())

            def turn(u):
                tt, _ = units[u]
                pe.wait_ge(*scaled.at(u + 1))
                if u:
                    pe.wait_ge(*unturned.at(u))
                for i, (c0, n) in enumerate(key_tiles(tt)):
                    for j in range(2):
                        ins = nc.tensor.transpose(ps[0:n, 4 + i // 2, (2 * (i % 2) + j) * P:(2 * (i % 2) + j) * P + P],
                                                  soft[:, u % 3, j, c0:c0 + n], k.ident)
                ins.then_inc(*turned.up())

            def values(u):
                tt, a = units[u]
                pe.wait_ge(*unturned.at(u + 1))
                if u >= 2:
                    pe.wait_ge(*stored.at(u - 1))
                tiles = key_tiles(tt)
                for j in range(2):
                    g = (2 * a + j) // 8
                    for i, (_, n) in enumerate(tiles):
                        ins = nc.tensor.matmul(ps[HD * j:HD * j + HD, 6 + u % 2, 0:P], k.v2[0:n, i, g * HD:(g + 1) * HD],
                                               pt[0:n, u % 2, i, j, :], start=i == 0, stop=i == len(tiles) - 1)
                ins.then_inc(*summed.up())

            scores(0)
            scores(1)
            for u in range(len(units) + 1):
                if u + 2 < len(units):
                    scores(u + 2)
                if u:
                    values(u - 1)
                if u < len(units):
                    turn(u)

        @block.vector
        def _(dve):
            def peaks(u):
                tt, a = units[u]
                s, b, n = u % 2, u % 3, keys(tt)
                dve.wait_ge(*scored.at(u + 1))
                if u >= 3:
                    dve.wait_ge(*turned.at(u - 2))
                dist = k.c("dist")[:, L * tt:L * tt + n]
                for j in range(2):
                    nc.vector.scalar_tensor_tensor(soft[:, b, j, 0:n], dist, -slope[2 * a + j],
                                                   ps[:, 2 * s + j, 0:n], ALU.mult,
                                                   ALU.add).then_inc(*(masked if j else stats).up())
                dve.wait_ge(*masked.last())
                dve.wait_ge(*stats.last())
                nc.vector.tensor_reduce(st[:, s, 0, :], soft[:, b, :, 0:n], AX.X, ALU.max).then_inc(*stats.up())
                dve.wait_ge(*stats.last())
                nc.vector.tensor_tensor(st[:, s, 0, :], st[:, s, 0, :], sinks[:, 2 * a:2 * a + 2],
                                        ALU.max).then_inc(*stats.up())
                dve.wait_ge(*stats.last())
                nc.vector.tensor_tensor(st[:, s, 3, :], sinks[:, 2 * a:2 * a + 2], st[:, s, 0, :],
                                        ALU.subtract).then_inc(*stats.up())
                dve.wait_ge(*stats.last())
                nc.vector.tensor_scalar(st[:, s, 1, :], st[:, s, 0, :], -1.0, None, ALU.mult).then_inc(*peaked.up())

            def scale(u):
                tt, a = units[u]
                s, b, n = u % 2, u % 3, keys(tt)
                dve.wait_ge(*exped.at(3 * (u + 1)))
                nc.vector.tensor_tensor(st[:, s, 2, :], st[:, s, 2, :], st[:, s, 3, :], ALU.add).then_inc(*stats.up())
                dve.wait_ge(*stats.last())
                nc.vector.reciprocal(st[:, s, 4, :], st[:, s, 2, :]).then_inc(*stats.up())
                dve.wait_ge(*stats.last())
                for j in range(2):
                    nc.vector.tensor_scalar(soft[:, b, j, 0:n], soft[:, b, j, 0:n], st[:, s, 4, j:j + 1], None,
                                            ALU.mult).then_inc(*(scaled if j else stats).up())

            def store(u):
                tt, a = units[u]
                dve.wait_ge(*summed.at(u + 1))
                cols = slice(META + tt * P, META + tt * P + P)
                nc.vector.tensor_tensor(k.y2[:, a, cols], ps[:, 6 + u % 2, 0:P], T[:, GATE + a, cols],
                                        ALU.mult).then_inc(*stored.up())

            for u in range(len(units) + 3):
                if u < len(units):
                    peaks(u)
                if 1 <= u <= len(units):
                    scale(u - 1)
                if u == 2:
                    for n in early(k, "attn_out"):
                        make_low(dve, k, n)
                if u >= 3:
                    store(u - 3)

        @block.scalar
        def _(act):
            def exps(u):
                tt, _ = units[u]
                s = u % 2
                act.wait_ge(*peaked.at(u + 1))
                nc.scalar.activation(st[:, s, 3, :], st[:, s, 3, :], ACT.Exp).then_inc(*exped.up())
                for j in range(2):
                    p = soft[:, u % 3, j, 0:keys(tt)]
                    nc.scalar.activation(p, p, ACT.Exp, bias=st[:, s, 1, j:j + 1],
                                         accum_out=st[:, s, 2, j:j + 1]).then_inc(*exped.up())

            def copy_turned(u):
                tt, _ = units[u]
                act.wait_ge(*turned.at(u + 1))
                if u >= 2:
                    act.wait_ge(*summed.at(u - 1))
                nc.scalar.activation(pt[0:META, u % 2, 0, :, :].rearrange("p j n -> p (j n)"), ps[0:META, 4, 0:2 * P],
                                     ACT.Copy).then_inc(*stats2.up())
                act.wait_ge(*stats2.last())
                nc.scalar.activation(pt[:, u % 2, 1:2 + tt, :, :].rearrange("p i j n -> p (i j n)"),
                                     k.flat[:, 4 * 512 + 2 * P:4 * 512 + (4 + 2 * tt) * P],
                                     ACT.Copy).then_inc(*unturned.up())

            stats2, = k.start("att_meta_copied")
            for u in range(len(units) + 1):
                if u < len(units):
                    exps(u)
                if u:
                    copy_turned(u - 1)
                if u == 2:
                    for n in early(k, "attn_out"):
                        make_high(act, k, n)


def meta_attention_stage(k):
    nc, ps, T = k.nc, k.ps, k.T2
    AK, GATE = 8, 10
    pe_done, vec, exped = k.start("meta_product", "meta_vector", "meta_exped")
    m = META
    k.meta_soft, k.meta_turned = k.carve(k.mid, (AH, META), (AH, META))
    soft, turned = k.meta_soft[0:m], k.meta_turned[0:m]
    st = k.small[0:m, 24:24 + 4 * AH].rearrange("p (a h) -> p a h", a=4)
    wide = lambda ap: ap.unsqueeze(2).broadcast_to([m, AH, m])
    with nc.Block() as block:

        @block.tensor
        def _(pe):
            for h in range(AH):
                rows = slice(HD * (h % 2), HD * (h % 2) + HD)
                ins = nc.tensor.matmul(ps[0:m, h % 2, (h // 2) * m:(h // 2) * m + m], T[rows, h // 2, 0:m],
                                       T[rows, AK + h // 8, 0:m], start=True, stop=True)
            ins.then_inc(*pe_done.up())
            pe.wait_ge(*vec.at(10))
            for h in range(AH):
                ins = nc.tensor.transpose(ps[0:m, 2, h * m:(h + 1) * m], soft[:, h, :], k.ident[0:m, 0:m])
            ins.then_inc(*pe_done.up())
            pe.wait_ge(*vec.at(11))
            for i in range(AH):
                h = 2 * (i % 8) + i // 8
                g = h // 8
                ins = nc.tensor.matmul(ps[HD * (h % 2):HD * (h % 2) + HD, 3, (h // 2) * m:(h // 2) * m + m],
                                       k.v2[0:m, 0, g * HD:(g + 1) * HD], turned[:, i, :], start=True, stop=True)
            ins.then_inc(*pe_done.up())

        @block.vector
        def _(dve):
            def done(ins):
                ins.then_inc(*vec.up())
                dve.wait_ge(*vec.last())
            sinks = k.p("sinks_placed")[0:m, :]
            dve.wait_ge(*pe_done.at(1))
            for o in range(2):
                done(nc.vector.tensor_tensor(soft[:, 8 * o:8 * o + 8, :], ps[0:m, o, 0:8 * m].rearrange("p (h n) -> p h n", h=8),
                                             k.c("meta_bias")[0:m, 8 * m * o:8 * m * (o + 1)].rearrange("p (h n) -> p h n", h=8),
                                             ALU.add))
            done(nc.vector.tensor_reduce(st[:, 0, :], soft, AX.X, ALU.max))
            done(nc.vector.tensor_tensor(st[:, 0, :], st[:, 0, :], sinks, ALU.max))
            done(nc.vector.tensor_tensor(st[:, 1, :], sinks, st[:, 0, :], ALU.subtract))
            done(nc.vector.tensor_tensor(soft, soft, wide(st[:, 0, :]), ALU.subtract))
            dve.wait_ge(*exped.at(2))
            done(nc.vector.tensor_reduce(st[:, 2, :], soft, AX.X, ALU.add))
            done(nc.vector.tensor_tensor(st[:, 2, :], st[:, 2, :], st[:, 1, :], ALU.add))
            done(nc.vector.reciprocal(st[:, 3, :], st[:, 2, :]))
            done(nc.vector.tensor_tensor(soft, soft, wide(st[:, 3, :]), ALU.mult))
            dve.wait_ge(*pe_done.at(2))
            done(nc.vector.tensor_copy(turned.rearrange("p h n -> p (h n)"), ps[0:m, 2, 0:AH * m]))
            dve.wait_ge(*pe_done.at(3))
            done(nc.vector.tensor_tensor(k.y2[:, :, 0:m], ps[:, 3, 0:8 * m].rearrange("p (c n) -> p c n", c=8),
                                         T[:, GATE:GATE + 8, 0:m], ALU.mult))

        @block.scalar
        def _(act):
            act.wait_ge(*vec.at(6))
            nc.scalar.activation(st[:, 1, :], st[:, 1, :], ACT.Exp).then_inc(*exped.up())
            nc.scalar.activation(soft, soft, ACT.Exp).then_inc(*exped.up())


def value_rows_stage(k, spans):
    nc, ps = k.nc, k.ps
    turned, copied = k.start("values_turned", "values_copied")
    with nc.Block() as block:

        @block.tensor
        def _(pe):
            for i, (c0, n) in enumerate(spans):
                nc.tensor.transpose(ps[0:n, i, 0:P], k.vT2[:, c0:c0 + n], k.ident).then_inc(*turned.up())

        @block.vector
        def _(dve):
            for i, (_, n) in enumerate(spans):
                dve.wait_ge(*turned.at(i + 1))
                nc.vector.tensor_copy(k.v2[0:n, i, :], ps[0:n, i, 0:P]).then_inc(*copied.up())


def second_block(k, stop):
    nc, ps = k.nc, k.ps
    n_const = sum(n for _, n in k.const_cols["second"][0])
    (k.const2, k.T2, k.v2, k.squares2, k.factors, k.soft2, k.pt2, k.y2, k.vT2) = k.carve(
        k.big, (n_const,), (18, L), (3, P), (2, L), (4, L), (3, 2, L), (2, 3, 2, P), (KC, L), (L,))
    k.bind("second", k.const2)
    k.flat = ps[:, :, :].rearrange("p b n -> p (b n)")
    final_norm_stage(k)
    if stop <= 21: return
    tiles = [(k.hm[0:META, :], META)] + [(k.h[:, tt, :], P) for tt in range(NT)]
    k.prefetch = k.tiles["attn_t"] + RING
    norm_stage(k, tiles, k.p("attn_norm"), L, "attn_t")
    end_early(k, "attn_t")
    V = 10

    def put(eng, i, src):
        if i <= V:
            return nc.vector.tensor_copy(k.vT2 if i == V else k.T2[:, i, :], src)
        return nc.scalar.activation(k.T2[:, i - 1, :], src, ACT.Silu)
    project_T(k, "attn_t", 19, L, (lambda i: "vector" if i <= V else "scalar", put), k.tiles["attn_out"] + RING)
    spans = [(0, META)] + [(META + tt * P, P) for tt in range(NT)]
    value_rows_stage(k, spans)
    if stop <= 22: return

    def apply_qk(c, wide):
        w = k.p("q_norm") if c < 8 else k.p("k_norm")
        yield nc.vector.scalar_tensor_tensor(k.T2[:, c, :], wide, w, k.T2[:, c, :], ALU.mult, ALU.mult)
    two = slice(0, HD), slice(HD, P)
    head_norm_stage(k, [k.T2[:, c, :] for c in range(10)], 20,
                    lambda c: k.c("pair")[:, 18 - 2 * c:38 - 2 * c],
                    lambda c: [(k.ident[0:20, 2 * c + o:2 * c + o + 1].broadcast_to([20, HD]), two[o]) for o in range(2)],
                    8.0 / HD, 8.0 * EPS, apply_qk)
    if stop <= 23: return
    meta_attention_stage(k)
    sink_attention_stage(k)
    end_early(k, "attn_out")
    if stop <= 24: return
    out_rows(k, "attn_out", [(k.hm, 0, META, 0)] + [(k.h[:, tt, :], 2 + 2 * tt, P, META + tt * P) for tt in range(NT)],
             k.y2, k.tiles["dn_qkv"] + RING)
    if stop <= 25: return
    deltanet(k, tiles, stop)


def conv_stage(k):
    nc, ps = k.nc, k.ps
    first = k.tiles["dn_qkv"]
    n = 2 * DNK + DNV
    conv, chain, silu, cleared = k.start("conv_done", "conv_chain", "conv_silu", "pads_cleared")
    silu2, = k.start("conv_silu_meta")
    high, low = k.pair(L)
    taps = k.p("conv").rearrange("p (c s) -> p c s", s=4)
    acc = k.squares2
    with nc.Block() as block:

        @block.sync
        def _(sp):
            load_tiles(sp, k, k.tiles["dn_ba"] + RING)

        @block.gpsimd
        def _(pool):
            for ap in (k.vT[:, :, 0, :, 0:PAD], k.kT[:, :, 0, :, 0:PAD], k.dq[:, :, 0, 0:PAD], k.state):
                nc.gpsimd.memset(ap, 0.0).then_inc(*cleared.up())
            for i in range(n):
                if k.low_nth[first + i][0] == "gpsimd":
                    make_low(pool, k, first + i)
            pool.wait_ge(*cleared.last())

        @block.tensor
        def _(pe):
            for i in range(n):
                if i >= 8:
                    pe.wait_ge(*conv.at(i - 7))
                tile_T(pe, k, first + i, ps[:, i % 8, 0:L], lambda c: (high[:, c, :], low[:, c, :]))

        @block.vector
        def _(dve):
            for i in range(-AHEAD, n):
                if i + AHEAD < n and k.low_nth[first + i + AHEAD][0] == "vector":
                    make_low(dve, k, first + i + AHEAD)
                if i < 0:
                    continue
                dve.wait_ge(k.ring.used.sem, first + i + 1)
                if i >= 2:
                    dve.wait_ge(*silu.at(i - 1))
                x, y = ps[:, i % 8, 0:L], acc[:, i % 2, :]
                nc.vector.tensor_scalar(y, x, taps[:, i, 3:4], None, ALU.mult).then_inc(*chain.up())
                for s in range(1, 4):
                    dve.wait_ge(*chain.last())
                    nc.vector.scalar_tensor_tensor(y[:, s:L], x[:, 0:L - s], taps[:, i, 3 - s:4 - s], y[:, s:L],
                                                   ALU.mult, ALU.add).then_inc(*(conv if s == 3 else chain).up())

        @block.scalar
        def _(act):
            for i in range(-AHEAD, n):
                if i + AHEAD < n:
                    make_high(act, k, first + i + AHEAD)
                if i < 0:
                    continue
                act.wait_ge(*conv.at(i + 1))
                y = acc[:, i % 2, :]
                if i < 2 * DNK:
                    nc.scalar.activation(k.qk[:, i, :], y, ACT.Silu).then_inc(*silu.up())
                else:
                    h = i - 2 * DNK
                    v = k.vT[:, h // 2, :, h % 2, :]
                    nc.scalar.activation(v[:, 0, PAD:CH], y[:, 0:META], ACT.Silu).then_inc(*silu2.up())
                    nc.scalar.activation(v[:, 1:NCH, :], y[:, META:L].rearrange("p (c s) -> p c s", c=NCH - 1),
                                         ACT.Silu).then_inc(*silu.up())


def delta_gates_stage(k):
    nc, ps = k.nc, k.ps
    vec, acted, made, clear = k.start("gate_vector", "gate_act", "gate_product", "gate_cleared")
    b, a = slice(0, 16), slice(32, 48)
    sp, ba = k.soft_plus, k.ba
    dup = k.dup
    n = NCH * DNK
    col = lambda ap: ap.rearrange("p (c i) -> p c i", c=NCH)
    with nc.Block() as block:

        @block.sync
        def _(sync):
            load_tiles(sync, k, k.prefetch)

        @block.gpsimd
        def _(pool):
            nc.gpsimd.memset(dup[0:48], 0.0).then_inc(*clear.up())

        @block.scalar
        def _(act):
            nc.scalar.activation(ba[b, :], ba[b, :], ACT.Sigmoid).then_inc(*acted.up())
            nc.scalar.activation(k.small[a, 0:1], k.p("a_log")[a, :], ACT.Exp).then_inc(*acted.up())
            act.wait_ge(*vec.at(2))
            nc.scalar.activation(sp[a, 1, :], sp[a, 1, :], ACT.Exp).then_inc(*acted.up())
            act.wait_ge(*acted.last())
            nc.scalar.activation(sp[a, 1, :], sp[a, 1, :], ACT.Ln, bias=1.0).then_inc(*acted.up())
            act.wait_ge(*vec.at(14))
            nc.scalar.activation(k.eG, k.G, ACT.Exp).then_inc(*acted.up())
            nc.scalar.activation(k.eGL, k.eGL, ACT.Exp).then_inc(*acted.up())
            nc.scalar.activation(k.egl, ps[:, 2, 0:2 * n], ACT.Exp).then_inc(*acted.up())

        @block.vector
        def _(dve):
            def done(ins):
                ins.then_inc(*vec.up())
                dve.wait_ge(*vec.last())
            done(nc.vector.tensor_scalar(sp[a, 0, :], ba[a, :], k.p("dt_bias")[a, :], None, ALU.add))
            done(nc.vector.scalar_tensor_tensor(sp[a, 1, :], sp[a, 0, :], -1.0, sp[a, 0, :], ALU.mult, ALU.min))
            dve.wait_ge(*acted.at(4))
            done(nc.vector.scalar_tensor_tensor(sp[a, 0, :], sp[a, 0, :], 0.0, sp[a, 1, :], ALU.max, ALU.add))
            done(nc.vector.tensor_scalar(ba[a, :], sp[a, 0, :], k.small[a, 0:1], -1.0, ALU.mult, ALU.mult))
            dve.wait_ge(*clear.at(1))
            done(nc.vector.tensor_copy(dup[0:48, 0, :, PAD:CH], ba[0:48, 0:META].unsqueeze(1).broadcast_to([48, 2, META])))
            done(nc.vector.tensor_copy(dup[0:48, 1:NCH], ba[0:48, META:L].rearrange("p (c s) -> p c s", c=NCH - 1)
                                       .unsqueeze(2).broadcast_to([48, NCH - 1, 2, CH])))
            dve.wait_ge(*made.at(1))
            turned = ps[:, 0, 0:48 * NCH].rearrange("p (c r) -> p c r", c=NCH)
            for j, (dst, c0) in enumerate(((k.beta, 0), (k.g, 32))):
                for o in range(2):
                    rows = slice(CH * o, CH * o + CH)
                    done(nc.vector.tensor_copy(col(dst)[rows], turned[rows, :, c0 + 8 * o:c0 + 8 * o + 8]))
            for o in range(2):
                done(nc.vector.tensor_scalar(k.gm[:, n * o:n * (o + 1)], k.g, k.c("half")[:, o:o + 1], None, ALU.mult))
            dve.wait_ge(*made.at(2))
            done(nc.vector.tensor_copy(k.G, ps[:, 1, 0:n]))
            done(nc.vector.tensor_tensor(k.eGL, ps[:, 1, n:2 * n], k.G, ALU.subtract))
            done(nc.vector.tensor_scalar(k.negG, k.G, -1.0, None, ALU.mult))
            dve.wait_ge(*acted.at(7))
            done(nc.vector.tensor_tensor(k.be, k.beta, k.eG, ALU.mult))

        @block.tensor
        def _(pe):
            pe.wait_ge(*vec.at(6))
            pe.wait_ge(*acted.at(1))
            for c in range(NCH):
                ins = nc.tensor.transpose(ps[:, 0, 48 * c:48 * c + 48], dup[0:48, c].rearrange("p o s -> p (o s)"),
                                          k.ident[0:48, 0:48])
            ins.then_inc(*made.up())
            pe.wait_ge(*vec.at(12))
            nc.tensor.matmul(ps[:, 1, 0:n], k.c("upper"), k.g, start=True, stop=True)
            nc.tensor.matmul(ps[:, 1, n:2 * n], k.c("block"), k.g, start=True, stop=True)
            nc.tensor.matmul(ps[:, 2, 0:2 * n], k.c("ones"), k.gm, start=True, stop=True).then_inc(*made.up())


def levels(c):
    return int(np.ceil(np.log2(META if c == 0 else CH))) - 1


def delta_stage(k):
    nc, ps = k.nc, k.ps
    gr, kk, kq, kr, vr, mt = k.start("d_sums", "d_kk", "d_kq", "d_krows", "d_vrows", "d_turned")
    power, grown, us, ws = k.start("d_power", "d_product", "d_u", "d_w")
    masked, m_done, attn, krows, vrows = k.start("d_masked", "d_m", "d_attn", "d_kscaled", "d_vscaled")
    rinit, ptaken, rtaken, decay, mtaken = k.start("d_rinit", "d_ptaken", "d_rtaken", "d_decay", "d_mtaken")
    p2taken, utaken, wtaken = k.start("d_p2taken", "d_utaken", "d_wtaken")
    old, inter, intra, grow_s, oturn = k.start("d_old", "d_inter", "d_intra", "d_state", "d_oturned")
    vnew, oscaled, summed, state, squared = k.start("d_vnew", "d_oscaled", "d_osum", "d_state_new", "d_squared")
    rooted, normed, stored, chain, mean = k.start("d_rooted", "d_normed", "d_stored", "d_chain", "d_mean")
    H = 4
    half = lambda ap, b: ap[:, H * b:H * b + H, :]
    flat = lambda ap: ap.rearrange("p i n -> p (i n)")
    bank = lambda b, n=1: k.flat[:, 512 * b:512 * (b + n)]
    quad = lambda b: ps[:, b, :].rearrange("p (i n) -> p i n", i=H)
    wide = lambda ap: ap.unsqueeze(2).broadcast_to([P, H, P])
    kT = lambda c, i: k.kT[:, i, c].rearrange("p o s -> p (o s)")
    vT = lambda c, i: k.vT[:, i, c].rearrange("p o s -> p (o s)")
    at = lambda c, i: DNK * c + i
    low, up_ = k.c("low"), k.c("up")
    lvl = lambda c, l, b: 2 * sum(levels(a) for a in range(c)) + 2 * (l - 1) + b + 1
    lvl4 = lambda c, l, b: 2 * sum(levels(a) - 1 for a in range(c)) + 2 * (l - 1) + b + 1
    st = k.small[:, 8:48].rearrange("p (a i) -> p a i", a=5)
    with nc.Block() as block:

        @block.sync
        def _(sp):
            load_tiles(sp, k, k.prefetch)

        @block.tensor
        def _(pe):
            def turn_out(c):
                pe.wait_ge(*normed.at(c))
                for i in range(DNK):
                    ins = nc.tensor.transpose(ps[:, 6 + i // H, (i % H) * P:(i % H) * P + P], k.o1[:, i, :], k.ident)
                ins.then_inc(*oturn.up())

            def key_products(n):
                c, b = n // 2, n % 2
                for i in range(H):
                    ins = nc.tensor.matmul(quad(1)[:, i, :], kT(c, H * b + i), kT(c, H * b + i), start=True, stop=True)
                ins.then_inc(*kk.up())

            for c in range(NCH):
                if c:
                    pe.wait_ge(*summed.at(c))
                for b in range(2):
                    n = 2 * c + b
                    if b:
                        pe.wait_ge(*masked.at(n))
                    for i in range(H):
                        g = k.g[:, at(c, H * b + i):at(c, H * b + i) + 1].broadcast_to([P, P])
                        ins = nc.tensor.matmul(quad(0)[:, i, :], g, k.c("upper"), start=True, stop=True)
                    ins.then_inc(*gr.up())
                    if b == 0:
                        key_products(n)
                        if c:
                            pe.wait_ge(*state.at(16 * c))
                    if b:
                        pe.wait_ge(*krows.at(n))
                    for i in range(H):
                        ins = nc.tensor.transpose(quad(3)[:, i, :], kT(c, H * b + i), k.ident)
                    ins.then_inc(*kr.up())
                    if b:
                        pe.wait_ge(*vrows.at(n))
                    for i in range(H):
                        ins = nc.tensor.transpose(quad(4)[:, i, :], vT(c, H * b + i), k.ident)
                    ins.then_inc(*vr.up())
                    if b:
                        pe.wait_ge(*m_done.at(n))
                        key_products(n)
                    if b:
                        pe.wait_ge(*attn.at(n))
                    for i in range(H):
                        q = k.dq[:, H * b + i, c, :].unsqueeze(1).broadcast_to([P, 2, CH])
                        ins = nc.tensor.matmul(quad(2)[:, i, :].rearrange("p (o s) -> p o s", o=2), kT(c, H * b + i), q,
                                               start=True, stop=True)
                    ins.then_inc(*kq.up())
                for b in range(2):
                    n = 2 * c + b
                    pe.wait_ge(*m_done.at(n + 1))
                    if c > 1:
                        pe.wait_ge(*oscaled.at(8 * (c - 1)))
                    for i in range(H):
                        ins = nc.tensor.transpose(quad(6 + b)[:, i, :], half(k.pw, b)[:, i, :], k.ident)
                    ins.then_inc(*mt.up())
                pe.wait_ge(*attn.at(2 * c + 2))
                pe.wait_ge(*krows.at(2 * c + 2))
                pe.wait_ge(*vrows.at(2 * c + 2))
                for l in range(1, levels(c) + 1):
                    if l == 3 and c > 1:
                        turn_out(c - 1)
                    for b in range(2):
                        n = 2 * c + b
                        if l == 1:
                            pe.wait_ge(*mtaken.at(n + 1))
                        else:
                            pe.wait_ge(*ptaken.at(lvl(c, l - 1, b)))
                            pe.wait_ge(*p2taken.at(lvl4(c, l - 1, b)))
                        for i in range(H):
                            m, t = half(k.pw, b)[:, i, :], half(k.pwT, b)[:, i, :]
                            ins = nc.tensor.matmul(quad(b)[:, i, :], t, m, start=True, stop=True)
                            if l < levels(c):
                                ins = nc.tensor.matmul(quad(2 + b)[:, i, :], m, t, start=True, stop=True)
                        ins.then_inc(*power.up())
                    for b in range(2):
                        pe.wait_ge(*ptaken.at(lvl(c, l, b)))
                        pe.wait_ge(*rinit.at(2 * c + b + 1))
                        if l > 1:
                            pe.wait_ge(*rtaken.at(lvl(c, l - 1, b)))
                        for i in range(H):
                            ins = nc.tensor.matmul(quad(4 + b)[:, i, :], half(k.pw, b)[:, i, :], half(k.R, b)[:, i, :],
                                                   start=True, stop=True)
                        ins.then_inc(*grown.up())
                for b in range(2):
                    pe.wait_ge(*rtaken.at(lvl(c, levels(c), b)))
                    for i in range(H):
                        ins = nc.tensor.matmul(quad(b)[:, i, :], half(k.R, b)[:, i, :], half(k.vb, b)[:, i, :], start=True, stop=True)
                    ins.then_inc(*us.up())
                    for i in range(H):
                        ins = nc.tensor.matmul(quad(2 + b)[:, i, :], half(k.kbg, b)[:, i, :], half(k.R, b)[:, i, :], start=True, stop=True)
                    ins.then_inc(*ws.up())
                if c:
                    pe.wait_ge(*wtaken.at(2 * c + 2))
                    if c > 1:
                        pe.wait_ge(*stored.at(2 * (c - 1)))
                    for dst, lhs, sig in ((4, lambda i, o: k.wT[:, i, CH * o:CH * o + CH], old),
                                          (6, lambda i, o: k.dq[:, i, c, :], inter)):
                        for i in range(DNK):
                            for o in range(2):
                                ins = nc.tensor.matmul(ps[CH * o:CH * o + CH, dst + i // H, (i % H) * P:(i % H) * P + P],
                                                       lhs(i, o), k.state[:, 2 * i + o, :], start=True, stop=True)
                        ins.then_inc(*sig.up())
                pe.wait_ge(*vnew.at(c + 1))
                pe.wait_ge(*wtaken.at(2 * c + 2))
                for i in range(DNK):
                    ins = nc.tensor.matmul(ps[:, i // H, (i % H) * P:(i % H) * P + P], k.attnT[:, i, :], k.vn[:, i, :],
                                           start=True, stop=True)
                ins.then_inc(*intra.up())
                for i in range(DNK):
                    for o in range(2):
                        rows = slice(CH * o, CH * o + CH)
                        ins = nc.tensor.matmul(ps[:, 2 + 2 * o + i // H, (i % H) * P:(i % H) * P + P],
                                               k.kst[rows, i, :], k.vn[rows, i, :], start=True, stop=True)
                ins.then_inc(*grow_s.up())
            turn_out(NCH - 1)

        @block.vector
        def _(dve):
            def take_mean(c):
                dve.wait_ge(*squared.at(8 * c))
                nc.vector.tensor_scalar(st[:, 1, :], st[:, 0, :], 1.0 / P, EPS, ALU.mult, ALU.add).then_inc(*mean.up())

            def norm_out(c):
                dve.wait_ge(*rooted.at(c))
                newton(nc, dve, chain, st[:, 1, :], st[:, 2, :], st[:, 3, :], st[:, 4, :])
                nc.vector.tensor_tensor(k.o1, k.o1, st[:, 3, :].unsqueeze(2).broadcast_to([P, DNK, P]),
                                        ALU.mult).then_inc(*normed.up())

            def store_out(c):
                dve.wait_ge(*oturn.at(c))
                for b in range(2):
                    cols = slice(META + CH * (c - 1), META + CH * c)
                    heads = slice(2 * H * b, 2 * H * (b + 1))
                    nc.vector.scalar_tensor_tensor(k.dy[:, heads, CH * (c - 1):CH * c],
                                                   bank(6 + b).rearrange("p (h s) -> p h s", s=CH), k.p("o_norm"),
                                                   k.z[:, heads, cols], ALU.mult, ALU.mult).then_inc(*stored.up())

            for c in range(NCH):
                def mask(b):
                    n = 2 * c + b
                    dve.wait_ge(*gr.at(n + 1))
                    nc.vector.tensor_tensor(half(k.E, b), quad(0), low.unsqueeze(1).broadcast_to([P, H, P]),
                                            ALU.subtract).then_inc(*chain.up())
                    nc.vector.tensor_tensor(half(k.ET, b), quad(0), up_.unsqueeze(1).broadcast_to([P, H, P]),
                                            ALU.add).then_inc(*masked.up())

                def rows(b):
                    n = 2 * c + b
                    cols = lambda ap: wide(ap[:, at(c, H * b):at(c, H * b) + H])
                    dve.wait_ge(*kr.at(n + 1))
                    nc.vector.tensor_tensor(half(k.kbg, b), quad(3), cols(k.be), ALU.mult).then_inc(*chain.up())
                    nc.vector.tensor_tensor(half(k.kst, b), quad(3), cols(k.eGL), ALU.mult).then_inc(*krows.up())
                    dve.wait_ge(*vr.at(n + 1))
                    nc.vector.tensor_tensor(half(k.vb, b), quad(4), cols(k.beta), ALU.mult).then_inc(*vrows.up())

                def products(b):
                    n = 2 * c + b
                    dve.wait_ge(*decay.at(8 * (n + 1)))
                    dve.wait_ge(*kk.at(n + 1))
                    for i in range(H):
                        j = at(c, H * b + i)
                        nc.vector.scalar_tensor_tensor(half(k.pw, b)[:, i, :], quad(1)[:, i, :], k.beta[:, j:j + 1],
                                                       half(k.E, b)[:, i, :], ALU.mult,
                                                       ALU.mult).then_inc(*(m_done if i == H - 1 else chain).up())
                    dve.wait_ge(*kq.at(n + 1))
                    nc.vector.tensor_tensor(half(k.attnT, b), quad(2), half(k.ET, b), ALU.mult).then_inc(*attn.up())
                    dve.wait_ge(*chain.last())

                if c:
                    dve.wait_ge(*grow_s.at(c))
                mask(0)
                rows(0)
                mask(1)
                rows(1)
                products(0)
                products(1)
                for b in range(2):
                    dve.wait_ge(*mtaken.at(2 * c + b + 1))
                    nc.vector.scalar_tensor_tensor(half(k.R, b), half(k.pwT, b), -1.0, k.ident.unsqueeze(1).broadcast_to([P, H, P]),
                                                   ALU.mult, ALU.add).then_inc(*rinit.up())
                if c > 1:
                    take_mean(c - 1)
                for l in range(1, levels(c) + 1):
                    if c > 1 and l == 2:
                        norm_out(c - 1)
                    if c > 1 and l == 4:
                        store_out(c - 1)
                    for b in range(2):
                        if l < levels(c):
                            dve.wait_ge(*power.at(lvl(c, l, b)))
                            dve.wait_ge(*rinit.at(2 * c + b + 1))
                            nc.vector.tensor_copy(flat(half(k.pwT, b)), bank(2 + b)).then_inc(*p2taken.up())
                    for b in range(2):
                        dve.wait_ge(*grown.at(lvl(c, l, b)))
                        if l == 1:
                            dve.wait_ge(*rinit.at(2 * c + b + 1))
                        else:
                            dve.wait_ge(*rtaken.at(lvl(c, l - 1, b)))
                        nc.vector.tensor_tensor(half(k.R, b), half(k.R, b), quad(4 + b), ALU.add).then_inc(*rtaken.up())
                dve.wait_ge(*utaken.at(2 * c + 2))
                if c:
                    dve.wait_ge(*old.at(c))
                    nc.vector.tensor_tensor(flat(k.vn), flat(k.u), bank(4, 2), ALU.subtract).then_inc(*vnew.up())
                else:
                    nc.vector.tensor_copy(flat(k.vn), flat(k.u)).then_inc(*vnew.up())
                dve.wait_ge(*intra.at(c + 1))
                if c:
                    dve.wait_ge(*oscaled.at(8 * c))
                    nc.vector.tensor_tensor(flat(k.o1), flat(k.o1), bank(0, 2), ALU.add).then_inc(*summed.up())
                else:
                    nc.vector.tensor_copy(k.small[:, 0:1], bank(0, 2)[:, 0:1]).then_inc(*summed.up())
                dve.wait_ge(*grow_s.at(c + 1))
                for i in range(DNK):
                    for o in range(2):
                        j = NCH * DNK * o + at(c, i)
                        nc.vector.scalar_tensor_tensor(k.state[:, 2 * i + o, :], k.state[:, 2 * i + o, :], k.egl[:, j:j + 1],
                                                       ps[:, 2 + 2 * o + i // H, (i % H) * P:(i % H) * P + P],
                                                       ALU.mult, ALU.add).then_inc(*state.up())
            take_mean(NCH - 1)
            norm_out(NCH - 1)
            store_out(NCH - 1)

        @block.scalar
        def _(act):
            def root(c):
                act.wait_ge(*mean.at(c))
                nc.scalar.activation(st[:, 2, :], st[:, 1, :], ACT.Sqrt).then_inc(*rooted.up())

            for c in range(NCH):
                for b in range(2):
                    act.wait_ge(*masked.at(2 * c + b + 1))
                    for i in range(H):
                        j = at(c, H * b + i)
                        e, t = half(k.E, b)[:, i, :], half(k.ET, b)[:, i, :]
                        nc.scalar.activation(e, e, ACT.Exp, bias=k.G[:, j:j + 1], scale=-1.0).then_inc(*decay.up())
                        nc.scalar.activation(t, t, ACT.Exp, bias=k.negG[:, j:j + 1]).then_inc(*decay.up())
                for b in range(2):
                    act.wait_ge(*mt.at(2 * c + b + 1))
                    nc.scalar.activation(flat(half(k.pwT, b)), bank(6 + b), ACT.Copy).then_inc(*mtaken.up())
                for l in range(1, levels(c) + 1):
                    if c > 1 and l == 2:
                        root(c - 1)
                    for b in range(2):
                        act.wait_ge(*power.at(lvl(c, l, b)))
                        nc.scalar.activation(flat(half(k.pw, b)), bank(b), ACT.Copy).then_inc(*ptaken.up())
                for b in range(2):
                    act.wait_ge(*us.at(2 * c + b + 1))
                    nc.scalar.activation(flat(half(k.u, b)), bank(b), ACT.Copy).then_inc(*utaken.up())
                    act.wait_ge(*ws.at(2 * c + b + 1))
                    nc.scalar.activation(flat(half(k.wT, b)), bank(2 + b), ACT.Copy).then_inc(*wtaken.up())
                if c:
                    act.wait_ge(*inter.at(c))
                    if c > 1:
                        act.wait_ge(*oturn.at(c - 1))
                    for i in range(DNK):
                        nc.scalar.activation(k.o1[:, i, :], ps[:, 6 + i // H, (i % H) * P:(i % H) * P + P], ACT.Copy,
                                             scale=k.eG[:, at(c, i):at(c, i) + 1]).then_inc(*oscaled.up())
                    act.wait_ge(*summed.at(c + 1))
                    for i in range(DNK):
                        nc.scalar.activation(k.out_squares[:, i, :], k.o1[:, i, :], ACT.Square,
                                             accum_out=st[:, 0, i:i + 1]).then_inc(*squared.up())
            root(NCH - 1)


def deltanet(k, tiles, stop):
    nc = k.nc
    k.prefetch = k.tiles["dn_qkv"] + RING
    n_const = sum(n for _, n in k.const_cols["second"][0])
    shapes = [(n_const,), (2 * DNK, L), (DNK, NCH, 2, CH), (DNK, NCH, 2, CH), (DNK, NCH, CH), (DNV, L), (DNV, S),
              (DNV, P)]
    k.const2, k.qk, k.vT, k.kT, k.dq, k.z, k.dy, k.state = k.carve(k.big, *shapes)
    start = sum(int(np.prod(s)) for s in shapes)
    norm_stage(k, tiles, k.p("dn_norm"), L, "dn_qkv")
    end_early(k, "dn_qkv")
    k.squares2, = k.carve(k.mid, (2, L))
    conv_stage(k)
    if stop <= 26: return
    k.ba, k.soft_plus, k.dup = k.carve(k.mid, (L,), (2, L), (NCH, 2, CH))

    def put(eng, i, src):
        if i == 0:
            return nc.vector.tensor_copy(k.ba, src)
        return nc.scalar.activation(k.z[:, i - 1, :], src, ACT.Silu)
    project_T(k, "dn_ba", 1 + DNV, L,
              (lambda i: "scalar" if i else "vector", put), k.tiles["dn_out"])
    n = NCH * DNK
    (k.beta, k.g, k.G, k.negG, k.eG, k.eGL, k.be, k.gm, k.egl) = k.carve(
        k.kept, (n,), (n,), (n,), (n,), (n,), (n,), (n,), (2 * n,), (2 * n,))
    k.prefetch = k.tiles["dn_out"]
    delta_gates_stage(k)
    k.squares2, k.factors = k.carve(k.mid, (2, L), (4, L))

    def unit(c, wide):
        x = k.qk[:, c, :]
        chunked = lambda ap: ap[:, META:L].rearrange("p (c s) -> p c s", c=NCH - 1)
        if c < DNK:
            for dst, w, s in ((k.dq[:, c, 0, PAD:CH], wide[:, 0:META], x[:, 0:META]),
                              (k.dq[:, c, 1:NCH, :], chunked(wide), chunked(x))):
                yield nc.vector.scalar_tensor_tensor(dst, w, DNK_SCALE, s, ALU.mult, ALU.mult)
        else:
            i = c - DNK
            two = lambda ap: ap.unsqueeze(1).broadcast_to([P, 2, META])
            four = lambda ap: chunked(ap).unsqueeze(2).broadcast_to([P, NCH - 1, 2, CH])
            yield nc.vector.tensor_tensor(k.kT[:, i, 0, :, PAD:CH], two(wide[:, 0:META]), two(x[:, 0:META]), ALU.mult)
            yield nc.vector.tensor_tensor(k.kT[:, i, 1:NCH, :, :], four(wide), four(x), ALU.mult)
    head_norm_stage(k, [k.qk[:, c, :] for c in range(2 * DNK)], 2 * DNK,
                    lambda c: k.c("one")[:, 15 - c:31 - c],
                    lambda c: [(k.ident[0:16, c:c + 1].broadcast_to([16, P]), slice(0, P))], 1.0, EPS, unit)
    if stop <= 27: return
    k.E, k.o1, k.wT, k.R = k.carve(k.spare, (DNK, P), (DNK, P), (DNK, P), (DNK, P))
    k.ET, k.out_squares = k.carve(k.ring.buf.rearrange("p s n -> p (s n)"), (DNK, P), (DNK, P))
    k.const2, k.kbg, k.kst, k.vb, k.attnT = k.carve(k.big, (n_const,), (DNK, P), (DNK, P), (DNK, P), (DNK, P))
    assert 4 * DNK * P <= 2 * DNK * L
    k.pw, k.pwT, k.u = k.carve(k.big[:, start:32768], (DNK, P), (DNK, P), (DNK, P))
    k.vn = k.u
    delta_stage(k)
    if stop <= 28: return
    out_rows(k, "dn_out", [(k.h[:, tt, :], 2 * tt, P, tt * P) for tt in range(NT)], k.dy,
             k.tiles["end"] + RING)
    sent, = k.start("output_sent")
    with nc.Block() as block:

        @block.sync
        def _(sp):
            for tt in range(NT):
                sp.dma_start(k.out[tt], k.h[:, tt, :]).then_inc(*sent.up(16))
            sp.wait_ge(*sent.last())


DNK_SCALE = P ** -0.5


def dn_lay_out(a):
    w = a["dn_w_in_2"][0]
    z, b, aa = w[:, 4096:6144], w[:, 6144:6160], w[:, 6160:6176]
    ba = np.zeros((D, P), w.dtype)
    order = [0, 2, 4, 6, 8, 10, 12, 14, 1, 3, 5, 7, 9, 11, 13, 15]
    ba[:, 0:16], ba[:, 32:48] = b[:, order], aa[:, order]
    return {"dn_qkv": chunks_T(w[:, :4096]), "dn_z": chunks_T(z), "dn_ba": chunks_T(ba),
            "dn_out": chunk_pairs(a["dn_w_out_2"][0])}


def dn_params(a):
    order = [0, 2, 4, 6, 8, 10, 12, 14, 1, 3, 5, 7, 9, 11, 13, 15]

    def rows(v):
        out = np.zeros((P, 1), v.dtype)
        out[32:48, 0] = v[order]
        return out
    return {"conv": a["dn_conv_w_2"][0].reshape(4, 32, P).transpose(2, 1, 0).reshape(P, -1),
            "a_log": rows(a["dn_a_log_2"][0]), "dt_bias": rows(a["dn_dt_bias_2"][0]),
            "o_norm": a["dn_o_norm_w_2"][0][:, None]}


def dn_consts():
    r = np.arange(P)
    same = (r[:, None] // CH) == (r[None, :] // CH)
    one = np.zeros((P, 31))
    one[:, 15] = 1
    half = np.stack([r < CH, r >= CH], 1)
    return {"upper": same & (r[:, None] <= r[None, :]), "block": same, "half": half, "one": one,
            "low": np.where(same & (r[:, None] > r[None, :]), 0, NEG),
            "up": np.where(same & (r[:, None] <= r[None, :]), 0, NEG)}


def second_constants():
    f = np.float32
    r = np.arange(P)
    q = r[:, None]
    dist = []
    for tt in range(NT):
        pos_q = META + tt * P + q
        pos = np.arange(L)[None, :]
        d = pos_q - pos
        ok = (d >= 0) & ((pos < META) | (d < P))
        dist.append(np.where(ok, np.minimum(d, P), 1e34))
    meta = np.zeros((P, AH, META), f)
    for i in range(AH):
        h = 2 * (i % 8) + i // 8
        d = np.arange(META)[:, None] - np.arange(META)[None, :]
        meta[:META, i] = np.where(d >= 0, -2.0 ** (-8.0 * (h + 1) / AH) * d, NEG)
    pair = np.zeros((P, 38), f)
    pair[:HD, 18] = pair[HD:, 19] = 1
    return {"dist": np.concatenate(dist, 1), "meta_bias": meta.reshape(P, -1), "pair": pair, **dn_consts()}


def lay_out_second(a):
    w = a["attn_w_in_2"][0]
    q, kk, v, gate = w[:, :1024], w[:, 1024:1152], w[:, 1152:1280], w[:, 1280:]
    twice = lambda m: np.concatenate([m[:, :HD], m[:, :HD], m[:, HD:], m[:, HD:]], 1)
    return {"attn_t": chunks_T(np.concatenate([q, twice(kk), v, gate], 1)),
            "attn_out": chunk_pairs(a["attn_w_out_2"][0]),
            "norm_final": np.broadcast_to(a["norm_final"], (P, D)), **dn_lay_out(a)}


def params_second(a):
    col = lambda v: v.reshape(-1, P).T
    both = lambda v: np.concatenate([v, v])[:, None]
    sinks = np.broadcast_to(a["attn_sinks_2"], (P, AH))
    return {"attn_norm": col(a["attn_norm_w_2"][0]), "dn_norm": col(a["dn_norm_w_2"][0]),
            "q_norm": both(a["attn_q_norm_w_2"][0]), "k_norm": both(a["attn_k_norm_w_2"][0]),
            "sinks": sinks, "sinks_placed": np.concatenate([sinks[:, 0::2], sinks[:, 1::2]], 1), **dn_params(a)}


class Build:

    def __init__(self, nc, ctx, dram, const_cols, param_cols):
        self.nc, self.ctx, self.dram = nc, ctx, dram
        self.signals, self.loaded, self.prefetch, self.split_early = {}, 0, RING, set()
        sb = lambda name, cols, dt=F32: ctx.enter_context(nc.sbuf_tensor(name, [P, cols], dt))
        self.ps = ctx.enter_context(nc.psum_tensor("banks", [P, 8, 512], F32))
        self.big, self.small = sb("big", 32768), sb("small", 96)
        self.kept = sb("kept", 2 * NT * PH * TOPK + NT * P)
        self.rows = sb("rows", (NT + 4) * D)
        self.h = self.rows[:, 0:NT * D].rearrange("p (t n) -> p t n", t=NT)
        self.hm = self.rows[:, NT * D:(NT + 1) * D]
        self.spare = self.rows[:, NT * D:]
        self.mid = self.rows[:, (NT + 1) * D:]
        self.const = {}
        self.const_cols = const_cols
        common = const_cols["common"]
        self.common = sb("const", common[1])
        self.bind("common", self.common[:, :])
        self.param_cols = param_cols[0]
        self.param = sb("param", param_cols[1])
        ring = sb("weights", RING * TILE)[:, :].rearrange("p (s n) -> p s n", s=RING)
        sem = lambda name: ctx.enter_context(nc.semaphore(name))
        halves = lambda name, cols: sb(name, 2 * cols, F32R)[:, :].rearrange("p (s n) -> p s n", s=2)
        self.high, self.low, self.parts = halves("tile_high", TILE), halves("tile_low", TILE), halves("parts", KC * L)
        self.high_made, self.high_used = Signal(sem("high_made")), Signal(sem("high_used"))
        self.low_made = {e: Signal(sem("low_made_" + e)) for e in ("vector", "gpsimd")}
        self.ring = Ring(ring, [sem(f"tile_landed_{s}") for s in range(RING)], Signal(sem("tile_used")))
        self.ident = self.c("ident")

    def pair(self, cols):
        return [self.parts[:, part, 0:KC * cols].rearrange("p (c n) -> p c n", c=KC) for part in range(2)]

    def bind(self, part, view):
        at = 0
        for name, cols in self.const_cols[part][0]:
            self.const[name] = view[:, at:at + cols]
            at += cols

    def c(self, name):
        return self.const[name]

    def p(self, name):
        a, n = self.param_cols[name]
        return self.param[:, a:a + n]

    def start(self, *names):
        for name in names:
            if name not in self.signals:
                self.signals[name] = Signal(self.ctx.enter_context(self.nc.semaphore(name)))
            self.signals[name].start()
        return [self.signals[name] for name in names]

    def carve(self, region, *shapes):
        at, pieces = 0, []
        for shape in shapes:
            n = int(np.prod(shape))
            piece = region[:, at:at + n]
            if len(shape) > 1:
                names = "abcd"[:len(shape)]
                piece = piece.rearrange(f"p ({' '.join(names)}) -> p {' '.join(names)}", **dict(zip(names, shape)))
            pieces.append(piece)
            at += n
        assert at <= region.shape[1], (at, region.shape)
        return pieces


def program(nc, dram, out, const_cols, param_cols, stop=99):
    with ExitStack() as ctx:
        k = Build(nc, ctx, dram, const_cols, param_cols)
        k.out = out
        plan(k)
        first_block(k, stop)
        if stop > 20:
            second_block(k, stop)
        drain(k)


def drain(k):
    with k.nc.Block() as block:

        @block.sync
        def _(sp):
            for s in range(RING):
                n = sum(k.ring.slots[i] == s for i in range(k.loaded))
                if n:
                    sp.wait_ge(k.ring.landed[s], 16 * n)


def first_block(k, stop):
    ps = k.ps
    (k.T, k.fv, k.vv, k.cmp_in, k.rot, k.gelu, k.kcmp, k.vcmp, k.negc, k.gates, k.soft, k.pt, k.ptc, k.yfox, k.ynsa,
     k.mergedT, k.const1) = k.carve(
        k.big, (N_IN_T, S), (NT, 512), (NT, 256), (2, 2, N_CMP, 16), (4, S), (2, 2, N_CMP), (2 * N_CMP,), (P,), (S,), (NT, 24),
        (3, 4, S), (3, 2, 4, P), (PH, P), (4, S), (4, S), (KC, S),
        (sum((n for _, n in k.const_cols['first'][0])),))
    k.vcmp = k.vcmp[0:N_CMP, :]
    k.bind("first", k.const1)
    input_stage(k)
    norm_stage(k, [(k.h[:, tt, :], P) for tt in range(NT)], k.p("norm_mix"), S, "in_t")
    end_early(k, "in_t")
    if stop <= 1: return
    def put(eng, i, src):
        if i < MERGE:
            return k.nc.vector.tensor_copy(k.T[:, i, :], src)
        return k.nc.scalar.activation(k.T[:, i, :], src, ACT.Sigmoid)
    project_T(k, "in_t", N_IN_T, S,
              (lambda i: "vector" if i < MERGE else "scalar", put), k.tiles["in_fv"] + RING)
    def copy(dst, banks):
        def finish():
            for tt in range(NT):
                yield k.nc.vector.tensor_copy(dst[:, tt, :], ps[:, banks + tt, 0:dst.shape[2]])
        return finish
    lhs = lambda c, tt: [ap[:, c, tt * P:tt * P + P] for ap in k.pair(S)]
    project_N(k, "in_fv", lhs, [
        (4, 2, 512, [(ps[:, tt, :], tt) for tt in range(NT)], copy(k.fv, 0)),
        (2, 4, 256, [(ps[:, 2 + tt, 0:256], tt) for tt in range(NT)], copy(k.vv, 2))],
        k.tiles["cmp_w1"] + RING)
    if stop <= 2: return
    prepare_stage(k)
    if stop <= 3: return
    attention_stage(k)
    end_early(k, "branch")
    if stop <= 4: return
    merge_stage(k)
    out_rows(k, "out1", [(k.h[:, tt, :], 2 * tt, P, tt * P) for tt in range(NT)], k.mergedT,
             k.tiles["wq"] + RING)
    if stop <= 5: return
    peer(k, stop)


def out_rows(k, name, tiles, x, prefetch):
    nc, ps, first = k.nc, k.ps, k.tiles[name]
    pairs, cols = x.shape[1] // 2, x.shape[2]
    x_high, x_low, added = k.start("lhs_high", "lhs_low", "rows_added")
    place = lambda q: slice(2 * (q % 4), 2 * (q % 4) + 2)
    high_x, low_x = k.pair(cols)
    with nc.Block() as block:

        @block.sync
        def _(sp):
            load_tiles(sp, k, prefetch)

        @block.scalar
        def _(act):
            for q in range(pairs):
                if q >= 4:
                    act.wait_ge(k.ring.used.sem, first + 2 * (q - 4) + 2)
                nc.scalar.activation(high_x[:, place(q), :], x[:, 2 * q:2 * q + 2, :], ACT.Copy).then_inc(*x_high.up())
                for half in range(2):
                    make_high(act, k, first + 2 * q + half)

        @block.vector
        def _(dve):
            for q in range(pairs):
                dve.wait_ge(*x_high.at(q + 1))
                nc.vector.tensor_tensor(low_x[:, place(q), :], x[:, 2 * q:2 * q + 2, :],
                                        high_x[:, place(q), :].bitcast(F32), ALU.subtract).then_inc(*x_low.up())
                for half in range(2):
                    make_low(dve, k, first + 2 * q + half)
            dve.wait_ge(k.ring.used.sem, first + 2 * pairs)
            for h, bank, rows, _ in tiles:
                nc.vector.tensor_tensor(h[0:rows], h[0:rows], ps[0:rows, bank:bank + 2, :].rearrange("p b n -> p (b n)"),
                                        ALU.add).then_inc(*added.up())

        @block.tensor
        def _(pe):
            for q in range(pairs):
                for half in range(2):
                    n = first + 2 * q + half
                    high, low = parts(k, n, 2)
                    await_high(pe, k, n)
                    for part, (xs, w) in enumerate(((high_x, high), (low_x, high), (high_x, low))):
                        if part < 2 and half == 0:
                            pe.wait_ge(*(x_high, x_low)[part].at(q + 1))
                        if part == 2:
                            await_low(pe, k, n)
                        for c in range(2):
                            for _, bank, rows, c0 in tiles:
                                ins = nc.tensor.matmul(ps[0:rows, bank + half, :], xs[:, place(q), c0:c0 + rows][:, c, :],
                                                       w[:, c, :], start=q + part + c == 0,
                                                       stop=q == pairs - 1 and part == 2 and c == 1)
                        if part == 1:
                            ins.then_inc(*k.high_used.up())
                    tile_used(ins, k, n)


def constants():
    f = np.float32
    r = np.arange(P)
    q, s = r[:, None], np.arange(S)[None, :]
    eye = np.eye(P, dtype=f)
    common = {"ident": eye, "ones": np.ones((P, P), f), "iota": np.tile(r[None, :].astype(f), (P, 1))}
    mask = np.concatenate([np.where(s <= q + P * tt, 0, NEG) for tt in range(NT)], 1)
    ends = np.where(np.arange(16) < N_CMP, np.arange(16) * 16 + 31, 10 ** 6)[None, :]
    keep = np.concatenate([ends <= q + P * tt for tt in range(NT)], 1)
    inv = (np.float32(500000.0) ** (-np.arange(0, 16, 2, dtype=f) / f(16))).astype(f)
    row = r % HD
    freq = np.where(row < 16, inv[row % 8], 0).astype(f)[:, None]

    def rope(pos):
        ang = (np.asarray(pos, f)[None, :] * freq).astype(f)
        sin = np.where(row[:, None] < 16, np.sin(ang), 0)
        return np.cos(ang), sin

    cos, sin = rope(np.arange(S))
    ccos, csin = rope(np.arange(16) * 16 + 31)
    perm = np.zeros((P, P), f)
    for m in range(P):
        if m % HD < 8:
            perm[m + 8, m] = -1
        elif m % HD < 16:
            perm[m - 8, m] = 1
    first = {"mask": mask, "cmask": np.where(keep, 0, NEG), "ckeep": keep, "cos": cos, "sin": sin,
             "ccos": ccos, "csin": csin, "perm": perm}
    return {"common": common, "first": first, "second": second_constants()}


def pack(parts):
    cols, arrays = {}, {}
    for part, named in parts.items():
        cols[part] = ([(n, a.shape[1]) for n, a in named.items()], sum(a.shape[1] for a in named.values()))
        arrays["const_" + part] = np.concatenate([a.astype(np.float32) for a in named.values()], 1)
    return cols, arrays


def chunks_T(w):
    n = w.shape[1] // P
    return w.reshape(KC, P, n, P).transpose(2, 1, 0, 3).reshape(n, P, TILE)


def chunks_N(w, cols):
    per = TILE // cols
    c, n = w.shape[0] // P, w.shape[1] // cols
    return w.reshape(c // per, per, P, n, cols).transpose(3, 0, 2, 1, 4).reshape(n * (c // per), P, TILE)


def chunk_pairs(w):
    return w.reshape(-1, 2, P, 2, 512).transpose(0, 3, 2, 1, 4).reshape(-1, P, TILE)


def lay_out(a):
    w = a["w_in"][0]
    at = np.cumsum([0, 512, 512, 512, 8, 512, 128, 128, 128, 128, 128, 128, 24, 2048])
    part = [w[:, at[i]:at[i + 1]] for i in range(13)]
    fq, fk, fv, fl, nq, kc, vc, ksl, vsl, kwn, vwn, gate, merge = part
    twice = lambda m: np.concatenate([m[:, :HD], m[:, :HD], m[:, HD:], m[:, HD:]], 1)
    misc = np.zeros((D, P), w.dtype)
    misc[:, 0:8], misc[:, GATE_ROW:GATE_ROW + 24] = fl, gate
    out = {"in_t": chunks_T(np.concatenate([fq, fk, nq, kc, vc, twice(ksl), twice(kwn), misc, merge], 1)),
           "in_fv": chunks_N(fv, 512),
           "in_vv": chunks_N(np.concatenate([vsl, vwn], 1), 256)}
    w1 = a["nsa_cmp_w1"][0].reshape(2, 2, 16, HD, P).transpose(0, 1, 3, 2, 4)
    out["cmp_w1"] = w1.reshape(2, P, 2, TILE).transpose(0, 2, 1, 3).reshape(4, P, TILE)
    out["branch"] = a["w_branch"][0].reshape(2, 4, P, KC, P).transpose(3, 2, 0, 1, 4).reshape(KC, P, TILE)
    out["out1"] = chunk_pairs(a["w_out"][0])
    out["wq"] = chunks_T(a["peer_wq"][0])
    out["subk"] = a["peer_subkeys"][0].reshape(16, NKEY, P).transpose(2, 0, 1).reshape(P, 2, TILE).transpose(1, 0, 2)
    u = a["peer_u"][0].reshape(NKEY, NKEY, KC, P)
    out["peer_u"] = u.transpose(1, 3, 2, 0).reshape(NKEY, P, TILE)
    out["peer_v"] = a["peer_v"][0].reshape(NKEY, NKEY, D).transpose(1, 0, 2)
    out["x"] = a["x"][0].reshape(NT, P, D).transpose(1, 0, 2)
    out["meta"] = a["meta_tokens_2"]
    out.update(lay_out_second(a))

    col = lambda v: v.reshape(-1, P).T
    rows = lambda v: np.concatenate([v.reshape(-1, 1), np.zeros((P - v.size, 1), v.dtype)])
    both = lambda v: np.concatenate([v, v])
    params = {"norm_mix": col(a["norm_mix"][0]), "norm_ffn": col(a["norm_ffn"][0]),
              "fbias": rows(a["fox_f_bias"][0]),
              "pos": both(a["nsa_cmp_pos"][0].transpose(2, 0, 1).reshape(HD, 64)),
              "w2k": np.concatenate([a["nsa_cmp_w2"][0, 0]] * 2, 1), "w2v": a["nsa_cmp_w2"][0, 1]}
    params.update(params_second(a))
    cols, at = {}, 0
    for n, v in params.items():
        cols[n] = (at, v.shape[1])
        at += v.shape[1]
    out["param"] = np.concatenate(list(params.values()), 1)
    return out, (cols, at)


def launch(nc, inputs, stop=99):
    arrays, param_cols = lay_out({n: np.asarray(v) for n, v in inputs.items()})
    const_cols, consts = pack(constants())
    arrays.update(consts)
    dram, given = {}, {}
    for name, v in arrays.items():
        given["in_" + name] = v = np.ascontiguousarray(v)
        dram[name] = nc.dram_tensor("in_" + name, v.shape, mybir.dt.from_np(v.dtype), kind="ExternalInput").ap()
    out = nc.dram_tensor("out", (NT, P, D), F32, kind="ExternalOutput").ap()
    program(nc, dram, out, const_cols, param_cols, stop)
    return given


def kernel(**inputs):
    import concourse.bacc as _bacc
    from concourse.bass_utils import run_bass_kernel_spmd as _run

    nc = _bacc.Bacc("TRN2", target_bir_lowering=False, num_devices=1)
    given = launch(nc, inputs)
    return _run(nc, [given], core_ids=[0]).results[0]["out"].reshape(1, S, D)
```
